# Optimizing a Trainium2 kernel written in Bass

```python
import math
import jax, jax.numpy as jnp
from jax import lax
import numpy as np
import jax
import jax.numpy as jnp

D_MODEL = 1024
BATCH = 1
SEQ = 256
DEPTH = 2

CHUNK = 64
Q_BLOCK = 128
HEAD_DIM = 64
HEADS_FOX = 6
HEADS_SB = 5
HEADS_DSA = 5
IDX_HEADS = 8
IDX_DIM = 64
DSA_TOPK_MAX = 256
D_FF = 4 * D_MODEL
PLE_DIM = 256
ROPE_THETA = 10000.0
LN_EPS = 1e-5
N_BRANCH = 3
NEG = -1e30
DEEPNORM_ALPHA = (2 * DEPTH) ** 0.25
DEEPNORM_BETA = (8 * DEPTH) ** -0.25

W_FOX = HEADS_FOX * HEAD_DIM
W_SB = HEADS_SB * HEAD_DIM
W_DSA = HEADS_DSA * HEAD_DIM
IN_SPLITS = (W_FOX, W_FOX, W_FOX, HEADS_FOX,
             W_SB, W_SB, W_SB,
             W_DSA, HEAD_DIM, HEAD_DIM,
             IDX_HEADS * IDX_DIM, IDX_DIM, IDX_HEADS,
             N_BRANCH * D_MODEL)
C_IN = sum(IN_SPLITS)


def split_cols(h):
    out = []
    o = 0
    for w in IN_SPLITS:
        out.append(h[..., o:o + w])
        o += w
    return out

def layer_norm(x, g, b):
    xf = x.astype(jnp.float32)
    mu = jnp.mean(xf, axis=-1, keepdims=True)
    var = jnp.mean(jnp.square(xf - mu), axis=-1, keepdims=True)
    y = (xf - mu) * lax.rsqrt(var + LN_EPS) * g.astype(jnp.float32) + b.astype(jnp.float32)
    return y.astype(x.dtype)

def rope(x, pos):
    half = x.shape[-1] // 2
    inv = ROPE_THETA ** (-jnp.arange(half, dtype=jnp.float32) / half)
    ang = pos.astype(jnp.float32)[:, None] * inv[None, :]
    cos = jnp.cos(ang)[None, :, None, :].astype(x.dtype)
    sin = jnp.sin(ang)[None, :, None, :].astype(x.dtype)
    x1, x2 = x[..., :half], x[..., half:]
    return jnp.concatenate([x1 * cos - x2 * sin, x2 * cos + x1 * sin], axis=-1)

def to_blocks(a):
    b, s = a.shape[:2]
    return jnp.moveaxis(a.reshape(b, s // Q_BLOCK, Q_BLOCK, *a.shape[2:]), 1, 0)

def from_blocks(a):
    nb, b, qb = a.shape[:3]
    return jnp.moveaxis(a, 0, 1).reshape(b, nb * qb, *a.shape[3:])

def fox_attention(q, k, v, log_f):
    b, s, h, dh = q.shape
    c = jnp.cumsum(log_f, axis=1)
    c_k = jnp.transpose(c, (0, 2, 1))[:, :, None, :]
    kpos = jnp.arange(s)
    scale = dh ** -0.5

    def block(args):
        qb, cb, bi = args
        qpos = bi * Q_BLOCK + jnp.arange(Q_BLOCK)
        logits = jnp.einsum('bqhd,bkhd->bhqk', qb, k).astype(jnp.float32) * scale
        logits = logits + jnp.transpose(cb, (0, 2, 1))[..., None] - c_k
        causal = kpos[None, :] <= qpos[:, None]
        logits = jnp.where(causal, logits, NEG)
        w = jax.nn.softmax(logits, axis=-1)
        return jnp.einsum('bhqk,bkhd->bqhd', w.astype(v.dtype), v)

    out = lax.map(block, (to_blocks(q), to_blocks(c), jnp.arange(s // Q_BLOCK)))
    return from_blocks(out).reshape(b, s, h * dh)

def stick_breaking_attention(q, k, v):
    b, s, h, dh = q.shape
    kpos = jnp.arange(s)
    scale = dh ** -0.5

    def block(args):
        qb, bi = args
        qpos = bi * Q_BLOCK + jnp.arange(Q_BLOCK)
        z = jnp.einsum('bqhd,bkhd->bhqk', qb, k).astype(jnp.float32) * scale
        strict = kpos[None, :] < qpos[:, None]
        log_not = jnp.where(strict, jax.nn.log_sigmoid(-z), 0.0)
        after = lax.cumsum(log_not, axis=3, reverse=True) - log_not
        a = jnp.where(strict, jnp.exp(jax.nn.log_sigmoid(z) + after), 0.0)
        return jnp.einsum('bhqk,bkhd->bqhd', a.astype(v.dtype), v)

    out = lax.map(block, (to_blocks(q), jnp.arange(s // Q_BLOCK)))
    return from_blocks(out).reshape(b, s, h * dh)

def dsa_attention(q, k, v, iq, ik, iw):
    b, s, h, dh = q.shape
    n_sel = min(DSA_TOPK_MAX, s // 4)
    kchunk = jnp.arange(s) // CHUNK
    bidx = jnp.arange(b)[:, None, None]
    scale = dh ** -0.5

    def block(args):
        qb, iqb, iwb, bi = args
        qchunk = (bi * Q_BLOCK + jnp.arange(Q_BLOCK)) // CHUNK
        admiss = kchunk[None, :] <= qchunk[:, None]
        idx_logits = jnp.einsum('bqhd,bkd->bqhk', iqb, ik).astype(jnp.float32)
        score = jnp.einsum('bqh,bqhk->bqk', iwb.astype(jnp.float32), jax.nn.relu(idx_logits))
        score = jnp.where(admiss[None], score, NEG)
        _, sel = lax.top_k(score, n_sel)
        sel_ok = (sel // CHUNK) <= qchunk[None, :, None]
        ks = k[bidx, sel]
        vs = v[bidx, sel]
        logits = jnp.einsum('bqhd,bqnd->bhqn', qb, ks).astype(jnp.float32) * scale
        logits = jnp.where(sel_ok[:, None], logits, NEG)
        w = jax.nn.softmax(logits, axis=-1)
        return jnp.einsum('bhqn,bqnd->bqhd', w.astype(vs.dtype), vs)

    out = lax.map(block, (to_blocks(q), to_blocks(iq), to_blocks(iw), jnp.arange(s // Q_BLOCK)))
    return from_blocks(out).reshape(b, s, h * dh)

def first_inputs(seed: int = 0) -> dict:
    key = jax.random.key(seed)
    ks = jax.random.split(key, 20)
    n = jax.random.normal
    f32 = jnp.float32
    L = DEPTH
    bt = DEEPNORM_BETA
    return {
        'x': n(ks[0], (BATCH, SEQ, D_MODEL), f32),
        'p': n(ks[1], (DEPTH, BATCH, SEQ, PLE_DIM), f32),
        'w_in': n(ks[2], (L, D_MODEL, C_IN), f32) * D_MODEL ** -0.5,
        'b_forget': 2.0 + 0.5 * n(ks[3], (L, HEADS_FOX), f32),
        'w_up_fox': n(ks[4], (L, W_FOX, D_MODEL), f32) * W_FOX ** -0.5 * bt,
        'w_up_sb': n(ks[5], (L, W_SB, D_MODEL), f32) * W_SB ** -0.5 * bt,
        'w_up_dsa': n(ks[6], (L, W_DSA, D_MODEL), f32) * W_DSA ** -0.5 * bt,
        'w_out': n(ks[7], (L, D_MODEL, D_MODEL), f32) * D_MODEL ** -0.5 * bt,
        'ln1_g': 1.0 + 0.05 * n(ks[8], (L, D_MODEL), f32),
        'ln1_b': 0.02 * n(ks[9], (L, D_MODEL), f32),
        'w_ff_in': n(ks[10], (L, D_MODEL, D_FF), f32) * D_MODEL ** -0.5,
        'w_ff_out': n(ks[11], (L, D_FF, D_MODEL), f32) * D_FF ** -0.5 * bt,
        'w_ple': n(ks[12], (L, PLE_DIM, D_MODEL), f32) * PLE_DIM ** -0.5 * bt,
        'w_ple_gate': n(ks[13], (L, D_MODEL, D_MODEL), f32) * D_MODEL ** -0.5,
        'ln2_g': 1.0 + 0.05 * n(ks[14], (L, D_MODEL), f32),
        'ln2_b': 0.02 * n(ks[15], (L, D_MODEL), f32),
    }

def first_block(x, p, w_in, b_forget, w_up_fox, w_up_sb, w_up_dsa, w_out, ln1_g, ln1_b,
              w_ff_in, w_ff_out, w_ple, w_ple_gate, ln2_g, ln2_b):
    b, s, _ = x.shape
    pos = jnp.arange(s)
    for i in range(DEPTH):
        h = x @ w_in[i]
        (fq, fk, fv, ff_logit, sq, sk, sv, dq, dk, dv, iq, ik, iw, g) = split_cols(h)
        fq = fq.reshape(b, s, HEADS_FOX, HEAD_DIM)
        fk = fk.reshape(b, s, HEADS_FOX, HEAD_DIM)
        fv = fv.reshape(b, s, HEADS_FOX, HEAD_DIM)
        log_f = jax.nn.log_sigmoid(ff_logit.astype(jnp.float32) + b_forget[i].astype(jnp.float32))
        o_fox = fox_attention(fq, fk, fv, log_f)

        o_sb = stick_breaking_attention(sq.reshape(b, s, HEADS_SB, HEAD_DIM),
                                        sk.reshape(b, s, HEADS_SB, HEAD_DIM),
                                        sv.reshape(b, s, HEADS_SB, HEAD_DIM))

        dq = rope(dq.reshape(b, s, HEADS_DSA, HEAD_DIM), pos)
        dk = rope(dk[:, :, None, :], pos)[:, :, 0, :]
        iq = rope(iq.reshape(b, s, IDX_HEADS, IDX_DIM), pos)
        ik = rope(ik[:, :, None, :], pos)[:, :, 0, :]
        o_dsa = dsa_attention(dq, dk, dv, iq, ik, iw)

        gates = jax.nn.sigmoid(g.reshape(b, s, N_BRANCH, D_MODEL))
        merged = (gates[:, :, 0] * (o_fox @ w_up_fox[i])
                  + gates[:, :, 1] * (o_sb @ w_up_sb[i])
                  + gates[:, :, 2] * (o_dsa @ w_up_dsa[i]))
        x = layer_norm(DEEPNORM_ALPHA * x + merged @ w_out[i], ln1_g[i], ln1_b[i])

        ffn = jnp.square(jax.nn.relu(x @ w_ff_in[i])) @ w_ff_out[i]
        ple = jax.nn.sigmoid(x @ w_ple_gate[i]) * (p[i] @ w_ple[i])
        x = layer_norm(DEEPNORM_ALPHA * x + ffn + ple, ln2_g[i], ln2_b[i])
    return x


GRID_W = 64
CTX_LEN = 256
N_MIXERS = 4
N_MOD = 9
D_FF_2 = 2816
EPS = 1e-6
ROPE_BASE = 10000.0
ROPE_DIM = 64
NEG_INF = -1e30

MLA_HEADS = 8
MLA_Q_RANK = 512
MLA_KV_RANK = 256
MLA_NOPE = 128
MLA_ROPE = ROPE_DIM
MLA_V = 128

SWA_Q_HEADS = 16
SWA_KV_HEADS = 4
SWA_GROUP = SWA_Q_HEADS // SWA_KV_HEADS
SWA_HEAD_DIM = ROPE_DIM
SWA_WINDOW = 128

NA_HEADS = 16
NA_HEAD_DIM = D_MODEL // NA_HEADS
NA_KH = 8
NA_KW = 16

DIFF_HEADS = 8
DIFF_HEAD_DIM = ROPE_DIM


def rms_norm(x, g):
    xf = x.astype(jnp.float32)
    y = xf * lax.rsqrt(jnp.mean(xf * xf, axis=-1, keepdims=True) + EPS)
    return (y * g.astype(jnp.float32)).astype(x.dtype)

def modulate(h, shift, scale):
    return h * (1.0 + scale) + shift

def swiglu(h, w_in, w_out):
    g, u = jnp.split(h @ w_in, 2, axis=-1)
    return (jax.nn.silu(g) * u) @ w_out

def axial_rope_tables(L, dim):
    t = jnp.arange(L, dtype=jnp.int32)
    row = (t // GRID_W).astype(jnp.float32)
    col = (t % GRID_W).astype(jnp.float32)
    n_freq = dim // 4
    inv = jnp.exp(-math.log(ROPE_BASE) * jnp.arange(n_freq, dtype=jnp.float32) / n_freq)
    ang = jnp.concatenate([row[:, None] * inv, col[:, None] * inv], axis=-1)
    return jnp.cos(ang), jnp.sin(ang)

def apply_rope(x, cos, sin):
    half = x.shape[-1] // 2
    x1 = x[..., :half].astype(jnp.float32)
    x2 = x[..., half:].astype(jnp.float32)
    return jnp.concatenate([x1 * cos - x2 * sin, x1 * sin + x2 * cos], axis=-1).astype(x.dtype)

def softmax32(s):
    return jax.nn.softmax(s.astype(jnp.float32), axis=-1)

def joint_softmax(*scores):
    sizes = [s.shape[-1] for s in scores]
    p = softmax32(jnp.concatenate([s.astype(jnp.float32) for s in scores], axis=-1))
    cuts = [int(v) for v in np.cumsum(sizes)[:-1]]
    return jnp.split(p, cuts, axis=-1)

def to_blocks_2(t):
    lead = t.shape[:-2]
    L, d = t.shape[-2], t.shape[-1]
    t = t.reshape(lead + (L // Q_BLOCK, Q_BLOCK, d))
    return jnp.moveaxis(t, -3, 0)

def from_blocks_2(t):
    t = jnp.moveaxis(t, 0, -3)
    lead = t.shape[:-3]
    nb, qb, d = t.shape[-3], t.shape[-2], t.shape[-1]
    return t.reshape(lead + (nb * qb, d))

def merge_heads(o):
    B, H, N, d = o.shape
    return o.transpose(0, 2, 1, 3).reshape(B, N, H * d)

def pv(eq, p, v):
    return jnp.einsum(eq, p.astype(v.dtype), v)

def mla_mixer(hx, hc, w_down, q_norm, kv_norm, w_uq, w_ukv, w_o, cos, sin, ctx_out):
    H = MLA_HEADS
    scale = (MLA_NOPE + MLA_ROPE) ** -0.5

    def project(h):
        B, N, _ = h.shape
        d = h @ w_down
        cq = rms_norm(d[..., :MLA_Q_RANK], q_norm)
        ckv = rms_norm(d[..., MLA_Q_RANK:MLA_Q_RANK + MLA_KV_RANK], kv_norm)
        k_rope = d[..., MLA_Q_RANK + MLA_KV_RANK:]
        q = (cq @ w_uq).reshape(B, N, H, MLA_NOPE + MLA_ROPE).transpose(0, 2, 1, 3)
        kv = (ckv @ w_ukv).reshape(B, N, H, MLA_NOPE + MLA_V).transpose(0, 2, 1, 3)
        return q[..., :MLA_NOPE], q[..., MLA_NOPE:], kv[..., :MLA_NOPE], k_rope, kv[..., MLA_NOPE:]

    qn_x, qr_x, kn_x, kr_x, v_x = project(hx)
    qn_c, qr_c, kn_c, kr_c, v_c = project(hc)
    qr_x_rot = apply_rope(qr_x, cos, sin)
    kr_x_rot = apply_rope(kr_x, cos, sin)

    def scores(qn, qr, kn, kr):
        s = jnp.einsum('bhqd,bhkd->bhqk', qn, kn) + jnp.einsum('bhqr,bkr->bhqk', qr, kr)
        return s.astype(jnp.float32) * scale

    def block(args):
        qn, qr_rot, qr_pl = args
        p_x, p_c = joint_softmax(scores(qn, qr_rot, kn_x, kr_x_rot), scores(qn, qr_pl, kn_c, kr_c))
        return pv('bhqk,bhkd->bhqd', p_x, v_x) + pv('bhqk,bhkd->bhqd', p_c, v_c)

    o_x = from_blocks_2(lax.map(block, (to_blocks_2(qn_x), to_blocks_2(qr_x_rot), to_blocks_2(qr_x))))
    out_x = merge_heads(o_x) @ w_o
    out_c = None
    if ctx_out:
        p = softmax32(scores(qn_c, qr_c, kn_c, kr_c))
        out_c = merge_heads(pv('bhqk,bhkd->bhqd', p, v_c)) @ w_o
    return out_x, out_c

def swa_mixer(hx, hc, w_qkv, sink, w_o, cos, sin, ctx_out):
    Hk, G, Dh = SWA_KV_HEADS, SWA_GROUP, SWA_HEAD_DIM
    scale = Dh ** -0.5

    def project(h):
        B, N, _ = h.shape
        p = h @ w_qkv
        q = p[..., :Hk * G * Dh].reshape(B, N, Hk, G, Dh).transpose(0, 2, 3, 1, 4)
        k = p[..., Hk * G * Dh:(Hk * G + Hk) * Dh].reshape(B, N, Hk, Dh).transpose(0, 2, 1, 3)
        v = p[..., (Hk * G + Hk) * Dh:].reshape(B, N, Hk, Dh).transpose(0, 2, 1, 3)
        return q, k, v

    B, L, _ = hx.shape
    C = hc.shape[1]
    q_x, k_x, v_x = project(hx)
    q_c, k_c, v_c = project(hc)
    q_x_rot = apply_rope(q_x, cos, sin)
    k_x_rot = apply_rope(k_x, cos, sin)
    pad = ((0, 0), (0, 0), (SWA_WINDOW, SWA_WINDOW), (0, 0))
    k_pad = jnp.pad(k_x_rot, pad)
    v_pad = jnp.pad(v_x, pad)
    span = Q_BLOCK + 2 * SWA_WINDOW
    qi = jnp.arange(Q_BLOCK)
    kj = jnp.arange(span)
    sink_b = sink.reshape(Hk, G)[None, :, :, None, None].astype(jnp.float32)

    def ctx_scores(q):
        return jnp.einsum('bkgqd,bkcd->bkgqc', q, k_c).astype(jnp.float32) * scale

    def block(args):
        n, q_rot, q_pl = args
        start = n * Q_BLOCK
        k_b = lax.dynamic_slice_in_dim(k_pad, start, span, axis=2)
        v_b = lax.dynamic_slice_in_dim(v_pad, start, span, axis=2)
        qpos = start + qi
        kpos = start - SWA_WINDOW + kj
        valid = ((jnp.abs(kpos[None, :] - qpos[:, None]) <= SWA_WINDOW)
                 & (kpos[None, :] >= 0) & (kpos[None, :] < L))
        s_w = jnp.einsum('bkgqd,bkjd->bkgqj', q_rot, k_b).astype(jnp.float32) * scale
        s_w = jnp.where(valid, s_w, NEG_INF)
        s_c = ctx_scores(q_pl)
        s_s = jnp.broadcast_to(sink_b, s_c.shape[:-1] + (1,))
        p_w, p_c, _ = joint_softmax(s_w, s_c, s_s)
        return pv('bkgqj,bkjd->bkgqd', p_w, v_b) + pv('bkgqc,bkcd->bkgqd', p_c, v_c)

    nb = L // Q_BLOCK
    o = from_blocks_2(lax.map(block, (jnp.arange(nb), to_blocks_2(q_x_rot), to_blocks_2(q_x))))
    out_x = o.transpose(0, 3, 1, 2, 4).reshape(B, L, Hk * G * Dh) @ w_o
    out_c = None
    if ctx_out:
        s_c = ctx_scores(q_c)
        s_s = jnp.broadcast_to(sink_b, s_c.shape[:-1] + (1,))
        p_c, _ = joint_softmax(s_c, s_s)
        o_c = pv('bkgqc,bkcd->bkgqd', p_c, v_c)
        out_c = o_c.transpose(0, 3, 1, 2, 4).reshape(B, C, Hk * G * Dh) @ w_o
    return out_x, out_c

def na_mixer(hx, hc, w_qkv, rpb, w_o, ctx_out):
    H, Dh = NA_HEADS, NA_HEAD_DIM
    scale = Dh ** -0.5

    def project(h):
        B, N, _ = h.shape
        p = (h @ w_qkv).reshape(B, N, 3, H, Dh).transpose(2, 0, 3, 1, 4)
        return p[0], p[1], p[2]

    B, L, _ = hx.shape
    rows = L // GRID_W
    kh = min(NA_KH, rows)
    kw = NA_KW
    q_x, k_x, v_x = project(hx)
    q_c, k_c, v_c = project(hc)
    col = jnp.arange(GRID_W)
    col_start = jnp.clip(col - kw // 2, 0, GRID_W - kw)
    key_cols = col_start[:, None] + jnp.arange(kw)[None, :]
    col_off = key_cols - col[:, None] + (NA_KW - 1)

    def block(args):
        r, q_row = args
        row_start = jnp.clip(r - kh // 2, 0, rows - kh)
        key_rows = row_start + jnp.arange(kh)
        idx = (key_rows[None, :, None] * GRID_W + key_cols[:, None, :]).reshape(-1)
        k_g = jnp.take(k_x, idx, axis=2).reshape(B, H, GRID_W, kh * kw, Dh)
        v_g = jnp.take(v_x, idx, axis=2).reshape(B, H, GRID_W, kh * kw, Dh)
        row_off = key_rows - r + (NA_KH - 1)
        bias = rpb[:, row_off[None, :, None], col_off[:, None, :]]
        bias = bias.reshape(H, GRID_W, kh * kw).astype(jnp.float32)
        s_n = jnp.einsum('bhqd,bhqkd->bhqk', q_row, k_g).astype(jnp.float32) * scale + bias[None]
        s_c = jnp.einsum('bhqd,bhcd->bhqc', q_row, k_c).astype(jnp.float32) * scale
        p_n, p_c = joint_softmax(s_n, s_c)
        return pv('bhqk,bhqkd->bhqd', p_n, v_g) + pv('bhqc,bhcd->bhqd', p_c, v_c)

    q_rows = q_x.reshape(B, H, rows, GRID_W, Dh).transpose(2, 0, 1, 3, 4)
    o = lax.map(block, (jnp.arange(rows), q_rows))
    out_x = o.transpose(1, 0, 3, 2, 4).reshape(B, L, H * Dh) @ w_o
    out_c = None
    if ctx_out:
        p = softmax32(jnp.einsum('bhqd,bhcd->bhqc', q_c, k_c).astype(jnp.float32) * scale)
        out_c = merge_heads(pv('bhqc,bhcd->bhqd', p, v_c)) @ w_o
    return out_x, out_c

def diff_mixer(hx, hc, w_qkv, lam_params, norm_g, w_o, cos, sin, lam_init, ctx_out):
    H, Dh = DIFF_HEADS, DIFF_HEAD_DIM
    scale = Dh ** -0.5

    def project(h):
        B, N, _ = h.shape
        p = h @ w_qkv
        q = p[..., :H * 2 * Dh].reshape(B, N, H, 2, Dh).transpose(0, 2, 3, 1, 4)
        k = p[..., H * 2 * Dh:H * 4 * Dh].reshape(B, N, H, 2, Dh).transpose(0, 2, 3, 1, 4)
        v = p[..., H * 4 * Dh:].reshape(B, N, H, 2 * Dh).transpose(0, 2, 1, 3)
        return q, k, v

    q_x, k_x, v_x = project(hx)
    q_c, k_c, v_c = project(hc)
    q_x_rot = apply_rope(q_x, cos, sin)
    k_x_rot = apply_rope(k_x, cos, sin)
    lp = lam_params.astype(jnp.float32)
    lam = jnp.exp(jnp.sum(lp[0] * lp[1])) - jnp.exp(jnp.sum(lp[2] * lp[3])) + lam_init

    def scores(q, k):
        return jnp.einsum('bhiqd,bhikd->bhiqk', q, k).astype(jnp.float32) * scale

    def block(args):
        q_rot, q_pl = args
        p_x, p_c = joint_softmax(scores(q_rot, k_x_rot), scores(q_pl, k_c))
        a_x = p_x[:, :, 0] - lam * p_x[:, :, 1]
        a_c = p_c[:, :, 0] - lam * p_c[:, :, 1]
        return pv('bhqk,bhkd->bhqd', a_x, v_x) + pv('bhqk,bhkd->bhqd', a_c, v_c)

    def finish(o):
        return merge_heads(rms_norm(o, norm_g) * (1.0 - lam_init)) @ w_o

    o_x = from_blocks_2(lax.map(block, (to_blocks_2(q_x_rot), to_blocks_2(q_x))))
    out_x = finish(o_x)
    out_c = None
    if ctx_out:
        p = softmax32(scores(q_c, k_c))
        out_c = finish(pv('bhqk,bhkd->bhqd', p[:, :, 0] - lam * p[:, :, 1], v_c))
    return out_x, out_c

def second_inputs(seed: int = 0) -> dict:
    key = jax.random.key(seed)
    keys = jax.random.split(key, 32)
    counter = [0]

    def normal(shape, std):
        k = keys[counter[0]]
        counter[0] += 1
        return jax.random.normal(k, shape, jnp.float32) * std

    def gain(shape):
        return 1.0 + normal(shape, 0.02)

    nA, nB, nC, nD = [len(range(m, DEPTH, N_MIXERS)) for m in range(N_MIXERS)]
    D = D_MODEL
    return {
        'x': normal((BATCH, SEQ, D), 1.0),
        'c': normal((BATCH, D), 1.0),
        'ctx': normal((BATCH, CTX_LEN, D), 1.0),
        'c_ctx': normal((D,), 1.0),
        'mod_w': normal((DEPTH, D, N_MOD * D), 0.5 * D ** -0.5),
        'mod_b': normal((DEPTH, N_MOD * D), 0.02),
        'norm_g': gain((DEPTH, 3, D)),
        'final_norm_g': gain((D,)),
        'ffn_w_in': normal((DEPTH, 2, D, 2 * D_FF_2), D ** -0.5),
        'ffn_w_out': normal((DEPTH, 2, D_FF_2, D), D_FF_2 ** -0.5),
        'mla_w_down': normal((nA, D, MLA_Q_RANK + MLA_KV_RANK + MLA_ROPE), D ** -0.5),
        'mla_q_norm': gain((nA, MLA_Q_RANK)),
        'mla_kv_norm': gain((nA, MLA_KV_RANK)),
        'mla_w_uq': normal((nA, MLA_Q_RANK, MLA_HEADS * (MLA_NOPE + MLA_ROPE)), MLA_Q_RANK ** -0.5),
        'mla_w_ukv': normal((nA, MLA_KV_RANK, MLA_HEADS * (MLA_NOPE + MLA_V)), MLA_KV_RANK ** -0.5),
        'mla_w_o': normal((nA, MLA_HEADS * MLA_V, D), (MLA_HEADS * MLA_V) ** -0.5),
        'swa_w_qkv': normal((nB, D, (SWA_Q_HEADS + 2 * SWA_KV_HEADS) * SWA_HEAD_DIM), D ** -0.5),
        'swa_sink': normal((nB, SWA_Q_HEADS), 0.5),
        'swa_w_o': normal((nB, SWA_Q_HEADS * SWA_HEAD_DIM, D), (SWA_Q_HEADS * SWA_HEAD_DIM) ** -0.5),
        'na_w_qkv': normal((nC, D, 3 * NA_HEADS * NA_HEAD_DIM), D ** -0.5),
        'na_rpb': normal((nC, NA_HEADS, 2 * NA_KH - 1, 2 * NA_KW - 1), 0.2),
        'na_w_o': normal((nC, NA_HEADS * NA_HEAD_DIM, D), (NA_HEADS * NA_HEAD_DIM) ** -0.5),
        'diff_w_qkv': normal((nD, D, 6 * DIFF_HEADS * DIFF_HEAD_DIM), D ** -0.5),
        'diff_lambda': normal((nD, 4, DIFF_HEAD_DIM), 0.1),
        'diff_norm_g': gain((nD, 2 * DIFF_HEAD_DIM)),
        'diff_w_o': normal((nD, 2 * DIFF_HEADS * DIFF_HEAD_DIM, D), (2 * DIFF_HEADS * DIFF_HEAD_DIM) ** -0.5),
    }

def second_block(x, c, ctx, c_ctx, mod_w, mod_b, norm_g, final_norm_g, ffn_w_in, ffn_w_out,
              mla_w_down, mla_q_norm, mla_kv_norm, mla_w_uq, mla_w_ukv, mla_w_o,
              swa_w_qkv, swa_sink, swa_w_o, na_w_qkv, na_rpb, na_w_o,
              diff_w_qkv, diff_lambda, diff_norm_g, diff_w_o):
    L = x.shape[1]
    cos, sin = axial_rope_tables(L, ROPE_DIM)
    xc = ctx
    cond_x = jax.nn.silu(c)
    cond_c = jax.nn.silu(c_ctx)
    for layer in range(DEPTH):
        kind = layer % N_MIXERS
        j = layer // N_MIXERS
        last = layer == DEPTH - 1
        mx = jnp.split((cond_x @ mod_w[layer] + mod_b[layer])[:, None, :], N_MOD, axis=-1)
        mc = jnp.split(cond_c @ mod_w[layer] + mod_b[layer], N_MOD, axis=-1)

        x = x + 0.5 * mx[2] * swiglu(modulate(rms_norm(x, norm_g[layer, 0]), mx[0], mx[1]),
                                     ffn_w_in[layer, 0], ffn_w_out[layer, 0])
        xc = xc + 0.5 * mc[2] * swiglu(modulate(rms_norm(xc, norm_g[layer, 0]), mc[0], mc[1]),
                                       ffn_w_in[layer, 0], ffn_w_out[layer, 0])

        hx = modulate(rms_norm(x, norm_g[layer, 1]), mx[3], mx[4])
        hc = modulate(rms_norm(xc, norm_g[layer, 1]), mc[3], mc[4])
        if kind == 0:
            ox, oc = mla_mixer(hx, hc, mla_w_down[j], mla_q_norm[j], mla_kv_norm[j], mla_w_uq[j],
                               mla_w_ukv[j], mla_w_o[j], cos, sin, not last)
        elif kind == 1:
            ox, oc = swa_mixer(hx, hc, swa_w_qkv[j], swa_sink[j], swa_w_o[j], cos, sin, not last)
        elif kind == 2:
            ox, oc = na_mixer(hx, hc, na_w_qkv[j], na_rpb[j], na_w_o[j], not last)
        else:
            lam_init = 0.8 - 0.6 * math.exp(-0.3 * layer)
            ox, oc = diff_mixer(hx, hc, diff_w_qkv[j], diff_lambda[j], diff_norm_g[j], diff_w_o[j],
                                cos, sin, lam_init, not last)
        x = x + mx[5] * ox

        x = x + 0.5 * mx[8] * swiglu(modulate(rms_norm(x, norm_g[layer, 2]), mx[6], mx[7]),
                                     ffn_w_in[layer, 1], ffn_w_out[layer, 1])
        if not last:
            xc = xc + mc[5] * oc
            xc = xc + 0.5 * mc[8] * swiglu(modulate(rms_norm(xc, norm_g[layer, 2]), mc[6], mc[7]),
                                           ffn_w_in[layer, 1], ffn_w_out[layer, 1])
    return rms_norm(x, final_norm_g)


def setup_inputs(seed=0):
    out = dict(first_inputs(seed))
    for name, value in second_inputs(seed + 1).items():
        if name != "x":
            out[name + "_2"] = value
    return out


def reference(
    x, p, w_in, b_forget, w_up_fox, w_up_sb, w_up_dsa, w_out, ln1_g, ln1_b, w_ff_in, w_ff_out,
    w_ple, w_ple_gate, ln2_g, ln2_b, c_2, ctx_2, c_ctx_2, mod_w_2, mod_b_2, norm_g_2,
    final_norm_g_2, ffn_w_in_2, ffn_w_out_2, mla_w_down_2, mla_q_norm_2, mla_kv_norm_2,
    mla_w_uq_2, mla_w_ukv_2, mla_w_o_2, swa_w_qkv_2, swa_sink_2, swa_w_o_2, na_w_qkv_2,
    na_rpb_2, na_w_o_2, diff_w_qkv_2, diff_lambda_2, diff_norm_g_2, diff_w_o_2,
):
    x = first_block(
        x, p, w_in, b_forget, w_up_fox, w_up_sb, w_up_dsa, w_out, ln1_g, ln1_b, w_ff_in,
        w_ff_out, w_ple, w_ple_gate, ln2_g, ln2_b,
    )
    return second_block(
        x, c_2, ctx_2, c_ctx_2, mod_w_2, mod_b_2, norm_g_2, final_norm_g_2, ffn_w_in_2,
        ffn_w_out_2, mla_w_down_2, mla_q_norm_2, mla_kv_norm_2, mla_w_uq_2, mla_w_ukv_2,
        mla_w_o_2, swa_w_qkv_2, swa_sink_2, swa_w_o_2, na_w_qkv_2, na_rpb_2, na_w_o_2,
        diff_w_qkv_2, diff_lambda_2, diff_norm_g_2, diff_w_o_2,
    )


_drawn_inputs = setup_inputs


def setup_inputs(seed=0):
    import zlib

    import numpy as np

    out = dict(_drawn_inputs(seed))
    spreads = {}
    factors = {'b_forget': 2.977,
     'mod_b_2': 2.841,
     'norm_g_2': 8.0,
     'final_norm_g_2': 2.775,
     'mla_q_norm_2': 8.0,
     'mla_kv_norm_2': 8.0,
     'swa_sink_2': 8.0}
    for name, (base, spread) in spreads.items():
        noise = np.random.default_rng([zlib.crc32(name.encode()), seed]).standard_normal(out[name].shape)
        drawn = base * np.exp(spread * noise) if base else spread * noise
        out[name] = jnp.asarray(drawn.astype(out[name].dtype))
    for name, factor in factors.items():
        out[name] = (out[name] * factor).astype(out[name].dtype)
    return out
```

```python
from contextlib import ExitStack

import concourse.bass as bass
import concourse.mybir as mybir
import numpy as np

F32 = mybir.dt.float32
F32R = mybir.dt.float32r
ALU = mybir.AluOpType
ACT = mybir.ActivationFunctionType
AX = mybir.AxisListType

P = 128
D = 1024
KT = D // P
S = 256
LAYERS = 2
DH = 64
HALF = 64

W_FOX, W_SB, W_DSA = 6 * DH, 5 * DH, 5 * DH
IDX_HEADS = 8
FQ, FK, FV = 0, W_FOX, 2 * W_FOX
FF = 3 * W_FOX
SQ = FF + 6
SK, SV = SQ + W_SB, SQ + 2 * W_SB
DQ = SQ + 3 * W_SB
DK = DQ + W_DSA
DV = DK + DH
IQ = DV + DH
IK = IQ + IDX_HEADS * DH
IW = IK + DH
GATE = IW + IDX_HEADS
D_FF = 4 * D
ALPHA = (2 * LAYERS) ** 0.25
LN_EPS = 1e-5
TOPK = min(256, S // 4)
SCALE = DH ** -0.5
NEG = -1e30
MARK = -3e38
N_MOD = 9
D_FF2 = 2816
FT2 = D_FF2 // P
HT = FT2 // 2
RMS_EPS = 1e-6
Q_RANK, KV_RANK = 512, 256
NOPE, ROPE, MV = 128, 64, 128
MLA_H = 8
MLA_SCALE = (NOPE + ROPE) ** -0.5
WINDOW = 128
SWA_H, SWA_KV = 16, 4

SLOTS = 3
CHUNK = 2048
LANDED = 128

T_FQ, T_FK, T_SQ, T_SK, T_SK4, T_SQ4, T_DQ, T_DK, T_IQ, T_IK = 0, 3, 6, 8, 10, 11, 12, 14, 15, 19
QK_TILES = 20
QKV_PIECES = [
    [(0, FQ, 256)], [(0, FQ + 256, 256)], [(0, FQ + 512, 256)],
    [(0, SQ, 256)], [(0, SK, 256)],
    [(0, SK + 256, 64), (64, FF, 6), (70, IW, 8), (128, SQ + 256, 64), (192, DQ + 256, 64)],
    [(0, DQ, 256)],
    [(0, DK, 64), (64, DK, 64), (128, IQ, 128)],
    [(0, IQ + 128, 256)],
    [(0, IQ + 384, 128), (128, IK, 64), (192, IK, 64)],
    [(0, FV, 256)],
    [(0, FV + 256, 128), (128, SV, 128)],
    [(0, SV + 128, 192), (192, DV, 64)],
]
FF_COL, IW_COL = 64, 70

MAIN = ([("qk", c) for c in range(10)] + [("v", c) for c in range(3)]
        + [("gate", (0, c)) for c in range(4)] + [("gate", (1, c)) for c in range(4)]
        + [("up", (0, c)) for c in range(2)] + [("gate", (2, c)) for c in range(4)]
        + [("up", (1, c)) for c in range(2)] + [("up", (2, c)) for c in range(2)]
        + [("out", c) for c in range(4)] + [("plegate", c) for c in range(4)] + [("ple", 0)]
        + [("ffin", c) for c in range(16)] + [("ffout", (c, k)) for c in range(8) for k in range(2)])
MODS = 36
CHUNKS1 = len(MAIN) + MODS
assert len(MAIN) == 2 * MODS and CHUNKS1 % SLOTS == 0


def stream1():
    out = []
    for m, item in enumerate(MAIN):
        out.append(item)
        if m % 2:
            out.append(("mod", m // 2))
    return out


HEADS = [("fox", h) for h in range(6)] + [("sb", h) for h in range(5)] + [("dsa", h) for h in range(5)]


def attention_script():
    fill = {0: 1, 1: 1, 2: 1, 3: 1,
            6: 1, 7: 1, 8: 1, 9: 1, 10: 2}
    out = []

    def close(a):
        out.append(("weigh", a))

    for a, (kind, h) in enumerate(HEADS):
        if kind == "dsa" and h == 0:
            out.append(("turn", a - 1))
            out.append(("weigh", a - 1))
            for i in range(IDX_HEADS):
                out.append(("index", i))
                if i % 2:
                    out.append(("chunk", None))
            out.append(("topk", None))
            out.append(("chunk", None))
            out.append(("chunk", None))
        if kind == "fox":
            out.append(("decay", a))
        out.append(("score", a))
        if a and not (kind == "dsa" and h == 0):
            out.append(("turn", a - 1))
        out += [("chunk", None)] * fill.get(a, 0)
        if a and not (kind == "dsa" and h == 0):
            close(a - 1)
    out.append(("turn", len(HEADS) - 1))
    out.append(("weigh", len(HEADS) - 1))
    return out


SCRIPT = attention_script()


def head_place(kind, h):
    if kind == "fox":
        return T_FQ + h // 2, T_FK + h // 2, h % 2, DH * h
    if kind == "sb":
        return (T_SQ4, T_SK4, 0, W_FOX + DH * h) if h == 4 else (T_SQ + h // 2, T_SK + h // 2, h % 2, W_FOX + DH * h)
    return (T_SQ4, T_DK, 1, W_FOX + W_SB) if h == 4 else (T_DQ + h // 2, T_DK, h % 2, W_FOX + W_SB)


def ends_tile(kind, h):
    return h % 2 == 1 or (kind != "fox" and h == 4)


SPLIT_TILES = (HT - 2, HT - 1)
FFN_CHUNKS = HT + len(SPLIT_TILES) + KT
assert FFN_CHUNKS % SLOTS == 0
MLA_UNITS = [(h, part) for h in range(MLA_H) for part in range(3)]
SWA_UNITS = [(h, part) for h in range(SWA_H) for part in range(2)]


def mla_end(unit):
    return (unit[0], 2 * S) if unit[1] == 2 else None


def swa_end(unit):
    return (unit[0] // 2, S) if unit[0] % 2 and unit[1] else None


def streams(width):
    return [(s, slice(S * s, S * s + S)) for s in range(width // S)]


class Counts:

    def __init__(self, eng, per_pass, measured):
        self.eng, self.per_pass, self.measured = eng, per_pass, measured
        self.seen, self.made = {}, {}
        self.i = self.loop = self.last = None

    def value(self, sem, n):
        if self.i is None:
            return n
        return n + self.i * self.per_pass[self.loop].get(sem.name, 0)

    def next(self, sem, k=1):
        self.seen[sem] = self.seen.get(sem, 0) + k
        return self.value(sem, self.seen[sem])

    def did(self, sem, k=1):
        self.made[sem] = self.made.get(sem, 0) + k
        self.last = sem
        return k

    def own(self):
        return self.value(self.last, self.made[self.last])

    def credit(self, sem, k=1):
        self.eng.sem_inc(sem, k)
        self.made[sem] = self.made.get(sem, 0) + k

    def passes(self, name, times, *rings):
        before = dict(self.seen), dict(self.made), [r.used for r in rings]
        for r in rings:
            r.seam()
        with self.eng.Fori(0, times) as i:
            self.i, self.loop = i, name
            yield i
            self.i = self.loop = None
        for r, n in zip(rings, before[2]):
            r.seam()
            self.note(name, r.free.name, r.used - n)
            r.used += (times - 1) * (r.used - n)
            r.seam()
        for now, then in ((self.seen, before[0]), (self.made, before[1])):
            for sem, n in now.items():
                step = n - then.get(sem, 0)
                if step:
                    self.note(name, sem.name, step)
                    now[sem] = n + (times - 1) * step

    def note(self, name, sem, step):
        had = self.measured.setdefault(name, {}).setdefault(sem, step)
        assert had == step, (name, sem, had, step)


class Ring:

    def __init__(self, counts, banks, full, free):
        self.counts, self.banks, self.full, self.free = counts, banks, full, free
        self.used = 0
        self.at = 0
        self.last_use = [0] * len(banks)

    def awaited(self):
        return self.counts.value(self.free, self.last_use[self.at % len(self.banks)] + 1)

    def all_used(self):
        return self.counts.value(self.free, self.used + 1)

    def claim(self):
        b = self.at % len(self.banks)
        self.at += 1
        self.used += 1
        self.last_use[b] = self.used
        return self.banks[b]

    def seam(self):
        self.at = 0
        self.last_use = [self.used] * len(self.banks)

def constants():
    p = np.arange(P)[:, None]
    k = np.arange(P)[None, :]
    f = np.float32
    zeros = np.zeros((P, P), f)
    out = {"ident": np.eye(P, dtype=f), "ones": np.ones((P, P), f)}
    r = np.zeros((P, P), f)
    for h in (0, HALF):
        for j in range(32):
            r[h + 32 + j, h + j] = -1
            r[h + j, h + 32 + j] = 1
    out["rot"] = r
    out["neg_tri"] = np.where(p >= k, -1, 0).astype(f)
    out["neg_ones"] = np.full((P, P), -1, f)
    out["row_mask"] = np.concatenate([zeros, np.where(k > p, NEG / SCALE, 0)], 1).astype(f)
    out["sb_mask"] = np.concatenate([np.where(p < k, 0, NEG), zeros], 1).astype(f)
    out["idx_mask"] = np.concatenate([zeros, np.where((p < 64) & (k >= 64), NEG, 0)], 1).astype(f)
    pos = np.arange(S, dtype=f)
    inv = f(10000.0) ** (-np.arange(32, dtype=f) / f(32))
    ang = (pos[:, None] * inv[None, :]).astype(f).T
    for name, fn, idle in (("cos", np.cos, 1), ("sin", np.sin, 0)):
        t = np.tile(fn(ang).astype(f), (4, 1))
        a = t.copy()
        a[:HALF] = idle
        out[name + "_a"], out[name + "_b"] = a, t
    inv = np.exp(f(-np.log(10000.0)) * np.arange(16, dtype=f) / f(16)).astype(f)
    row, col = (np.arange(S) // 64).astype(f), (np.arange(S) % 64).astype(f)
    ang = np.concatenate([row[:, None] * inv, col[:, None] * inv], -1).astype(f).T
    out["cos_2"], out["sin_2"] = (np.tile(fn(ang).astype(f), (4, 1)) for fn in (np.cos, np.sin))
    q, kk = np.arange(P)[:, None], np.arange(S)[None, :]
    out["win_mask"] = np.concatenate([np.where(abs(kk - (q + P * b)) <= WINDOW, 0, NEG / SCALE) for b in range(2)], 1).astype(f)
    return out


FIXED_CONSTS = {"ident": P, "ones": P, "rot": P}
PHASE1_CONSTS = {"neg_tri": P, "neg_ones": P, "row_mask": S, "sb_mask": S, "idx_mask": S,
                 "cos_a": S, "sin_a": S, "cos_b": S, "sin_b": S}
PHASE2_CONSTS = {"cos_2": S, "sin_2": S, "win_mask": 2 * S}
CONST_AT = {}
for _group in (FIXED_CONSTS, PHASE1_CONSTS, PHASE2_CONSTS):
    _a = 0
    for _name, _n in _group.items():
        CONST_AT[_name] = (_a, _n)
        _a += _n
N_FIXED = sum(FIXED_CONSTS.values())
N_PHASE = sum(PHASE1_CONSTS.values())
N_PHASE2 = sum(PHASE2_CONSTS.values())
N_ROWS_DMA = 4 * LAYERS + LAYERS + 1 + LAYERS + 4

PER_PASS = {'ffn00': {'a_free': 11,
           'a_full': 11,
           'chunk_used': 21,
           'd_free': 19,
           'd_full': 19,
           'hi_made': 21,
           'landed0': 896,
           'landed1': 896,
           'landed2': 896,
           'lo_made': 21,
           's_free': 0,
           't_free': 0,
           'unit_hi_made': 11,
           'unit_lo_made': 11,
           'unit_ready': 11,
           'v_free': 0,
           'v_step': 8},
 'ffn01': {'a_free': 11,
           'a_full': 11,
           'chunk_used': 21,
           'd_free': 19,
           'd_full': 19,
           'hi_made': 21,
           'landed0': 896,
           'landed1': 896,
           'landed2': 896,
           'lo_made': 21,
           's_free': 0,
           't_free': 0,
           'unit_hi_made': 11,
           'unit_lo_made': 11,
           'unit_ready': 11,
           'v_free': 0,
           'v_step': 8},
 'ffn10': {'a_free': 11,
           'a_full': 11,
           'chunk_used': 21,
           'd_free': 19,
           'd_full': 19,
           'hi_made': 21,
           'landed0': 896,
           'landed1': 896,
           'landed2': 896,
           'lo_made': 21,
           's_free': 0,
           't_free': 0,
           'unit_hi_made': 11,
           'unit_lo_made': 11,
           'unit_ready': 11,
           'v_free': 0,
           'v_step': 8},
 'ffn11': {'a_free': 11,
           'a_full': 11,
           'chunk_used': 21,
           'd_free': 19,
           'd_full': 19,
           'hi_made': 21,
           'landed0': 896,
           'landed1': 896,
           'landed2': 896,
           'lo_made': 21,
           's_free': 0,
           't_free': 0,
           'unit_hi_made': 11,
           'unit_lo_made': 11,
           'unit_ready': 11,
           'v_free': 0},
 'layers': {'a_free': 40,
            'a_full': 40,
            'a_step': 8,
            'abs_ready': 5,
            'arg_ready': 5,
            'bf_in': 16,
            'centred': 2,
            'chunk_used': 108,
            'd_free': 90,
            'd_full': 90,
            'exp_made': 22,
            'f_hi_made': 16,
            'f_lo_made': 16,
            'ff_abs': 1,
            'ff_log': 1,
            'ff_sum': 1,
            'gate_used': 12,
            'hi_made': 108,
            'landed0': 4608,
            'landed1': 4608,
            'landed2': 4608,
            'lo_made': 108,
            'log_made': 5,
            'logits_ready': 11,
            'm_hi_made': 1,
            'm_lo_made': 1,
            'm_ready': 1,
            'o_hi_made': 9,
            'o_lo_made': 9,
            'o_ready': 9,
            'p_copied': 1,
            'p_hi_made': 1,
            'p_in': 16,
            'p_lo_made': 1,
            'p_room': 1,
            'relu_used': 8,
            'roped': 5,
            'rstd_made': 2,
            's_free': 20,
            's_full': 18,
            'soft_ready': 5,
            'squared': 2,
            'stick_ready': 5,
            't_free': 17,
            't_full': 17,
            'v_free': 9,
            'v_full': 16,
            'v_step': 207,
            'var_full': 2,
            'weights_ready': 11,
            'x_hi_made': 2,
            'x_lo_made': 2,
            'x_ready': 2}}


def build(nc, dram, out, per_pass, measured, stop=None):
    ctx = ExitStack()
    with ctx:
        def sem(name):
            return ctx.enter_context(nc.semaphore(name))

        base = (nc.sbuf_base + 31) // 32 * 32
        top = [base]

        def fixed(name, shape, dt=F32):
            size = 4 * int(np.prod(shape[1:]))
            t = nc.alloc_sbuf_tensor_at(name, shape, dt, offset=top[0])
            top[0] += (size + 31) // 32 * 32
            return t

        raw = [fixed(f"raw{s}", [P, CHUNK]) for s in range(SLOTS)]
        w_hi = [fixed(f"w_hi{s}", [P, CHUNK], F32R) for s in range(SLOTS)]
        w_lo = [fixed(f"w_lo{s}", [P, CHUNK], F32R) for s in range(SLOTS)]
        xs = fixed("xs", [P, KT, 2 * S])
        cst = fixed("cst", [P, N_FIXED])
        phase = fixed("phase", [P, N_PHASE])
        cols_a = fixed("cols_a", [P, 120])
        cols_mod = fixed("cols_mod", [P, LAYERS, 72])
        cols_d = fixed("cols_d", [P, 22])
        bf = fixed("bf", [P, 1])
        ln_cols = fixed("ln_cols", [P, 4, KT])
        mods = fixed("mods", [P, LAYERS, 144])
        cond_hi = fixed("cond_hi", [P, KT, 2], F32R)
        cond_lo = fixed("cond_lo", [P, KT, 2], F32R)
        cond = fixed("cond", [P, 2, KT])
        small = fixed("small", [P, 64])
        eps1 = small[:, 0:1]
        eps2 = small[:, 1:2]
        one = small[:, 2:3]
        stat = [small[:, 8 + 8 * b:16 + 8 * b] for b in range(3)]
        amod = fixed("amod", [P, KT, 2])
        hgate = fixed("hgate", [P, KT, 2])
        sink = fixed("sink", [P, SWA_H])
        nsink = fixed("nsink", [P, SWA_H])
        cq8 = fixed("cq8", [P, 2, 6])
        iwt = fixed("iwt", [P, 2, 8])
        top8 = fixed("top8", [P, 2, 8])
        t1 = fixed("t1", [P, 2, 512])
        t2 = fixed("t2", [P, 2, 512])
        t3 = fixed("t3", [P, 2, 512])
        prob = [t1[:, 0, :], t1[:, 1, :], t3[:, 0, :]]
        work = top[0]

        def mod_col(l, j, k, s):
            a = 16 * j + 2 * k + s
            return mods[:, l, a:a + 1]
        assert work + 94 * 1024 <= nc.sbuf_usable_end, (work, nc.sbuf_usable_end)

        def at(name, kib, shape, dt=F32):
            t = nc.alloc_sbuf_tensor_at(name, shape, dt, offset=work + int(kib * 1024))
            assert kib * 1024 + 4 * int(np.prod(shape[1:])) <= 94 * 1024, name
            return t

        x_hi = at("x_hi", 0, [P, KT, S], F32R)
        x_lo = at("x_lo", 8, [P, KT, S], F32R)
        qk = at("qk", 16, [P, QK_TILES, S])
        v_tok = at("v_tok", 36, [P, 2, 768])
        gates = at("gates", 43, [P, 2, KT, S])
        o_hi = at("o_hi", 59, [P, 2, 3, S], F32R)
        o_lo = at("o_lo", 65, [P, 2, 3, S], F32R)
        decay = at("decay", 71, [P, 2, 384])
        score = at("score", 74, [P, 384])
        chosen = at("chosen", 75.5, [P, 384])
        o32 = at("o32", 77, [P, 2, S])
        merged = at("merged", 79, [P, KT, S])
        p_tok = at("p_tok", 87, [P, 2, 256])
        p_hi = at("p_hi", 89, [P, 2, S], F32R)
        p_lo = at("p_lo", 91, [P, 2, S], F32R)
        m_hi = at("m_hi", 16, [P, KT, S], F32R)
        m_lo = at("m_lo", 24, [P, KT, S], F32R)
        f_hi = at("f_hi", 16, [P, 32, S], F32R)
        f_lo = at("f_lo", 48, [P, 32, S], F32R)
        sq1 = at("sq1", 80, [P, KT, S])
        ple_g = at("ple_g", 80, [P, KT, S])
        rows_a = at("rows_a", 32, [P, P])
        rows_m = at("rows_m", 33, [P, LAYERS, P])
        rows_d = at("rows_d", 35, [P, P])
        x_tok = at("x_tok", 40, [P, 2, D])
        c_tok = at("c_tok", 48, [P, 2, D])
        y_tok = at("y_tok", 60, [P, 2, D])

        h_hi = at("h_hi", 0, [P, KT, 2 * S], F32R)
        h_lo = at("h_lo", 16, [P, KT, 2 * S], F32R)
        un_hi = at("un_hi", 32, [P, HT, 2 * S], F32R)
        un_lo = at("un_lo", 54.5, [P, HT, 2 * S], F32R)
        sq2 = at("sq2", 78, [P, KT, 2 * S])
        qn = at("qn", 0, [P, MLA_H, 2 * S])
        kn = at("kn", 16, [P, MLA_H, 2 * S])
        cqkv = at("cqkv", 32, [P, 6, 2 * S])
        vm = at("vm", 32, [P, 4, D])
        sqm = at("sqm", 44, [P, 6, 2 * S])
        cq_hi = at("cq_hi", 44, [P, 4, 2 * S], F32R)
        cq_lo = at("cq_lo", 52, [P, 4, 2 * S], F32R)
        ckv_hi = at("ckv_hi", 60, [P, 2, 2 * S], F32R)
        ckv_lo = at("ckv_lo", 64, [P, 2, 2 * S], F32R)
        om_hi = at("om_hi", 48, [P, KT, 2 * S], F32R)
        om_lo = at("om_lo", 64, [P, KT, 2 * S], F32R)
        qr = at("qr", 80, [P, 4, 2 * S])
        qrot = at("qrot", 88, [P, 4, S])
        kr = at("kr", 92, [P, 2 * S])
        q2 = at("q2", 32, [P, KT, S])
        q2rot = at("q2rot", 40, [P, KT, S])
        kd = at("kd", 48, [P, SWA_KV, 2 * S])
        vw = at("vw", 56, [P, 4, SWA_KV * DH])
        ow_hi = at("ow_hi", 60, [P, KT, S], F32R)
        ow_lo = at("ow_lo", 68, [P, KT, S], F32R)

        def const(t, name):
            a, n = CONST_AT[name]
            return t[:, a:a + n]

        ident, ones, rot = (const(cst, n) for n in ("ident", "ones", "rot"))
        neg_tri, neg_ones, row_mask, sb_mask, idx_mask = (
            const(phase, n) for n in ("neg_tri", "neg_ones", "row_mask", "sb_mask", "idx_mask"))
        cos_a, sin_a, cos_b, sin_b = (const(phase, n) for n in ("cos_a", "sin_a", "cos_b", "sin_b"))
        cos_2, sin_2, win_mask = (const(phase, n) for n in ("cos_2", "sin_2", "win_mask"))

        bank = [nc.alloc_psum_tensor(f"bank{b}", [P, 512], F32) for b in range(8)]

        landed = [sem(f"landed{s}") for s in range(SLOTS)]
        hi_made, lo_made, chunk_used = sem("hi_made"), sem("lo_made"), sem("chunk_used")
        raw_set = sem("raw_set")
        consts_in, rows_in, x_in, bf_in, p_in, phase_in = (
            sem(n) for n in ("consts_in", "rows_in", "x_in", "bf_in", "p_in", "phase_in"))
        d_full, d_free = sem("d_full"), sem("d_free")
        a_full, a_free = sem("a_full"), sem("a_free")
        s_full, s_free = sem("s_full"), sem("s_free")
        t_full, t_free = sem("t_full"), sem("t_free")
        v_full, v_free = sem("v_full"), sem("v_free")
        apart = sem("apart")
        v_step, a_step = sem("v_step"), sem("a_step")
        x_copied = sem("x_copied")
        x_ready, x_hi_made, x_lo_made = sem("x_ready"), sem("x_hi_made"), sem("x_lo_made")
        cond_exp, cond_ready, cond_hi_made, cond_lo_made = (
            sem(n) for n in ("cond_exp", "cond_ready", "cond_hi_made", "cond_lo_made"))
        p_room, p_copied, p_hi_made, p_lo_made = (sem(n) for n in ("p_room", "p_copied", "p_hi_made", "p_lo_made"))
        roped = sem("roped")
        ff_abs, ff_log, ff_sum = sem("ff_abs"), sem("ff_log"), sem("ff_sum")
        logits_ready, exp_made, weights_ready, turned = (
            sem(n) for n in ("logits_ready", "exp_made", "weights_ready", "turned"))
        abs_ready, log_made, soft_ready, arg_ready, stick_ready = (
            sem(n) for n in ("abs_ready", "log_made", "soft_ready", "arg_ready", "stick_ready"))
        relu_made, relu_used = sem("relu_made"), sem("relu_used")
        o_ready, o_hi_made, o_lo_made = sem("o_ready"), sem("o_hi_made"), sem("o_lo_made")
        gate_exp, gate_used = sem("gate_exp"), sem("gate_used")
        m_ready, m_hi_made, m_lo_made = sem("m_ready"), sem("m_hi_made"), sem("m_lo_made")
        centred, squared, var_full, rstd_made, result_ready = (
            sem(n) for n in ("centred", "squared", "var_full", "rstd_made", "result_ready"))
        ple_exp = sem("ple_exp")
        relu2_made, f_hi_made, f_lo_made = sem("relu2_made"), sem("f_hi_made"), sem("f_lo_made")
        u_ready, h_hi_made, h_lo_made = sem("u_ready"), sem("h_hi_made"), sem("h_lo_made")
        unit_ready, unit_hi_made, unit_lo_made = sem("unit_ready"), sem("unit_hi_made"), sem("unit_lo_made")
        cq_ready, q_ready = sem("cq_ready"), sem("q_ready")
        turn_full = sem("turn_full")
        o_full, o_free = sem("o_full"), sem("o_free")
        stored, y_copied = sem("stored"), sem("y_copied")

        block = ctx.enter_context(nc.Block())

        @block.sync
        def _(sp):
            c = Counts(sp, per_pass, measured)
            n = [0]

            def chunk(pieces):
                s = n[0] % SLOTS
                sp.wait_ge(lo_made, c.value(lo_made, n[0] + 1))
                for k, (dst, src) in enumerate(pieces(raw[s])):
                    last = k == len(pieces(raw[s])) - 1
                    sp.dma_start(dst, src).then_inc(landed[s], c.did(landed[s], LANDED - 16 * k if last else 16))
                n[0] += 1

            def view(slot, kt, width):
                return slot[:, 0:kt * width].rearrange("p (k n) -> p k n", k=kt)

            def whole(src, kt, width):
                return lambda slot: [(view(slot, kt, width), src.rearrange("(k p) n -> p k n", p=P))]

            sp.dma_start(cst[:, :], dram["constants"][:, 0:N_FIXED]).then_inc(consts_in, 16)
            sp.dma_start(phase[:, :], dram["constants"][:, N_FIXED:N_FIXED + N_PHASE]).then_inc(consts_in, 16)
            rows = 0
            for l in range(LAYERS):
                for name in ("ln1_g", "ln1_b", "ln2_g", "ln2_b"):
                    sp.dma_start(rows_a[rows:rows + KT, :], dram[name][l].rearrange("(t p) -> t p", p=P)).then_inc(rows_in, 16)
                    rows += KT
            for l in range(LAYERS):
                sp.dma_start(rows_a[rows:rows + 24, :], dram["norm_g_2"][l].rearrange("a (t p) -> (a t) p", p=P)).then_inc(rows_in, 16)
                rows += 24
            sp.dma_start(rows_a[rows:rows + KT, :], dram["final_norm_g_2"].rearrange("(t p) -> t p", p=P)).then_inc(rows_in, 16)
            for l in range(LAYERS):
                sp.dma_start(rows_m[0:72, l, :], dram["mod_b_2"][l].rearrange("(t p) -> t p", p=P)).then_inc(rows_in, 16)
            sp.dma_start(rows_d[0:4, :], dram["mla_q_norm_2"][0].rearrange("(t p) -> t p", p=P)).then_inc(rows_in, 16)
            sp.dma_start(rows_d[4:6, :], dram["mla_kv_norm_2"][0].rearrange("(t p) -> t p", p=P)).then_inc(rows_in, 16)
            sp.dma_start(rows_d[6:14, :], dram["c_2"][0].rearrange("(t p) -> t p", p=P)).then_inc(rows_in, 16)
            sp.dma_start(rows_d[14:22, :], dram["c_ctx_2"].rearrange("(t p) -> t p", p=P)).then_inc(rows_in, 16)
            sp.dma_start(x_tok[:, :, :], dram["x"][0].rearrange("(t p) d -> p t d", p=P)).then_inc(x_in, 16)
            sp.dma_start(c_tok[:, :, :], dram["ctx_2"][0].rearrange("(t p) d -> p t d", p=P)).then_inc(x_in, 16)
            sp.wait_ge(raw_set, c.value(raw_set, 1))

            for i in c.passes("layers", LAYERS):
                w_in, ups = dram["w_in"][i], [dram[k][i] for k in ("w_up_fox", "w_up_sb", "w_up_dsa")]

                def qkv(pieces):
                    return lambda slot: [(view(slot, KT, 256)[:, :, a:a + w],
                                          w_in[:, b:b + w].rearrange("(k p) n -> p k n", p=P)) for a, b, w in pieces]

                def up(b, half):
                    src, cols = ups[b], slice(512 * half, 512 * half + 512)
                    if b == 0:
                        return whole(src[:, cols], 3, 512)
                    return lambda slot: [
                        (view(slot, 3, 512)[:, 0:2, :], src[0:256, cols].rearrange("(k p) n -> p k n", p=P)),
                        (view(slot, 3, 512)[0:HALF, 2, :], src[256:320, cols])]

                for k, (kind, what) in enumerate(stream1()):
                    if k == 6:
                        sp.wait_ge(p_room, c.next(p_room))
                        sp.dma_start(p_tok[:, :, :], dram["p"][i, 0].rearrange("(t p) d -> p t d", p=P)).then_inc(p_in, c.did(p_in, 16))
                        sp.dma_start(bf[FF_COL:FF_COL + 6, :], dram["b_forget"][i].rearrange("(a b) -> a b", b=1)).then_inc(bf_in, c.did(bf_in, 16))
                    if kind in ("qk", "v"):
                        chunk(qkv(QKV_PIECES[what + (10 if kind == "v" else 0)]))
                    elif kind == "gate":
                        chunk(qkv([(0, GATE + D * what[0] + 256 * what[1], 256)]))
                    elif kind == "up":
                        chunk(up(*what))
                    elif kind == "mod":
                        chunk(whole(dram["mod_w_2"][i][:, 256 * what:256 * what + 256], KT, 256))
                    elif kind == "out":
                        chunk(whole(dram["w_out"][i][:, 256 * what:256 * what + 256], KT, 256))
                    elif kind == "plegate":
                        chunk(whole(dram["w_ple_gate"][i][:, 256 * what:256 * what + 256], KT, 256))
                    elif kind == "ple":
                        chunk(whole(dram["w_ple"][i], 2, D))
                    elif kind == "ffin":
                        chunk(whole(dram["w_ff_in"][i][:, 256 * what:256 * what + 256], KT, 256))
                    else:
                        col, k2 = what
                        chunk(whole(dram["w_ff_out"][i][2048 * k2:2048 * k2 + 2048, P * col:P * col + P], 16, P))
            n[0] += (LAYERS - 1) * CHUNKS1
            sp.wait_ge(m_ready, LAYERS)
            sp.dma_start(phase[:, 0:N_PHASE2], dram["constants"][:, N_FIXED + N_PHASE:]).then_inc(phase_in, 16)
            sp.dma_start(sink[:, :], dram["swa_sink_2"][0:1, :].to_broadcast([P, SWA_H])).then_inc(phase_in, 16)

            def each_k(srcs, kt, heads, width):
                def pieces(slot):
                    v = slot[:, 0:kt * heads * width].rearrange("p (k h n) -> p k h n", k=kt, h=heads)
                    return [(v[:, k], srcs(k)) for k in range(kt)]
                return pieces

            def unit_ffn(l, which):
                w_in, w_out = dram["ffn_w_in_2"][l, which], dram["ffn_w_out_2"][l, which]
                for j in c.passes(f"ffn{l}{which}", 2):
                    for t in range(HT):
                        g, u = (w_in[:, bass.ds(j * (HT * P) + (a + P * t), P)].rearrange("(k p) n -> p k n", p=P)
                                for a in (0, D_FF2))
                        if t in SPLIT_TILES:
                            chunk(lambda slot: [(view(slot, KT, P), g)])
                            chunk(lambda slot: [(view(slot, KT, P), u)])
                        else:
                            chunk(lambda slot: [(view(slot, KT, 2 * P)[:, :, 0:P], g), (view(slot, KT, 2 * P)[:, :, P:2 * P], u)])
                    for t in range(KT):
                        chunk(whole(w_out[bass.ds(j * (HT * P), HT * P), P * t:P * t + P], HT, P))
                n[0] += FFN_CHUNKS

            def columns(w, cols):
                return lambda slot: [(view(slot, KT, 256)[:, :, a:a + z], w[:, b:b + z].rearrange("(k p) n -> p k n", p=P))
                                     for a, b, z in cols]

            unit_ffn(0, 0)
            down = dram["mla_w_down_2"][0]
            for q in range(3):
                chunk(whole(down[:, 256 * q:256 * q + 256], KT, 256))
            kr_src = down[:, Q_RANK + KV_RANK:].rearrange("(k p) n -> p k n", p=P)
            chunk(lambda slot: [(view(slot, KT, P)[:, :, 0:ROPE], kr_src), (view(slot, KT, P)[:, :, ROPE:P], kr_src)])
            uq = dram["mla_w_uq_2"][0].rearrange("(k p) (h n) -> k p h n", p=P, h=MLA_H)
            ukv = dram["mla_w_ukv_2"][0].rearrange("(k p) (h n) -> k p h n", p=P, h=MLA_H)
            for q in range(2):
                chunk(each_k(lambda k: uq[k][:, 4 * q:4 * q + 4, 0:NOPE], 4, 4, NOPE))
            chunk(each_k(lambda k: uq[k][:, :, NOPE:NOPE + ROPE], 4, MLA_H, ROPE))
            chunk(each_k(lambda k: ukv[k][:, :, 0:NOPE], 2, MLA_H, NOPE))
            chunk(each_k(lambda k: ukv[k][:, :, NOPE:NOPE + MV], 2, MLA_H, MV))
            for q in range(4):
                chunk(whole(dram["mla_w_o_2"][0][:, 256 * q:256 * q + 256], KT, 256))
            unit_ffn(0, 1)
            unit_ffn(1, 0)
            qkv_w = dram["swa_w_qkv_2"][0]
            k_at, v_at = SWA_H * DH, (SWA_H + SWA_KV) * DH
            for q in range(2):
                chunk(columns(qkv_w, [(DH * j, k_at + DH * (2 * q + j // 2), DH) for j in range(4)]))
            chunk(columns(qkv_w, [(0, v_at, 256)]))
            for q in range(4):
                chunk(columns(qkv_w, [(0, 256 * q, 256)]))
            for q in range(4):
                chunk(columns(dram["swa_w_o_2"][0], [(0, 256 * q, 256)]))
            unit_ffn(1, 1)
            for _ in range(2):
                sp.wait_ge(lo_made, c.value(lo_made, n[0] + 1))
                sp.sem_inc(landed[n[0] % SLOTS], LANDED)
                n[0] += 1
            sp.wait_ge(y_copied, 1)
            sp.dma_start(out.rearrange("(t p) d -> p t d", p=P), y_tok[:, :, :]).then_inc(stored, 16)
            sp.wait_ge(stored, 16)

        @block.scalar
        def _(act):
            c = Counts(act, per_pass, measured)
            n = [0]

            def prep(upto):
                while n[0] <= upto:
                    s = n[0] % SLOTS
                    act.wait_ge(landed[s], c.value(landed[s], LANDED * (n[0] // SLOTS + 1)))
                    act.wait_ge(chunk_used, c.value(chunk_used, n[0] + 1))
                    act.copy(w_hi[s][:, :], raw[s][:, :]).then_inc(hi_made, c.did(hi_made))
                    n[0] += 1

            def do(func, o, i, bias=0.0, scale=1.0, **kw):
                return act.activation(o, i, func, bias=bias, scale=scale, **kw)

            def split_hi(dst, src, ready, made):
                act.wait_ge(ready, c.next(ready))
                act.wait_ge(c.last, c.own())
                do(ACT.Copy, dst, src).then_inc(made, c.did(made))

            def rstd(b, width, cnt, eps):
                act.wait_ge(var_full, c.next(var_full))
                act.wait_ge(c.last, c.own())
                do(ACT.Ln, t1[:, 0, 0:width], b[:, 0:width], bias=eps, scale=1.0 / cnt).then_inc(a_step, c.did(a_step))
                act.wait_ge(c.last, c.own())
                do(ACT.Exp, t1[:, 1, 0:width], t1[:, 0, 0:width], scale=-0.5).then_inc(rstd_made, c.did(rstd_made))

            a_at = [0]
            used = [0]

            def passed():
                prep(used[0] + 2)
                used[0] += 1

            c.credit(a_free)
            act.wait_ge(raw_set, 1)
            prep(1)
            act.wait_ge(cond_ready, c.next(cond_ready))
            act.wait_ge(c.last, c.own())
            do(ACT.Exp, t3[:, 0, 0:16].rearrange("p (c k) -> p c k", c=2), cond[:, :, :], scale=-1.0).then_inc(cond_exp, c.did(cond_exp))
            act.wait_ge(cond_ready, c.next(cond_ready))
            act.wait_ge(c.last, c.own())
            do(ACT.Copy, cond_hi[:, :, :].rearrange("p k c -> p c k"), cond[:, :, :]).then_inc(cond_hi_made, c.did(cond_hi_made))

            def mod_skip():
                passed()

            def advance(m):
                if m % 2:
                    mod_skip()

            for i in c.passes("layers", LAYERS):
                a_at[0] = 0
                m = 0
                split_hi(x_hi[:, :, :], xs[:, :, 0:S], x_ready, x_hi_made)
                for _ in range(5):
                    passed(), advance(m)
                    m += 1
                split_hi(p_hi[:, :, :], t3[:, 0, :].rearrange("p (t s) -> p t s", t=2), p_copied, p_hi_made)
                for _ in range(8):
                    passed(), advance(m)
                    m += 1
                act.wait_ge(ff_abs, c.next(ff_abs))
                fr = slice(FF_COL, FF_COL + 6)
                act.wait_ge(c.last, c.own())
                do(ACT.Exp, t3[fr, 0, 256:512], t3[fr, 0, 0:256], scale=-1.0).then_inc(a_step, c.did(a_step))
                act.wait_ge(c.last, c.own())
                do(ACT.Ln, t3[fr, 0, 256:512], t3[fr, 0, 256:512], bias=one[fr, :]).then_inc(ff_log, c.did(ff_log))

                for what, a in SCRIPT:
                    kind = HEADS[a][0] if what in ("score", "turn", "weigh") else None
                    if what == "score" and kind != "sb":
                        act.wait_ge(logits_ready, c.next(logits_ready))
                        st, L = stat[a % 2], t1[:, a % 2, :]
                        act.wait_ge(c.last, c.own())
                        do(ACT.Exp, L[:, 0:128], L[:, 0:128], bias=st[:, 2:3], scale=SCALE, accum_out=st[:, 4:5]).then_inc(exp_made, c.did(exp_made))
                        do(ACT.Exp, L[:, 128:384], L[:, 128:384], bias=st[:, 3:4], scale=SCALE,
                           accum_out=st[:, 5:6]).then_inc(exp_made, c.did(exp_made))
                    elif what == "score":
                        act.wait_ge(abs_ready, c.next(abs_ready))
                        z = t3[:, a % 2, 0:384]
                        act.wait_ge(c.last, c.own())
                        do(ACT.Exp, z, z, scale=-1.0).then_inc(a_step, c.did(a_step))
                        act.wait_ge(c.last, c.own())
                        do(ACT.Ln, z, z, bias=one).then_inc(log_made, c.did(log_made))
                    elif what == "turn" and kind == "sb":
                        act.wait_ge(arg_ready, c.next(arg_ready))
                        act.wait_ge(c.last, c.own())
                        do(ACT.Exp, t2[:, a % 2, 0:384], t2[:, a % 2, 0:384]).then_inc(stick_ready, c.did(stick_ready))
                    elif what == "weigh" and ends_tile(*HEADS[a]):
                        br, h = ("fox", "sb", "dsa").index(kind), HEADS[a][1]
                        rows = slice(0, P if h % 2 else HALF)
                        split_hi(o_hi[rows, br % 2, h // 2, :], o32[rows, (h // 2) % 2, :], o_ready, o_hi_made)
                    elif what == "index":
                        act.wait_ge(a_full, c.next(a_full))
                        if a >= 2:
                            act.wait_ge(relu_used, c.next(relu_used))
                        do(ACT.Relu, t3[:, a % 2, 0:384], bank[6 + a_at[0] % 2][:, 0:384]).then_inc(a_free, c.did(a_free))
                        a_at[0] += 1
                    elif what == "chunk":
                        passed()
                        kind, w = MAIN[m]
                        if kind == "gate":
                            b, col = w
                            act.wait_ge(a_full, c.next(a_full))
                            if w == (2, 0):
                                act.wait_ge(gate_used, c.next(gate_used, 4))
                            act.wait_ge(c.last, c.own())
                            do(ACT.Exp, gates[:, b % 2, 2 * col:2 * col + 2, :],
                               bank[6 + a_at[0] % 2][:, :].rearrange("p (t s) -> p t s", t=2), scale=-1.0).then_inc(a_free, c.did(a_free))
                            a_at[0] += 1
                        advance(m)
                        m += 1
                act.wait_ge(relu_used, c.next(relu_used, 2))
                for _ in range(2):
                    passed(), advance(m)
                    m += 1
                act.wait_ge(gate_used, c.next(gate_used, 8))
                split_hi(m_hi[:, :, :], merged[:, :, :], m_ready, m_hi_made)
                for _ in range(4):
                    passed(), advance(m)
                    m += 1
                act.wait_ge(centred, c.next(centred))
                act.wait_ge(c.last, c.own())
                do(ACT.Square, sq1[:, :, :], xs[:, :, 0:S]).then_inc(squared, c.did(squared))
                rstd(bank[1], S, D, eps1)
                split_hi(x_hi[:, :, :], xs[:, :, 0:S], x_ready, x_hi_made)
                for k in range(4):
                    passed(), advance(m)
                    m += 1
                    act.wait_ge(a_full, c.next(a_full))
                    act.wait_ge(c.last, c.own())
                    do(ACT.Exp, ple_g[:, 2 * k:2 * k + 2, :],
                       bank[6 + a_at[0] % 2][:, :].rearrange("p (t s) -> p t s", t=2), scale=-1.0).then_inc(a_free, c.did(a_free))
                    a_at[0] += 1
                passed(), advance(m)
                m += 1
                for k in range(16):
                    passed(), advance(m)
                    m += 1
                    act.wait_ge(a_full, c.next(a_full))
                    if k >= 2:
                        act.wait_ge(f_lo_made, c.next(f_lo_made))
                    act.wait_ge(c.last, c.own())
                    do(ACT.Relu, t1[:, k % 2, :], bank[6 + a_at[0] % 2][:, :]).then_inc(a_free, c.did(a_free))
                    a_at[0] += 1
                    act.wait_ge(c.last, c.own())
                    do(ACT.Square, f_hi[:, 2 * k:2 * k + 2, :],
                       t1[:, k % 2, :].rearrange("p (t s) -> p t s", t=2)).then_inc(f_hi_made, c.did(f_hi_made))
                act.wait_ge(f_lo_made, c.next(f_lo_made, 2))
                for k in range(16):
                    passed(), advance(m)
                    m += 1
                assert m == len(MAIN)
                act.wait_ge(centred, c.next(centred))
                act.wait_ge(c.last, c.own())
                do(ACT.Square, sq1[:, :, :], xs[:, :, 0:S]).then_inc(squared, c.did(squared))
                rstd(bank[1], S, D, eps1)
                act.wait_ge(c.last, c.own())
            n[0] += (LAYERS - 1) * CHUNKS1
            used[0] += (LAYERS - 1) * CHUNKS1
            c.credit(turned)

            def state_rms(width):
                act.wait_ge(x_ready, c.next(x_ready))
                act.wait_ge(c.last, c.own())
                do(ACT.Square, sq2[:, :, 0:width], xs[:, :, 0:width]).then_inc(squared, c.did(squared))
                rstd(bank[0], width, D, eps2)

            def modulated(l, j, width):
                state_rms(width)
                for k in range(KT):
                    act.wait_ge(u_ready, c.next(u_ready))
                    for s, cols in streams(width):
                        signal = h_hi_made if cols.stop == width else a_step
                        do(ACT.Identity, h_hi[:, k, cols], t2[:, k % 2, cols],
                           bias=mod_col(l, 3 * j, k, s)).then_inc(signal, c.did(signal))

            def unit_ffn(l, which, width):
                modulated(l, 2 * which, width)
                for j in c.passes(f"ffn{l}{which}", 2):
                    a_at[0] = 0

                    def unit_hi(t):
                        act.wait_ge(unit_ready, c.next(unit_ready))
                        act.wait_ge(c.last, c.own())
                        do(ACT.Copy, un_hi[:, t, 0:width], t2[:, t % 2, 0:width]).then_inc(unit_hi_made, c.did(unit_hi_made))

                    for t in range(HT):
                        passed()
                        act.wait_ge(a_full, c.next(a_full))
                        act.wait_ge(c.last, c.own())
                        do(ACT.Silu, t1[:, t % 2, 0:width], bank[6 + a_at[0] % 2][:, 0:width]).then_inc(a_free, c.did(a_free))
                        a_at[0] += 1
                        if t in SPLIT_TILES:
                            passed()
                        if t:
                            unit_hi(t - 1)
                    unit_hi(HT - 1)
                    for t in range(KT):
                        passed()
                n[0] += FFN_CHUNKS
                used[0] += FFN_CHUNKS

            def soft_attention(units, scale, hi, ends, with_sink):
                for s in range(len(units) + 4):
                    if s >= 4 and ends(units[s - 4]) is not None:
                        t, width = ends(units[s - 4])
                        act.wait_ge(o_full, c.next(o_full))
                        do(ACT.Copy, hi[:, t, 0:width], bank[4 + t % 2][:, 0:width]).then_inc(o_hi_made, c.did(o_hi_made))
                    if 2 <= s < len(units) + 2:
                        act.wait_ge(turn_full, c.next(turn_full))
                        do(ACT.Copy, t2[:, s % 2, :], bank[2][:, :]).then_inc(turned, c.did(turned))
                    if s < len(units):
                        act.wait_ge(logits_ready, c.next(logits_ready))
                        st, L, b = stat[s % 3], prob[s % 3], bank[s % 2]
                        h, part = units[s]
                        if part < 2:
                            act.wait_ge(c.last, c.own())
                            signal = a_step if with_sink else exp_made
                            do(ACT.Exp, L, b[:, :], bias=st[:, 2:3], scale=scale, accum_out=st[:, 4:5]).then_inc(signal, c.did(signal))
                            if with_sink:
                                act.wait_ge(c.last, c.own())
                                do(ACT.Exp, st[:, 5:6], sink[:, h:h + 1], bias=st[:, 2:3]).then_inc(exp_made, c.did(exp_made))
                        else:
                            for q in range(2):
                                act.wait_ge(c.last, c.own())
                                signal = exp_made if q else a_step
                                do(ACT.Exp, L[:, S * q:S * q + S], b[:, S * q:S * q + S], bias=st[:, 2 + q:3 + q], scale=scale,
                                   accum_out=st[:, 4 + q:5 + q]).then_inc(signal, c.did(signal))

            def mla():
                modulated(0, 1, 2 * S)
                for _ in range(3):
                    passed()
                act.wait_ge(cq_ready, c.next(cq_ready))
                act.wait_ge(c.last, c.own())
                do(ACT.Square, sqm[:, :, :], cqkv[:, :, :]).then_inc(squared, c.did(squared))
                passed()
                rstd(bank[0], 2 * S, Q_RANK, eps2)
                act.wait_ge(var_full, c.next(var_full))
                act.wait_ge(c.last, c.own())
                do(ACT.Ln, t3[:, 0, :], bank[1][:, :], bias=eps2, scale=1.0 / KV_RANK).then_inc(a_step, c.did(a_step))
                act.wait_ge(c.last, c.own())
                do(ACT.Exp, t3[:, 1, :], t3[:, 0, :], scale=-0.5).then_inc(rstd_made, c.did(rstd_made))
                for k in range(6):
                    act.wait_ge(u_ready, c.next(u_ready))
                    dst = cq_hi[:, k, :] if k < 4 else ckv_hi[:, k - 4, :]
                    do(ACT.Copy, dst, cqkv[:, k, :]).then_inc(h_hi_made, c.did(h_hi_made))
                for _ in range(5):
                    passed()
                soft_attention(MLA_UNITS, MLA_SCALE, om_hi, mla_end, False)
                for _ in range(4):
                    passed()

            def swa():
                modulated(1, 1, 2 * S)
                for _ in range(7):
                    passed()
                soft_attention(SWA_UNITS, SCALE, ow_hi, swa_end, True)
                for _ in range(4):
                    passed()

            unit_ffn(0, 0, 2 * S)
            mla()
            unit_ffn(0, 1, 2 * S)
            unit_ffn(1, 0, 2 * S)
            swa()
            unit_ffn(1, 1, S)
            state_rms(S)

        @block.vector
        def _(dve):
            c = Counts(dve, per_pass, measured)
            n, used = [0], [0]

            def prep(upto):
                while n[0] <= upto:
                    s = n[0] % SLOTS
                    dve.wait_ge(hi_made, c.value(hi_made, n[0] + 1))
                    dve.tensor_tensor(w_lo[s][:, :], raw[s][:, :], w_hi[s][:, :].bitcast(F32), ALU.subtract).then_inc(lo_made, c.did(lo_made))
                    n[0] += 1

            def passed():
                prep(used[0] + 2)
                used[0] += 1

            def tt(o, a, b, op):
                return dve.tensor_tensor(o, a, b, op)

            def ts(o, a, s1, s2, op0, op1=None):
                kw = {} if op1 is None else {"op1": op1}
                return dve.tensor_scalar(o, a, s1, s2, op0, **kw)

            def stt(o, a, s1, b, op0, op1):
                return dve.scalar_tensor_tensor(out=o, in0=a, scalar=s1, in1=b, op0=op0, op1=op1)

            def copy(o, a):
                return dve.tensor_copy(o, a)

            def recip(o, a):
                return dve.reciprocal(o, a)

            def lo(dst, src, hi, hi_sem, sem):
                dve.wait_ge(hi_sem, c.next(hi_sem))
                dve.wait_ge(c.last, c.own())
                tt(dst, src, hi.bitcast(F32), ALU.subtract).then_inc(sem, c.did(sem))

            d_at, s_at = [0], [0]

            def bump(sem):
                dve.wait_ge(c.last, c.own())
                dve.sem_inc(sem, 1)
                c.made[sem] = c.made.get(sem, 0) + 1

            def settle_apart():
                dve.wait_ge(c.last, c.own())
                dve.sem_inc(apart, 1)

            def d_bank():
                d_at[0] += 1
                return bank[4 + (d_at[0] - 1) % 2]

            def s_bank():
                s_at[0] += 1
                return bank[(s_at[0] - 1) % 2]

            def pair(t):
                return t.rearrange("p (t s) -> p t s", t=2)

            for s in range(SLOTS):
                dve.memset(raw[s][:, :], 0.0).then_inc(v_step, c.did(v_step))
            dve.memset(eps1, LN_EPS).then_inc(v_step, c.did(v_step))
            dve.memset(eps2, RMS_EPS).then_inc(v_step, c.did(v_step))
            dve.memset(one, 1.0).then_inc(v_step, c.did(v_step))
            dve.wait_ge(c.last, c.own())
            c.credit(lo_made, SLOTS)
            for s in (d_free, s_free, t_free, v_free, p_room, raw_set):
                c.credit(s)
            c.seen[a_free] = 1
            dve.wait_ge(consts_in, 32)
            prep(1)
            dve.wait_ge(d_full, c.next(d_full))
            b = d_bank()
            dve.wait_ge(c.last, c.own())
            copy(cols_a[:, :], b[:, 0:120]).then_inc(v_step, c.did(v_step))
            copy(cols_mod[:, :, :], b[:, 120:264].rearrange("p (l t) -> p l t", l=2)).then_inc(v_step, c.did(v_step))
            copy(cols_d[:, :], b[:, 264:286]).then_inc(d_free, c.did(d_free))
            dve.wait_ge(c.last, c.own())
            copy(cond[:, :, :], cols_d[:, 6:22].rearrange("p (c k) -> p c k", c=2)).then_inc(cond_ready, c.did(cond_ready))
            e = t3[:, 0, 0:16].rearrange("p (c k) -> p c k", c=2)
            dve.wait_ge(cond_exp, c.next(cond_exp))
            dve.wait_ge(c.last, c.own())
            ts(e, e, 1.0, None, ALU.add).then_inc(v_step, c.did(v_step))
            dve.wait_ge(c.last, c.own())
            recip(e, e).then_inc(v_step, c.did(v_step))
            dve.wait_ge(c.last, c.own())
            tt(cond[:, :, :], cond[:, :, :], e, ALU.mult).then_inc(cond_ready, c.did(cond_ready))
            lo(cond_lo[:, :, :].rearrange("p k c -> p c k"), cond[:, :, :],
               cond_hi[:, :, :].rearrange("p k c -> p c k"), cond_hi_made, cond_lo_made)
            for half in range(2):
                for q in range(4):
                    dve.wait_ge(d_full, c.next(d_full))
                    b = d_bank()
                    copy(xs[:, 2 * q:2 * q + 2, half * S:half * S + S], pair(b[:, :])).then_inc(d_free, c.did(d_free))
            bump(x_ready)

            def layer_norm(g, bias):
                x = xs[:, :, 0:S]
                dve.wait_ge(s_full, c.next(s_full))
                b = s_bank()
                dve.wait_ge(c.last, c.own())
                for k in range(KT):
                    signal = s_free if k == KT - 1 else v_step
                    stt(xs[:, k, 0:S], b[:, 0:S], -1.0 / D, xs[:, k, 0:S], ALU.mult, ALU.add).then_inc(signal, c.did(signal))
                bump(centred)
                dve.wait_ge(rstd_made, c.next(rstd_made))
                bump(s_free)
                s_at[0] += 1
                for k in range(KT):
                    tt(xs[:, k, 0:S], xs[:, k, 0:S], t1[:, 1, 0:S], ALU.mult).then_inc(v_step, c.did(v_step))
                dve.wait_ge(c.last, c.own())
                for k in range(KT):
                    ts(xs[:, k, 0:S], xs[:, k, 0:S], ln_cols[:, g, k:k + 1], ln_cols[:, bias, k:k + 1], ALU.mult, ALU.add).then_inc(v_step, c.did(v_step))
                bump(x_ready)

            for i in c.passes("layers", LAYERS):
                d_at[0] = s_at[0] = 0
                m = 0

                def chunk_of(m):
                    passed()

                def mod(m):
                    if m % 2 == 0:
                        return
                    passed()
                    j = m // 2
                    dve.wait_ge(d_full, c.next(d_full))
                    b = d_bank()
                    dve.wait_ge(c.last, c.own())
                    tt(mods[:, i, 4 * j:4 * j + 4].rearrange("p (t c) -> p t c", c=2),
                       b[:, 0:4].rearrange("p (t c) -> p t c", c=2),
                       cols_mod[:, i, 2 * j:2 * j + 2].unsqueeze(2).to_broadcast([P, 2, 2]), ALU.add).then_inc(d_free, c.did(d_free))

                def up_done(w):
                    b, half = w
                    for q in range(2):
                        t = 4 * half + 2 * q
                        g = gates[:, b % 2, t:t + 2, :]
                        dve.wait_ge(c.last, c.own())
                        dve.wait_ge(d_full, c.next(d_full))
                        tt(g, pair(d_bank()[:, :]), g, ALU.mult).then_inc(d_free, c.did(d_free))
                        if b == 0:
                            dve.wait_ge(c.last, c.own())
                            copy(merged[:, t:t + 2, :], g).then_inc(gate_used, c.did(gate_used))
                        else:
                            dve.wait_ge(c.last, c.own())
                            tt(merged[:, t:t + 2, :], merged[:, t:t + 2, :], g, ALU.add).then_inc(gate_used, c.did(gate_used))

                dve.wait_ge(c.last, c.own())
                copy(ln_cols[:, :, :], cols_a[:, bass.ds(i * 32, 32)].rearrange("p (a k) -> p a k", k=KT)).then_inc(v_step, c.did(v_step))
                lo(x_lo[:, :, :], xs[:, :, 0:S], x_hi[:, :, :], x_hi_made, x_lo_made)
                for k in range(5):
                    chunk_of(m)
                    dve.wait_ge(c.last, c.own())
                    dve.wait_ge(d_full, c.next(d_full))
                    copy(qk[:, 2 * k:2 * k + 2, :], pair(d_bank()[:, :])).then_inc(d_free, c.did(d_free))
                    mod(m)
                    m += 1
                dve.wait_ge(t_full, c.next(t_full))
                dve.wait_ge(c.last, c.own())
                copy(t3[:, 0, :], bank[2][:, :]).then_inc(t_free, c.did(t_free))
                bump(p_room)
                bump(p_copied)
                lo(p_lo[:, :, :], pair(t3[:, 0, :]), p_hi[:, :, :], p_hi_made, p_lo_made)
                for k in range(5, 10):
                    chunk_of(m)
                    dve.wait_ge(c.last, c.own())
                    dve.wait_ge(d_full, c.next(d_full))
                    copy(qk[:, 2 * k:2 * k + 2, :], pair(d_bank()[:, :])).then_inc(d_free, c.did(d_free))
                    if k == 5:
                        dve.wait_ge(c.last, c.own())
                        dve.wait_ge(d_full, c.next(d_full))
                        copy(iwt[:, :, :], d_bank()[:, 0:16].rearrange("p (t c) -> p t c", t=2)).then_inc(d_free, c.did(d_free))
                    mod(m)
                    m += 1
                for k in range(3):
                    chunk_of(m)
                    dve.wait_ge(c.last, c.own())
                    dve.wait_ge(d_full, c.next(d_full))
                    copy(v_tok[:, :, 256 * k:256 * k + 256], pair(d_bank()[:, :])).then_inc(d_free, c.did(d_free))
                    mod(m)
                    m += 1
                fr = slice(FF_COL, FF_COL + 6)
                z, w, cum = qk[fr, T_SK4, :], t3[fr, 0, 256:512], t3[fr, 1, 0:256]
                dve.wait_ge(bf_in, c.next(bf_in, 16))
                dve.wait_ge(c.last, c.own())
                ts(z, z, bf[fr, :], None, ALU.add).then_inc(v_step, c.did(v_step))
                dve.wait_ge(c.last, c.own())
                stt(t3[fr, 0, 0:256], z, -1.0, z, ALU.mult, ALU.max).then_inc(ff_abs, c.did(ff_abs))
                dve.wait_ge(ff_log, c.next(ff_log))
                dve.wait_ge(c.last, c.own())
                stt(w, z, 0.0, w, ALU.min, ALU.subtract).then_inc(v_step, c.did(v_step))
                dve.wait_ge(c.last, c.own())
                dve.tensor_tensor_scan(cum, ones[fr, 0:1].to_broadcast([6, S]), w, 0.0, ALU.mult, ALU.add).then_inc(ff_sum, c.did(ff_sum))
                dve.wait_ge(d_full, c.next(d_full))
                b = d_bank()
                dve.wait_ge(c.last, c.own())
                ts(cq8[:, :, :], b[:, 0:12].rearrange("p (t h) -> p t h", t=2), 1.0 / SCALE, None, ALU.mult).then_inc(d_free, c.did(d_free))
                for k, (t, cnt) in enumerate([(11, 1), (12, 2), (14, 2), (16, 2), (18, 2)]):
                    dve.wait_ge(d_full, c.next(d_full))
                    b = d_bank()
                    cs, sn = (cos_a, sin_a) if k == 0 else (cos_b, sin_b)
                    for j in range(cnt):
                        dve.wait_ge(c.last, c.own())
                        signal = d_free if j == cnt - 1 else v_step
                        tt(t2[:, k % 2, S * j:S * j + S], b[:, S * j:S * j + S], sn, ALU.mult).then_inc(signal, c.did(signal))
                    for j in range(cnt):
                        tt(qk[:, t + j, :], qk[:, t + j, :], cs, ALU.mult).then_inc(v_step, c.did(v_step))
                    dve.wait_ge(c.last, c.own())
                    tt(qk[:, t:t + cnt, :], qk[:, t:t + cnt, :],
                       t2[:, k % 2, 0:cnt * S].rearrange("p (t s) -> p t s", t=cnt), ALU.add).then_inc(roped, c.did(roped))

                for what, a in SCRIPT:
                    kind, h = HEADS[a] if what in ("score", "turn", "weigh", "decay") else (None, None)
                    if what == "decay":
                        dve.wait_ge(d_full, c.next(d_full))
                        b = d_bank()
                        dve.wait_ge(c.last, c.own())
                        stt(decay[:, a % 2, 0:128], b[:, 0:128], -1.0 / SCALE, row_mask[:, 128:256], ALU.mult, ALU.add).then_inc(v_step, c.did(v_step))
                        dve.wait_ge(c.last, c.own())
                        stt(decay[:, a % 2, 128:384], b[:, 0:256], -1.0 / SCALE, row_mask, ALU.mult, ALU.add).then_inc(d_free, c.did(d_free))
                    elif what == "score" and kind != "sb":
                        dve.wait_ge(s_full, c.next(s_full))
                        b, L, st = s_bank(), t1[:, a % 2, :], stat[a % 2]
                        if kind == "fox":
                            dve.wait_ge(c.last, c.own())
                            stt(L[:, 0:128], b[:, 0:128], cq8[:, 0, h:h + 1], decay[:, a % 2, 0:128], ALU.add, ALU.add).then_inc(v_step, c.did(v_step))
                            dve.wait_ge(c.last, c.own())
                            stt(L[:, 128:384], b[:, 128:384], cq8[:, 1, h:h + 1], decay[:, a % 2, 128:384], ALU.add, ALU.add).then_inc(s_free, c.did(s_free))
                        else:
                            dve.wait_ge(c.last, c.own())
                            tt(L[:, 0:384], b[:, 0:384], chosen[:, :], ALU.add).then_inc(s_free, c.did(s_free))
                        dve.wait_ge(c.last, c.own())
                        dve.tensor_reduce(st[:, 0:1], L[:, 0:128], AX.X, ALU.max).then_inc(v_step, c.did(v_step))
                        dve.tensor_reduce(st[:, 1:2], L[:, 128:384], AX.X, ALU.max).then_inc(v_step, c.did(v_step))
                        dve.wait_ge(c.last, c.own())
                        ts(st[:, 2:4], st[:, 0:2], -SCALE, None, ALU.mult).then_inc(logits_ready, c.did(logits_ready))
                    elif what == "score":
                        dve.wait_ge(s_full, c.next(s_full))
                        b, z = s_bank(), t1[:, a % 2, :]
                        dve.wait_ge(c.last, c.own())
                        stt(z[:, 0:256], b[:, 0:256], SCALE, sb_mask, ALU.mult, ALU.add).then_inc(v_step, c.did(v_step))
                        dve.wait_ge(c.last, c.own())
                        stt(z[:, 256:384], b[:, 256:384], SCALE, sb_mask[:, 0:128], ALU.mult, ALU.add).then_inc(s_free, c.did(s_free))
                        dve.wait_ge(c.last, c.own())
                        stt(t3[:, a % 2, 0:384], z[:, 0:384], -1.0, z[:, 0:384], ALU.mult, ALU.max).then_inc(abs_ready, c.did(abs_ready))
                    elif what == "turn" and kind != "sb":
                        L, st = t1[:, a % 2, :], stat[a % 2]
                        dve.wait_ge(exp_made, c.next(exp_made, 2))
                        dve.wait_ge(c.last, c.own())
                        recip(st[:, 6:8], st[:, 4:6]).then_inc(v_step, c.did(v_step))
                        dve.wait_ge(c.last, c.own())
                        ts(L[:, 0:128], L[:, 0:128], st[:, 6:7], None, ALU.mult).then_inc(v_step, c.did(v_step))
                        ts(L[:, 128:384], L[:, 128:384], st[:, 7:8], None, ALU.mult).then_inc(weights_ready, c.did(weights_ready))
                        dve.wait_ge(t_full, c.next(t_full))
                        dve.wait_ge(c.last, c.own())
                        copy(t2[:, a % 2, 0:384], bank[2][:, 0:384]).then_inc(t_free, c.did(t_free))
                    elif what == "turn":
                        z, sp_ = t1[:, a % 2, 0:384], t3[:, a % 2, 0:384]
                        dve.wait_ge(log_made, c.next(log_made))
                        dve.wait_ge(c.last, c.own())
                        stt(sp_, z, 0.0, sp_, ALU.max, ALU.add).then_inc(soft_ready, c.did(soft_ready))
                        dve.wait_ge(t_full, c.next(t_full))
                        dve.wait_ge(c.last, c.own())
                        tt(t2[:, a % 2, 0:384], bank[2][:, 0:384], z, ALU.add).then_inc(t_free, c.did(t_free))
                        bump(arg_ready)
                    elif what == "weigh":
                        dve.wait_ge(v_full, c.next(v_full))
                        if ends_tile(kind, h):
                            rows, br = slice(0, P if h % 2 else HALF), ("fox", "sb", "dsa").index(kind)
                            dve.wait_ge(c.last, c.own())
                            copy(o32[rows, (h // 2) % 2, :], bank[3][rows, 0:S]).then_inc(v_free, c.did(v_free))
                            bump(o_ready)
                            lo(o_lo[rows, br % 2, h // 2, :], o32[rows, (h // 2) % 2, :], o_hi[rows, br % 2, h // 2, :],
                               o_hi_made, o_lo_made)
                    elif what == "index":
                        dve.wait_ge(a_free, c.next(a_free))
                        for q, cols, first in ((0, slice(0, 128), idx_mask[:, 128:256]), (1, slice(128, 384), idx_mask)):
                            r = t3[:, a % 2, cols]
                            if q == 0:
                                dve.wait_ge(c.last, c.own())
                            signal = relu_used if q else v_step
                            stt(score[:, cols], r, iwt[:, q, a:a + 1], first if a == 0 else score[:, cols], ALU.mult, ALU.add).then_inc(signal, c.did(signal))
                    elif what == "topk":
                        settle_apart()
                        for r in range(TOPK // 8):
                            for q, cols in ((0, slice(0, 128)), (1, slice(128, 384))):
                                dve.max(top8[:, q, :], score[:, cols]).then_inc(v_step, c.did(v_step))
                            settle_apart()
                            for q, cols in ((0, slice(0, 128)), (1, slice(128, 384))):
                                dve.match_replace(out=score[:, cols], in_to_replace=top8[:, q, :],
                                                         in_values=score[:, cols], imm_value=MARK).then_inc(v_step, c.did(v_step))
                            settle_apart()
                        dve.wait_ge(c.last, c.own())
                        ts(chosen[:, :], score[:, :], MARK, NEG / SCALE, ALU.not_equal, ALU.mult).then_inc(v_step, c.did(v_step))
                    elif what == "chunk":
                        chunk_of(m)
                        kind, w = MAIN[m]
                        if kind == "gate":
                            b, col = w
                            g = gates[:, b % 2, 2 * col:2 * col + 2, :]
                            dve.wait_ge(a_free, c.next(a_free))
                            dve.wait_ge(c.last, c.own())
                            ts(g, g, 1.0, None, ALU.add).then_inc(v_step, c.did(v_step))
                            dve.wait_ge(c.last, c.own())
                            recip(g, g).then_inc(v_step, c.did(v_step))
                        else:
                            up_done(w)
                        mod(m)
                        m += 1

                for w in ((2, 0), (2, 1)):
                    chunk_of(m)
                    up_done(w)
                    mod(m)
                    m += 1
                bump(m_ready)
                lo(m_lo[:, :, :], merged[:, :, :], m_hi[:, :, :], m_hi_made, m_lo_made)
                for k in range(4):
                    chunk_of(m)
                    dve.wait_ge(c.last, c.own())
                    dve.wait_ge(d_full, c.next(d_full))
                    stt(xs[:, 2 * k:2 * k + 2, 0:S], xs[:, 2 * k:2 * k + 2, 0:S], ALPHA, pair(d_bank()[:, :]), ALU.mult, ALU.add).then_inc(d_free, c.did(d_free))
                    mod(m)
                    m += 1
                layer_norm(0, 1)
                lo(x_lo[:, :, :], xs[:, :, 0:S], x_hi[:, :, :], x_hi_made, x_lo_made)
                for k in range(4):
                    chunk_of(m)
                    mod(m)
                    m += 1
                dve.wait_ge(a_free, c.next(a_free, 4))
                dve.wait_ge(c.last, c.own())
                ts(ple_g[:, :, :], ple_g[:, :, :], 1.0, None, ALU.add).then_inc(v_step, c.did(v_step))
                dve.wait_ge(c.last, c.own())
                recip(ple_g[:, :, :], ple_g[:, :, :]).then_inc(v_step, c.did(v_step))
                chunk_of(m)
                for k in range(4):
                    if k == 0:
                        dve.wait_ge(c.last, c.own())
                    dve.wait_ge(d_full, c.next(d_full))
                    tt(ple_g[:, 2 * k:2 * k + 2, :], pair(d_bank()[:, :]), ple_g[:, 2 * k:2 * k + 2, :], ALU.mult).then_inc(d_free, c.did(d_free))
                dve.wait_ge(c.last, c.own())
                stt(xs[:, :, 0:S], xs[:, :, 0:S], ALPHA, ple_g[:, :, :], ALU.mult, ALU.add).then_inc(v_step, c.did(v_step))
                mod(m)
                m += 1
                for k in range(16):
                    chunk_of(m)
                    dve.wait_ge(f_hi_made, c.next(f_hi_made))
                    dve.wait_ge(a_free, c.next(a_free))
                    sq = pair(t2[:, k % 2, :])
                    r = pair(t1[:, k % 2, :])
                    dve.wait_ge(c.last, c.own())
                    tt(sq, r, r, ALU.mult).then_inc(v_step, c.did(v_step))
                    dve.wait_ge(c.last, c.own())
                    tt(f_lo[:, 2 * k:2 * k + 2, :], sq, f_hi[:, 2 * k:2 * k + 2, :].bitcast(F32), ALU.subtract).then_inc(f_lo_made, c.did(f_lo_made))
                    mod(m)
                    m += 1
                for k in range(16):
                    chunk_of(m)
                    if k % 2:
                        t = k // 2
                        dve.wait_ge(c.last, c.own())
                        dve.wait_ge(d_full, c.next(d_full))
                        tt(xs[:, t, 0:S], d_bank()[:, 0:S], xs[:, t, 0:S], ALU.add).then_inc(d_free, c.did(d_free))
                    mod(m)
                    m += 1
                layer_norm(2, 3)
                dve.wait_ge(c.last, c.own())
            n[0] += (LAYERS - 1) * CHUNKS1
            used[0] += (LAYERS - 1) * CHUNKS1
            c.credit(o_free)
            dve.wait_ge(phase_in, 32)
            dve.wait_ge(c.last, c.own())
            ts(nsink[:, :], sink[:, :], -1.0, None, ALU.mult).then_inc(v_step, c.did(v_step))

            def modulated(l, j, width):
                def triple(k):
                    return mods[:, l, 16 * k:16 * k + 16].rearrange("p (t c) -> p t c", c=2)
                g = cols_a[:, 64 + 24 * l + 8 * j:72 + 24 * l + 8 * j]
                dve.wait_ge(c.last, c.own())
                stt(amod[:, :, :], triple(3 * j + 1), 1.0, g.unsqueeze(2).to_broadcast([P, KT, 2]), ALU.add, ALU.mult).then_inc(v_step, c.did(v_step))
                ts(hgate[:, :, :], triple(3 * j + 2), 0.5 if j != 1 else 1.0, None, ALU.mult).then_inc(v_step, c.did(v_step))
                dve.wait_ge(rstd_made, c.next(rstd_made))
                bump(s_free)
                for k in range(KT + 1):
                    if k < KT:
                        dve.wait_ge(c.last, c.own())
                        for s, cols in streams(width):
                            signal = u_ready if cols.stop == width else v_step
                            stt(t2[:, k % 2, cols], xs[:, k, cols], amod[:, k, s:s + 1], t1[:, 1, cols], ALU.mult, ALU.mult).then_inc(signal, c.did(signal))
                    if k:
                        dve.wait_ge(h_hi_made, c.next(h_hi_made))
                        for s, cols in streams(width):
                            if k == KT and s == 0:
                                dve.wait_ge(c.last, c.own())
                            signal = h_lo_made if cols.stop == width else v_step
                            stt(h_lo[:, k - 1, cols], t2[:, (k - 1) % 2, cols], mod_col(l, 3 * j, k - 1, s),
                                h_hi[:, k - 1, cols].bitcast(F32), ALU.add, ALU.subtract).then_inc(signal, c.did(signal))

            def unit_ffn(l, which, width):
                modulated(l, 2 * which, width)
                for j in c.passes(f"ffn{l}{which}", 2):
                    d_at[0] = 0

                    def unit_lo(t):
                        dve.wait_ge(unit_hi_made, c.next(unit_hi_made))
                        tt(un_lo[:, t, 0:width], t2[:, t % 2, 0:width], un_hi[:, t, 0:width].bitcast(F32), ALU.subtract).then_inc(unit_lo_made, c.did(unit_lo_made))

                    for t in range(HT):
                        passed()
                        if t in SPLIT_TILES:
                            passed()
                        dve.wait_ge(a_free, c.next(a_free))
                        dve.wait_ge(c.last, c.own())
                        dve.wait_ge(d_full, c.next(d_full))
                        tt(t2[:, t % 2, 0:width], d_bank()[:, 0:width], t1[:, t % 2, 0:width], ALU.mult).then_inc(d_free, c.did(d_free))
                        bump(unit_ready)
                        if t:
                            unit_lo(t - 1)
                    unit_lo(HT - 1)
                    for t in range(KT):
                        passed()
                        dve.wait_ge(d_full, c.next(d_full))
                        b = d_bank()
                        dve.wait_ge(c.last, c.own())
                        for s, cols in streams(width):
                            signal = d_free if cols.stop == width else v_step
                            stt(xs[:, t, cols], b[:, cols], hgate[:, t, s:s + 1], xs[:, t, cols], ALU.mult, ALU.add).then_inc(signal, c.did(signal))
                    dve.wait_ge(c.last, c.own())
                n[0] += FFN_CHUNKS
                used[0] += FFN_CHUNKS
                d_at[0] = 0
                bump(x_ready)

            def rotate(dst, src):
                k, cnt = d_at[0] % 2, src.shape[1]
                turn = t2[:, k, 0:S * cnt].rearrange("p (t s) -> p t s", t=cnt)
                cs, sn = (z.unsqueeze(1).to_broadcast([P, cnt, S]) for z in (cos_2, sin_2))
                dve.wait_ge(d_full, c.next(d_full))
                b = d_bank()
                dve.wait_ge(c.last, c.own())
                tt(turn, b[:, 0:S * cnt].rearrange("p (t s) -> p t s", t=cnt), sn, ALU.mult).then_inc(d_free, c.did(d_free))
                tt(dst, src, cs, ALU.mult).then_inc(v_step, c.did(v_step))
                dve.wait_ge(c.last, c.own())
                tt(dst, dst, turn, ALU.add).then_inc(roped, c.did(roped))

            def soft_attention(units, scale, hi, lo_part, ends, with_sink):
                for s in range(len(units) + 4):
                    if 1 <= s <= len(units):
                        st, L = stat[(s - 1) % 3], prob[(s - 1) % 3]
                        dve.wait_ge(exp_made, c.next(exp_made))
                        if units[s - 1][1] < 2:
                            if with_sink:
                                dve.wait_ge(c.last, c.own())
                                tt(st[:, 4:5], st[:, 4:5], st[:, 5:6], ALU.add).then_inc(v_step, c.did(v_step))
                            dve.wait_ge(c.last, c.own())
                            recip(st[:, 6:7], st[:, 4:5]).then_inc(s_free, c.did(s_free))
                            dve.wait_ge(c.last, c.own())
                            ts(L, L, st[:, 6:7], None, ALU.mult).then_inc(weights_ready, c.did(weights_ready))
                        else:
                            dve.wait_ge(c.last, c.own())
                            recip(st[:, 6:8], st[:, 4:6]).then_inc(s_free, c.did(s_free))
                            for q in range(2):
                                dve.wait_ge(c.last, c.own())
                                signal = weights_ready if q else v_step
                                ts(L[:, S * q:S * q + S], L[:, S * q:S * q + S], st[:, 6 + q:7 + q], None, ALU.mult).then_inc(signal, c.did(signal))
                    if s < len(units):
                        h, part = units[s]
                        st, b = stat[s % 3], bank[s % 2]
                        dve.wait_ge(s_full, c.next(s_full))
                        if with_sink:
                            dve.wait_ge(c.last, c.own())
                            tt(b[:, 0:S], b[:, 0:S], win_mask[:, S * part:S * part + S], ALU.add).then_inc(v_step, c.did(v_step))
                        dve.wait_ge(c.last, c.own())
                        if part < 2:
                            dve.tensor_reduce(st[:, 0:1], b[:, :], AX.X, ALU.max).then_inc(v_step, c.did(v_step))
                            if with_sink:
                                dve.wait_ge(c.last, c.own())
                                stt(st[:, 2:3], st[:, 0:1], -scale, nsink[:, h:h + 1], ALU.mult, ALU.min).then_inc(logits_ready, c.did(logits_ready))
                            else:
                                dve.wait_ge(c.last, c.own())
                                ts(st[:, 2:3], st[:, 0:1], -scale, None, ALU.mult).then_inc(logits_ready, c.did(logits_ready))
                        else:
                            dve.tensor_reduce(st[:, 0:2], pair(b[:, :]), AX.X, ALU.max).then_inc(v_step, c.did(v_step))
                            dve.wait_ge(c.last, c.own())
                            ts(st[:, 2:4], st[:, 0:2], -scale, None, ALU.mult).then_inc(logits_ready, c.did(logits_ready))
                    if s >= 4 and ends(units[s - 4]) is not None:
                        t, width = ends(units[s - 4])
                        lo(lo_part[:, t, 0:width], bank[4 + t % 2][:, 0:width], hi[:, t, 0:width], o_hi_made, o_free)

            def mla():
                modulated(0, 1, 2 * S)
                for q in range(3):
                    passed()
                    for j in range(2):
                        dve.wait_ge(c.last, c.own())
                        dve.wait_ge(d_full, c.next(d_full))
                        copy(cqkv[:, 2 * q + j, :], d_bank()[:, :]).then_inc(d_free, c.did(d_free))
                bump(cq_ready)
                passed()
                dve.wait_ge(c.last, c.own())
                dve.wait_ge(d_full, c.next(d_full))
                copy(kr[:, :], d_bank()[:, :]).then_inc(d_free, c.did(d_free))
                dve.wait_ge(rstd_made, c.next(rstd_made, 2))
                bump(s_free)
                bump(s_free)
                for k in range(6):
                    r = t1[:, 1, :] if k < 4 else t3[:, 1, :]
                    stt(cqkv[:, k, :], cqkv[:, k, :], cols_d[:, k:k + 1], r, ALU.mult, ALU.mult).then_inc(u_ready, c.did(u_ready))
                for k in range(6):
                    hi, lo_part = (cq_hi[:, k, :], cq_lo[:, k, :]) if k < 4 else (ckv_hi[:, k - 4, :], ckv_lo[:, k - 4, :])
                    lo(lo_part, cqkv[:, k, :], hi, h_hi_made, h_lo_made)
                for q in range(2):
                    passed()
                    for j in range(4):
                        dve.wait_ge(c.last, c.own())
                        dve.wait_ge(d_full, c.next(d_full))
                        copy(qn[:, 4 * q + j, :], d_bank()[:, :]).then_inc(d_free, c.did(d_free))
                passed()
                for j in range(4):
                    dve.wait_ge(c.last, c.own())
                    dve.wait_ge(d_full, c.next(d_full))
                    copy(qr[:, j, :], d_bank()[:, :]).then_inc(d_free, c.did(d_free))
                bump(q_ready)
                passed()
                for j in range(MLA_H):
                    dve.wait_ge(c.last, c.own())
                    dve.wait_ge(d_full, c.next(d_full))
                    copy(kn[:, j, :], d_bank()[:, :]).then_inc(d_free, c.did(d_free))
                passed()
                for j in range(8):
                    dve.wait_ge(c.last, c.own())
                    dve.wait_ge(d_full, c.next(d_full))
                    copy(vm[:, j // 2, 512 * (j % 2):512 * (j % 2) + 512], d_bank()[:, :]).then_inc(d_free, c.did(d_free))
                for q in range(2):
                    rotate(qrot[:, 2 * q:2 * q + 2, :], qr[:, 2 * q:2 * q + 2, 0:S])
                rotate(kr[:, 0:S].unsqueeze(1), kr[:, 0:S].unsqueeze(1))
                soft_attention(MLA_UNITS, MLA_SCALE, om_hi, om_lo, mla_end, False)
                for q in range(4):
                    passed()
                    for j in range(2):
                        dve.wait_ge(d_full, c.next(d_full))
                        b = d_bank()
                        dve.wait_ge(c.last, c.own())
                        for s, cols in streams(2 * S):
                            signal = d_free if s else v_step
                            stt(xs[:, 2 * q + j, cols], b[:, cols], hgate[:, 2 * q + j, s:s + 1], xs[:, 2 * q + j, cols],
                                ALU.mult, ALU.add).then_inc(signal, c.did(signal))
                bump(x_ready)

            def swa():
                modulated(1, 1, 2 * S)
                for q in range(2):
                    passed()
                    for j in range(2):
                        dve.wait_ge(c.last, c.own())
                        dve.wait_ge(d_full, c.next(d_full))
                        copy(kd[:, 2 * q + j, :], d_bank()[:, :]).then_inc(d_free, c.did(d_free))
                passed()
                for j in range(2):
                    dve.wait_ge(c.last, c.own())
                    dve.wait_ge(d_full, c.next(d_full))
                    copy(vw[:, 2 * j:2 * j + 2, :], pair(d_bank()[:, :])).then_inc(d_free, c.did(d_free))
                for q in range(4):
                    passed()
                    dve.wait_ge(c.last, c.own())
                    dve.wait_ge(d_full, c.next(d_full))
                    copy(q2[:, 2 * q:2 * q + 2, :], pair(d_bank()[:, :])).then_inc(d_free, c.did(d_free))
                bump(q_ready)
                for q in range(2):
                    rotate(kd[:, 2 * q:2 * q + 2, 0:S], kd[:, 2 * q:2 * q + 2, 0:S])
                for q in range(4):
                    rotate(q2rot[:, 2 * q:2 * q + 2, :], q2[:, 2 * q:2 * q + 2, :])
                soft_attention(SWA_UNITS, SCALE, ow_hi, ow_lo, swa_end, True)
                for q in range(4):
                    passed()
                    dve.wait_ge(d_full, c.next(d_full))
                    b = d_bank()
                    dve.wait_ge(c.last, c.own())
                    for j in range(2):
                        signal = d_free if j else v_step
                        stt(xs[:, 2 * q + j, 0:S], b[:, S * j:S * j + S], hgate[:, 2 * q + j, 0:1], xs[:, 2 * q + j, 0:S],
                            ALU.mult, ALU.add).then_inc(signal, c.did(signal))
                bump(x_ready)

            unit_ffn(0, 0, 2 * S)
            mla()
            unit_ffn(0, 1, 2 * S)
            unit_ffn(1, 0, 2 * S)
            swa()
            unit_ffn(1, 1, S)
            dve.wait_ge(rstd_made, c.next(rstd_made))
            for k in range(KT):
                stt(xs[:, k, 0:S], xs[:, k, 0:S], cols_a[:, 112 + k:113 + k], t1[:, 1, 0:S], ALU.mult, ALU.mult).then_inc(v_step, c.did(v_step))
            bump(result_ready)
            d_at[0] = 0
            for t in range(2):
                for q in range(2):
                    dve.wait_ge(d_full, c.next(d_full))
                    copy(y_tok[:, t, 512 * q:512 * q + 512], d_bank()[:, :]).then_inc(d_free, c.did(d_free))
            bump(y_copied)

        @block.tensor
        def _(pe):
            c = Counts(pe, per_pass, measured)
            n = [0]
            owed = [False]
            rd = Ring(c, bank[4:6], d_full, d_free)
            ra = Ring(c, bank[6:8], a_full, a_free)
            rs = Ring(c, bank[0:2], s_full, s_free)
            rt = Ring(c, bank[2:3], t_full, t_free)
            rv = Ring(c, bank[3:4], v_full, v_free)
            rings = (rd, ra, rs, rt, rv)

            def mm(o, l, r, start, stop, give=None, transpose=False):
                ins = pe.transpose(o, l, r) if transpose else pe.matmul(o, l, r, start=start, stop=stop)
                if give is not None:
                    ins.then_inc(give, c.did(give))
                elif owed[0]:
                    ins.then_inc(chunk_used, c.did(chunk_used))
                    owed[0] = False

            def flush():
                if owed[0]:
                    pe.wait_ge(rd.free, rd.awaited())
                    b = rd.claim()
                    rd.used -= 1
                    rd.at -= 1
                    rd.last_use[rd.at % 2] = rd.used
                    mm(b[:, 0:2], ident, ident[:, 0:2], True, True)

            def chunk():
                s = n[0] % SLOTS
                pe.wait_ge(lo_made, c.value(lo_made, n[0] + 1 + SLOTS))
                n[0] += 1
                return w_hi[s], w_lo[s]

            def parts(w, kt, width):
                return [t[:, 0:kt * width].rearrange("p (k n) -> p k n", k=kt) for t in w]

            def product(o, l, r, first, last, give=None):
                mm(o, l[0], r[0], first, False)
                mm(o, l[0], r[1], False, False)
                mm(o, l[1], r[0], False, last, give)

            def tile(o, w, col, x, kts, first=True, last=True, give=None, width=P):
                for q, (k, r) in enumerate(kts):
                    end = q == len(kts) - 1
                    product(o, [t[:, k, col:col + width] for t in w], r, first and q == 0, last and end,
                            give if end else None)

            def x_tiles(hi, lo, kt, cols=slice(0, S)):
                return [(k, (hi[:, k, cols], lo[:, k, cols])) for k in range(kt)]

            c.credit(chunk_used, SLOTS)
            pe.wait_ge(consts_in, 32)
            pe.wait_ge(rows_in, 16 * N_ROWS_DMA)
            pe.wait_ge(rd.free, rd.awaited())
            b = rd.claim()
            mm(b[:, 0:120], rows_a[0:120, :], ident[0:120, 0:120], True, True, transpose=True)
            for l in range(LAYERS):
                mm(b[:, 120 + 72 * l:192 + 72 * l], rows_m[0:72, l, :], ident[0:72, 0:72], True, True, transpose=True)
            mm(b[:, 264:286], rows_d[0:22, :], ident[0:22, 0:22], True, True, d_full, transpose=True)
            pe.wait_ge(x_in, 32)
            for src in (x_tok, c_tok):
                for q in range(4):
                    pe.wait_ge(rd.free, rd.awaited())
                    b = rd.claim()
                    for j in range(4):
                        k, t = 2 * q + j // 2, j % 2
                        mm(b[:, P * j:P * j + P], src[:, t, P * k:P * k + P], ident, True, True,
                           d_full if j == 3 else None, transpose=True)
            pe.wait_ge(cond_hi_made, c.next(cond_hi_made))
            pe.wait_ge(cond_lo_made, c.next(cond_lo_made))

            def layer_norm_sums():
                pe.wait_ge(rd.free, rd.all_used())
                pe.wait_ge(rs.free, rs.awaited())
                b = rs.claim()
                for k in range(KT):
                    mm(b[:, 0:S], ones, xs[:, k, 0:S], k == 0, k == KT - 1, s_full if k == KT - 1 else None)
                pe.wait_ge(squared, c.next(squared))
                pe.wait_ge(rs.free, rs.awaited())
                b = rs.claim()
                for k in range(KT):
                    mm(b[:, 0:S], ones, sq1[:, k, :], k == 0, k == KT - 1, var_full if k == KT - 1 else None)

            for i in c.passes("layers", LAYERS, *rings):
                m = 0

                def done(m):
                    owed[0] = True
                    if m % 2 == 0:
                        return
                    w = parts(chunk(), KT, 256)
                    pe.wait_ge(rd.free, rd.awaited())
                    b = rd.claim()
                    for t in range(2):
                        tile(b[:, 2 * t:2 * t + 2], w, P * t, None,
                             [(k, (cond_hi[:, k, :], cond_lo[:, k, :])) for k in range(KT)],
                             give=d_full if t else None)
                    owed[0] = True

                def two_tiles(w, ring, xk, give):
                    pe.wait_ge(ring.free, ring.awaited())
                    b = ring.claim()
                    for t in range(2):
                        tile(b[:, S * t:S * t + S], w, P * t, None, xk, give=give if t else None)

                def up_chunk(w):
                    b, half = w
                    if half == 0:
                        pe.wait_ge(o_lo_made, c.next(o_lo_made, 3))
                    w = parts(chunk(), 3, 512)
                    for q in range(2):
                        pe.wait_ge(rd.free, rd.awaited())
                        d = rd.claim()
                        for t in range(2):
                            for k in range(3):
                                rows = slice(0, HALF if b and k == 2 else P)
                                cols = slice(P * (2 * q + t), P * (2 * q + t) + P)
                                product(d[:, S * t:S * t + S], [z[rows, k, cols] for z in w],
                                        (o_hi[rows, b % 2, k, :], o_lo[rows, b % 2, k, :]), k == 0, k == 2,
                                        d_full if t and k == 2 else None)

                xk = x_tiles(x_hi, x_lo, KT)
                pe.wait_ge(x_hi_made, c.next(x_hi_made))
                pe.wait_ge(x_lo_made, c.next(x_lo_made))
                for k in range(10):
                    if k == 5:
                        pe.wait_ge(p_in, c.next(p_in, 16))
                        pe.wait_ge(rt.free, rt.awaited())
                        b = rt.claim()
                        for j in range(4):
                            mm(b[:, P * j:P * j + P], p_tok[:, j % 2, P * (j // 2):P * (j // 2) + P], ident, True, True,
                               t_full if j == 3 else None, transpose=True)
                    w = parts(chunk(), KT, 256)
                    two_tiles(w, rd, xk, d_full)
                    if k == 5:
                        pe.wait_ge(rd.free, rd.awaited())
                        b = rd.claim()
                        for t in range(2):
                            for kk in range(KT):
                                toks = slice(P * t, P * t + P)
                                product(b[:, 8 * t:8 * t + 8], (x_hi[:, kk, toks], x_lo[:, kk, toks]),
                                        [q[:, kk, IW_COL:IW_COL + 8] for q in w], kk == 0, kk == KT - 1,
                                        d_full if t and kk == KT - 1 else None)
                    done(m)
                    m += 1
                for k in range(3):
                    w = parts(chunk(), KT, 256)
                    pe.wait_ge(rd.free, rd.awaited())
                    b = rd.claim()
                    for t in range(2):
                        for kk in range(KT):
                            toks = slice(P * t, P * t + P)
                            product(b[:, S * t:S * t + S], (x_hi[:, kk, toks], x_lo[:, kk, toks]),
                                    [q[:, kk, :] for q in w], kk == 0, kk == KT - 1,
                                    d_full if t and kk == KT - 1 else None)
                    done(m)
                    m += 1
                flush()
                fr = slice(FF_COL, FF_COL + 6)
                cum = t3[fr, 1, 0:256]
                pe.wait_ge(ff_sum, c.next(ff_sum))
                pe.wait_ge(rd.free, rd.awaited())
                b = rd.claim()
                pe.sem_inc(apart, 1)
                for t in range(2):
                    mm(b[:, 6 * t:6 * t + 6], cum[:, P * t:P * t + P], ident[fr, fr], True, True, d_full if t else None, transpose=True)
                for k, (t, cnt) in enumerate([(11, 1), (12, 2), (14, 2), (16, 2), (18, 2)]):
                    pe.wait_ge(rd.free, rd.awaited())
                    b = rd.claim()
                    for j in range(cnt):
                        mm(b[:, S * j:S * j + S], rot, qk[:, t + j, :], True, True, d_full if j == cnt - 1 else None)
                pe.wait_ge(roped, c.next(roped, 5))

                v_tiles = 0
                for what, a in SCRIPT:
                    if what in ("score", "turn", "weigh", "decay"):
                        kind, h = HEADS[a]
                        tq, tk, half, vcol = head_place(kind, h)
                        hp = slice(HALF * half, HALF * half + HALF)
                    if what == "decay":
                        pe.wait_ge(rd.free, rd.awaited())
                        b = rd.claim()
                        mm(b[:, 0:S], ident[fr, FF_COL + h:FF_COL + h + 1].to_broadcast([6, P]), cum, True, True, d_full)
                    elif what == "score" and kind != "sb":
                        pe.wait_ge(rs.free, rs.awaited())
                        b = rs.claim()
                        mm(b[:, 0:128], qk[hp, tq, 0:128], qk[hp, tk, 0:128], True, True)
                        mm(b[:, 128:384], qk[hp, tq, 128:256], qk[hp, tk, :], True, True, s_full)
                    elif what == "score":
                        pe.wait_ge(rs.free, rs.awaited())
                        b = rs.claim()
                        mm(b[:, 0:256], qk[hp, tk, 0:128], qk[hp, tq, :], True, True)
                        mm(b[:, 256:384], qk[hp, tk, 128:256], qk[hp, tq, 128:256], True, True, s_full)
                    elif what == "turn" and kind != "sb":
                        pe.wait_ge(weights_ready, c.next(weights_ready))
                        pe.wait_ge(rt.free, rt.awaited())
                        b = rt.claim()
                        for j in range(3):
                            mm(b[:, P * j:P * j + P], t1[:, a % 2, P * j:P * j + P], ident, True, True, t_full if j == 2 else None, transpose=True)
                    elif what == "turn":
                        pe.wait_ge(soft_ready, c.next(soft_ready))
                        pe.wait_ge(rt.free, rt.awaited())
                        b = rt.claim()
                        z = t3[:, a % 2, :]
                        mm(b[:, 0:256], neg_tri, z[:, 0:256], True, False)
                        mm(b[:, 128:256], neg_ones, z[:, 256:384], False, True)
                        mm(b[:, 256:384], neg_tri, z[:, 256:384], True, True, t_full)
                    elif what == "weigh":
                        if kind == "sb":
                            pe.wait_ge(stick_ready, c.next(stick_ready))
                        else:
                            pe.wait_ge(rt.free, rt.all_used())
                        if h % 2 == 0:
                            pe.wait_ge(rv.free, rv.awaited())
                            ob = rv.claim()
                        wt, o = t2[:, a % 2, :], ob[HALF * (h % 2):HALF * (h % 2) + HALF, 0:S]
                        mm(o, v_tok[:, 0, vcol:vcol + DH], wt[:, 0:256], True, False)
                        mm(ob[HALF * (h % 2):HALF * (h % 2) + HALF, 128:256], v_tok[:, 1, vcol:vcol + DH], wt[:, 256:384], False, True, v_full)
                    elif what == "index":
                        pe.wait_ge(ra.free, ra.awaited())
                        b = ra.claim()
                        hp = slice(HALF * (a % 2), HALF * (a % 2) + HALF)
                        q = T_IQ + a // 2
                        mm(b[:, 0:128], qk[hp, q, 0:128], qk[hp, T_IK, 0:128], True, True)
                        mm(b[:, 128:384], qk[hp, q, 128:256], qk[hp, T_IK, :], True, True, a_full)
                    elif what == "chunk":
                        kind, w = MAIN[m]
                        if kind == "gate":
                            two_tiles(parts(chunk(), KT, 256), ra, xk, a_full)
                        else:
                            up_chunk(w)
                        done(m)
                        m += 1

                for w in ((2, 0), (2, 1)):
                    up_chunk(w)
                    done(m)
                    m += 1
                pe.wait_ge(m_hi_made, c.next(m_hi_made))
                pe.wait_ge(m_lo_made, c.next(m_lo_made))
                mk = x_tiles(m_hi, m_lo, KT)
                for k in range(4):
                    two_tiles(parts(chunk(), KT, 256), rd, mk, d_full)
                    done(m)
                    m += 1
                flush()
                layer_norm_sums()
                pe.wait_ge(x_hi_made, c.next(x_hi_made))
                pe.wait_ge(x_lo_made, c.next(x_lo_made))
                for k in range(4):
                    two_tiles(parts(chunk(), KT, 256), ra, xk, a_full)
                    done(m)
                    m += 1
                pe.wait_ge(p_hi_made, c.next(p_hi_made))
                pe.wait_ge(p_lo_made, c.next(p_lo_made))
                w = parts(chunk(), 2, D)
                for q in range(4):
                    pe.wait_ge(rd.free, rd.awaited())
                    b = rd.claim()
                    for t in range(2):
                        tile(b[:, S * t:S * t + S], w, P * (2 * q + t), None, x_tiles(p_hi, p_lo, 2), give=d_full if t else None)
                done(m)
                m += 1
                for k in range(16):
                    two_tiles(parts(chunk(), KT, 256), ra, xk, a_full)
                    done(m)
                    m += 1
                pe.wait_ge(f_lo_made, c.next(f_lo_made, 16))
                for k in range(16):
                    w = parts(chunk(), 16, P)
                    if k % 2 == 0:
                        pe.wait_ge(rd.free, rd.awaited())
                        ob = rd.claim()
                    tile(ob[:, 0:S], w, 0, None, [(q, (f_hi[:, 16 * (k % 2) + q, :], f_lo[:, 16 * (k % 2) + q, :])) for q in range(16)],
                         first=(k % 2 == 0), last=(k % 2 == 1), give=d_full if k % 2 else None)
                    done(m)
                    m += 1
                flush()
                layer_norm_sums()
            n[0] += (LAYERS - 1) * CHUNKS1
            rt2 = Ring(c, bank[2:3], turn_full, turned)
            ro = Ring(c, bank[4:6], o_full, o_free)
            pe.wait_ge(phase_in, 32)

            def squares_sum(src, kts, width):
                pe.wait_ge(rs.free, rs.awaited())
                b = rs.claim()
                for q, k in enumerate(kts):
                    mm(b[:, 0:width], ones, src[:, k, 0:width], q == 0, q == len(kts) - 1, var_full if q == len(kts) - 1 else None)

            def modulated(width):
                rs.seam()
                pe.wait_ge(squared, c.next(squared))
                squares_sum(sq2, range(KT), width)
                pe.wait_ge(h_lo_made, c.next(h_lo_made, KT))
                return x_tiles(h_hi, h_lo, KT, slice(0, width))

            def unit_ffn(l, which, width):
                xk = modulated(width)
                for j in c.passes(f"ffn{l}{which}", 2, *rings):
                    for t in range(HT):
                        w = parts(chunk(), KT, P if t in SPLIT_TILES else 2 * P)
                        pe.wait_ge(ra.free, ra.awaited())
                        tile(ra.claim()[:, 0:width], w, 0, None, xk, give=a_full)
                        if t in SPLIT_TILES:
                            owed[0] = True
                            w = parts(chunk(), KT, P)
                        pe.wait_ge(rd.free, rd.awaited())
                        tile(rd.claim()[:, 0:width], w, 0 if t in SPLIT_TILES else P, None, xk, give=d_full)
                        owed[0] = True
                    pe.wait_ge(unit_lo_made, c.next(unit_lo_made, HT))
                    uk = x_tiles(un_hi, un_lo, HT, slice(0, width))
                    for t in range(KT):
                        pe.wait_ge(rd.free, rd.awaited())
                        tile(rd.claim()[:, 0:width], parts(chunk(), HT, P), 0, None, uk, give=d_full)
                        owed[0] = True
                    flush()
                n[0] += FFN_CHUNKS

            def rotation(srcs):
                pe.wait_ge(rd.free, rd.awaited())
                b = rd.claim()
                for j, src in enumerate(srcs):
                    mm(b[:, S * j:S * j + S], rot, src, True, True, d_full if j == len(srcs) - 1 else None)

            def soft_attention(units, score, weigh):
                pe.wait_ge(rd.free, rd.all_used())
                rs.seam()
                ro.seam()
                for s in range(len(units) + 3):
                    if s < len(units):
                        pe.wait_ge(rs.free, rs.awaited())
                        score(rs.claim(), *units[s])
                    if 2 <= s < len(units) + 2:
                        pe.wait_ge(weights_ready, c.next(weights_ready))
                        pe.wait_ge(rt2.free, rt2.awaited())
                        b = rt2.claim()
                        for j in range(4):
                            mm(b[:, P * j:P * j + P], prob[(s - 2) % 3][:, P * j:P * j + P], ident, True, True,
                               turn_full if j == 3 else None, transpose=True)
                    if s >= 3:
                        if s == len(units) + 2:
                            pe.wait_ge(rt2.free, rt2.all_used())
                        else:
                            pe.wait_ge(turned, c.value(turned, rt2.used))
                        weigh(t2[:, (s - 3) % 2, :], *units[s - 3])
                pe.wait_ge(ro.free, ro.all_used())
                rs.seam()

            def mla():
                xk = modulated(2 * S)
                for q in range(4):
                    w = parts(chunk(), KT, 256 if q < 3 else P)
                    for j in range(2 if q < 3 else 1):
                        pe.wait_ge(rd.free, rd.awaited())
                        tile(rd.claim()[:, :], w, P * j, None, xk, give=d_full)
                    owed[0] = True
                flush()
                rs.seam()
                pe.wait_ge(squared, c.next(squared))
                squares_sum(sqm, range(4), 2 * S)
                squares_sum(sqm, range(4, 6), 2 * S)
                pe.wait_ge(h_lo_made, c.next(h_lo_made, 6))
                qk_, kvk = x_tiles(cq_hi, cq_lo, 4, slice(0, 2 * S)), x_tiles(ckv_hi, ckv_lo, 2, slice(0, 2 * S))
                for q in range(3):
                    w = parts(chunk(), 4, 512)
                    for j in range(4):
                        pe.wait_ge(rd.free, rd.awaited())
                        tile(rd.claim()[:, :], w, P * j, None, qk_, give=d_full)
                    owed[0] = True
                w = parts(chunk(), 2, D)
                for j in range(MLA_H):
                    pe.wait_ge(rd.free, rd.awaited())
                    tile(rd.claim()[:, :], w, P * j, None, kvk, give=d_full)
                owed[0] = True
                w = parts(chunk(), 2, D)
                for j in range(8):
                    toks = slice(P * (j // 2), P * (j // 2) + P)
                    pe.wait_ge(rd.free, rd.awaited())
                    b = rd.claim()
                    for k in range(2):
                        product(b[:, :], (ckv_hi[:, k, toks], ckv_lo[:, k, toks]),
                                [z[:, k, 512 * (j % 2):512 * (j % 2) + 512] for z in w], k == 0, k == 1, d_full if k else None)
                owed[0] = True
                flush()
                pe.wait_ge(q_ready, c.next(q_ready))
                for q in range(2):
                    rotation([qr[:, 2 * q + j, 0:S] for j in range(2)])
                rotation([kr[:, 0:S]])
                pe.wait_ge(roped, c.next(roped, 3))

                def score(b, h, part):
                    hp = slice(HALF * (h % 2), HALF * (h % 2) + HALF)
                    if part < 2:
                        toks = slice(P * part, P * part + P)
                        mm(b[:, :], qn[:, h, toks], kn[:, h, :], True, False)
                        mm(b[:, 0:S], qrot[hp, h // 2, toks], kr[hp, 0:S], False, False)
                        mm(b[:, S:2 * S], qr[hp, h // 2, toks], kr[hp, S:2 * S], False, True, s_full)
                    else:
                        for q in range(2):
                            toks = slice(S + P * q, S + P * q + P)
                            mm(b[:, S * q:S * q + S], qn[:, h, toks], kn[:, h, S:2 * S], True, False)
                            mm(b[:, S * q:S * q + S], qr[hp, h // 2, toks], kr[hp, S:2 * S], False, True, s_full if q else None)

                ob = [None]

                def weigh(wt, h, part):
                    if part == 0:
                        pe.wait_ge(ro.free, ro.awaited())
                        ob[0] = ro.claim()
                    if part < 2:
                        for k in range(4):
                            mm(ob[0][:, P * part:P * part + P], vm[:, k, P * h:P * h + P], wt[:, P * k:P * k + P], k == 0, k == 3)
                    else:
                        for q in range(2):
                            for k in range(2):
                                mm(ob[0][:, S + P * q:S + P * q + P], vm[:, 2 + k, P * h:P * h + P],
                                   wt[:, P * (2 * q + k):P * (2 * q + k) + P], k == 0, k == 1, o_full if q and k else None)

                soft_attention(MLA_UNITS, score, weigh)
                ok = x_tiles(om_hi, om_lo, KT, slice(0, 2 * S))
                for q in range(4):
                    w = parts(chunk(), KT, 256)
                    for j in range(2):
                        pe.wait_ge(rd.free, rd.awaited())
                        tile(rd.claim()[:, :], w, P * j, None, ok, give=d_full)
                    owed[0] = True
                flush()

            def swa():
                xk = modulated(2 * S)
                for q in range(2):
                    w = parts(chunk(), KT, 256)
                    for j in range(2):
                        pe.wait_ge(rd.free, rd.awaited())
                        tile(rd.claim()[:, :], w, P * j, None, xk, give=d_full)
                    owed[0] = True
                w = parts(chunk(), KT, 256)
                for j in range(2):
                    pe.wait_ge(rd.free, rd.awaited())
                    b = rd.claim()
                    for t in range(2):
                        toks = slice(P * (2 * j + t), P * (2 * j + t) + P)
                        for k in range(KT):
                            product(b[:, S * t:S * t + S], (h_hi[:, k, toks], h_lo[:, k, toks]), [z[:, k, :] for z in w],
                                    k == 0, k == KT - 1, d_full if t and k == KT - 1 else None)
                owed[0] = True
                for q in range(4):
                    w = parts(chunk(), KT, 256)
                    pe.wait_ge(rd.free, rd.awaited())
                    b = rd.claim()
                    for j in range(2):
                        tile(b[:, S * j:S * j + S], w, P * j, None, x_tiles(h_hi, h_lo, KT), give=d_full if j else None)
                    owed[0] = True
                flush()
                pe.wait_ge(q_ready, c.next(q_ready))
                for q in range(2):
                    rotation([kd[:, 2 * q + j, 0:S] for j in range(2)])
                for q in range(4):
                    rotation([q2[:, 2 * q + j, :] for j in range(2)])
                pe.wait_ge(roped, c.next(roped, 6))

                def score(b, h, part):
                    hp, toks, g = slice(HALF * (h % 2), HALF * (h % 2) + HALF), slice(P * part, P * part + P), h // (SWA_H // SWA_KV)
                    mm(b[:, 0:S], q2rot[hp, h // 2, toks], kd[hp, g, 0:S], True, True)
                    mm(b[:, S:2 * S], q2[hp, h // 2, toks], kd[hp, g, S:2 * S], True, True, s_full)

                ob = [None]

                def weigh(wt, h, part):
                    if h % 2 == 0 and part == 0:
                        pe.wait_ge(ro.free, ro.awaited())
                        ob[0] = ro.claim()
                    g = h // (SWA_H // SWA_KV)
                    o = ob[0][HALF * (h % 2):HALF * (h % 2) + HALF, P * part:P * part + P]
                    for k in range(4):
                        mm(o, vw[:, k, DH * g:DH * g + DH], wt[:, P * k:P * k + P], k == 0, k == 3,
                           o_full if k == 3 and h % 2 and part else None)

                soft_attention(SWA_UNITS, score, weigh)
                ok = x_tiles(ow_hi, ow_lo, KT)
                for q in range(4):
                    w = parts(chunk(), KT, 256)
                    pe.wait_ge(rd.free, rd.awaited())
                    b = rd.claim()
                    for j in range(2):
                        tile(b[:, S * j:S * j + S], w, P * j, None, ok, give=d_full if j else None)
                    owed[0] = True
                flush()

            unit_ffn(0, 0, 2 * S)
            mla()
            unit_ffn(0, 1, 2 * S)
            unit_ffn(1, 0, 2 * S)
            swa()
            unit_ffn(1, 1, S)
            rs.seam()
            pe.wait_ge(squared, c.next(squared))
            squares_sum(sq2, range(KT), S)
            pe.wait_ge(result_ready, c.next(result_ready))
            rd.seam()
            for t in range(2):
                for q in range(2):
                    pe.wait_ge(rd.free, rd.awaited())
                    b = rd.claim()
                    for j in range(4):
                        mm(b[:, P * j:P * j + P], xs[:, 4 * q + j, P * t:P * t + P], ident, True, True,
                           d_full if j == 3 else None, transpose=True)


INPUTS = ["x", "p", "w_in", "b_forget", "w_up_fox", "w_up_sb", "w_up_dsa", "w_out", "ln1_g", "ln1_b", "w_ff_in",
          "w_ff_out", "w_ple", "w_ple_gate", "ln2_g", "ln2_b", "c_2", "ctx_2", "c_ctx_2", "mod_w_2", "mod_b_2",
          "norm_g_2", "final_norm_g_2", "ffn_w_in_2", "ffn_w_out_2", "mla_w_down_2", "mla_q_norm_2",
          "mla_kv_norm_2", "mla_w_uq_2", "mla_w_ukv_2", "mla_w_o_2", "swa_w_qkv_2", "swa_sink_2", "swa_w_o_2"]


def kernel(**inputs):
    import concourse.bacc as bacc
    from concourse.bass_utils import run_bass_kernel_spmd

    nc = bacc.Bacc("TRN2", target_bir_lowering=False, num_devices=1)
    arrays, dram = {}, {}
    for name in INPUTS:
        arrays[f"in_{name}"] = np.ascontiguousarray(inputs[name])
        dram[name] = nc.dram_tensor(f"in_{name}", arrays[f"in_{name}"].shape, F32, kind="ExternalInput").ap()
    table = constants()
    arrays["constants"] = np.concatenate([table[k] for g in (FIXED_CONSTS, PHASE1_CONSTS, PHASE2_CONSTS) for k in g], 1)
    dram["constants"] = nc.dram_tensor("constants", arrays["constants"].shape, F32, kind="ExternalInput").ap()
    out = nc.dram_tensor("out", (1, S, D), F32, kind="ExternalOutput").ap()
    measured = {}
    build(nc, dram, out[0], PER_PASS, measured)
    assert measured == PER_PASS, measured
    r = run_bass_kernel_spmd(nc, [arrays], core_ids=[0])
    return r.results[0]["out"]
```

```python
from contextlib import ExitStack

import concourse.bass as bass
import concourse.mybir as mybir
import numpy as np

F32 = mybir.dt.float32
F32R = mybir.dt.float32r
ALU = mybir.AluOpType
ACT = mybir.ActivationFunctionType
AX = mybir.AxisListType
EXP_LN_SET = 6

P = 128
D = 1024
KT = D // P
S = 256
LAYERS = 2
DH = 64
HALF = 64

W_FOX, W_SB, W_DSA = 6 * DH, 5 * DH, 5 * DH
IDX_HEADS = 8
FQ, FK, FV = 0, W_FOX, 2 * W_FOX
FF = 3 * W_FOX
SQ = FF + 6
SK, SV = SQ + W_SB, SQ + 2 * W_SB
DQ = SQ + 3 * W_SB
DK = DQ + W_DSA
DV = DK + DH
IQ = DV + DH
IK = IQ + IDX_HEADS * DH
IW = IK + DH
GATE = IW + IDX_HEADS
D_FF = 4 * D
ALPHA = (2 * LAYERS) ** 0.25
LN_EPS = 1e-5
TOPK = min(256, S // 4)
SCALE = DH ** -0.5
NEG = -1e30
MARK = -3e38
N_MOD = 9
D_FF2 = 2816
FT2 = D_FF2 // P
HT = FT2 // 2
RMS_EPS = 1e-6
Q_RANK, KV_RANK = 512, 256
NOPE, ROPE, MV = 128, 64, 128
MLA_H = 8
MLA_SCALE = (NOPE + ROPE) ** -0.5
WINDOW = 128
SWA_H, SWA_KV = 16, 4

SLOTS = 3
CHUNK = 2048
LANDED = 128

T_FQ, T_FK, T_SQ, T_SK, T_SK4, T_SQ4, T_DQ, T_DK, T_IQ, T_IK = 0, 3, 6, 8, 10, 11, 12, 14, 15, 19
QK_TILES = 20
QKV_PIECES = [
    [(0, FQ, 256)], [(0, FQ + 256, 256)], [(0, FQ + 512, 256)],
    [(0, SQ, 256)], [(0, SK, 256)],
    [(0, SK + 256, 64), (64, FF, 6), (70, IW, 8), (128, SQ + 256, 64), (192, DQ + 256, 64)],
    [(0, DQ, 256)],
    [(0, DK, 64), (64, DK, 64), (128, IQ, 128)],
    [(0, IQ + 128, 256)],
    [(0, IQ + 384, 128), (128, IK, 64), (192, IK, 64)],
    [(0, FV, 256)],
    [(0, FV + 256, 128), (128, SV, 128)],
    [(0, SV + 128, 192), (192, DV, 64)],
]
FF_COL, IW_COL = 64, 70

MAIN = ([("qk", c) for c in range(10)] + [("v", c) for c in range(3)]
        + [("gate", (0, c)) for c in range(4)] + [("gate", (1, c)) for c in range(4)]
        + [("up", (0, c)) for c in range(2)] + [("gate", (2, c)) for c in range(4)]
        + [("up", (1, c)) for c in range(2)] + [("up", (2, c)) for c in range(2)]
        + [("out", c) for c in range(4)] + [("plegate", c) for c in range(4)] + [("ple", 0)]
        + [("ffin", c) for c in range(16)] + [("ffout", (c, k)) for c in range(8) for k in range(2)])
MODS = 36
CHUNKS1 = len(MAIN) + MODS
assert len(MAIN) == 2 * MODS and CHUNKS1 % SLOTS == 0


def stream1():
    out = []
    for m, item in enumerate(MAIN):
        out.append(item)
        if m % 2:
            out.append(("mod", m // 2))
    return out


HEADS = [("fox", h) for h in range(6)] + [("sb", h) for h in range(5)] + [("dsa", h) for h in range(5)]


def attention_script():
    fill = {0: 1, 1: 1, 2: 1, 3: 1,
            6: 1, 7: 1, 8: 1, 9: 1, 10: 2}
    out = []

    def close(a):
        out.append(("weigh", a))

    for a, (kind, h) in enumerate(HEADS):
        if kind == "dsa" and h == 0:
            out.append(("turn", a - 1))
            out.append(("weigh", a - 1))
            for i in range(IDX_HEADS):
                out.append(("index", i))
                if i % 2:
                    out.append(("chunk", None))
            out.append(("topk", None))
            out.append(("chunk", None))
            out.append(("chunk", None))
        if kind == "fox":
            out.append(("decay", a))
        out.append(("score", a))
        if a and not (kind == "dsa" and h == 0):
            out.append(("turn", a - 1))
        out += [("chunk", None)] * fill.get(a, 0)
        if a and not (kind == "dsa" and h == 0):
            close(a - 1)
    out.append(("turn", len(HEADS) - 1))
    out.append(("weigh", len(HEADS) - 1))
    return out


SCRIPT = attention_script()


def head_place(kind, h):
    if kind == "fox":
        return T_FQ + h // 2, T_FK + h // 2, h % 2, DH * h
    if kind == "sb":
        return (T_SQ4, T_SK4, 0, W_FOX + DH * h) if h == 4 else (T_SQ + h // 2, T_SK + h // 2, h % 2, W_FOX + DH * h)
    return (T_SQ4, T_DK, 1, W_FOX + W_SB) if h == 4 else (T_DQ + h // 2, T_DK, h % 2, W_FOX + W_SB)


def ends_tile(kind, h):
    return h % 2 == 1 or (kind != "fox" and h == 4)


SPLIT_TILES = (HT - 2, HT - 1)
FFN_CHUNKS = HT + len(SPLIT_TILES) + KT
assert FFN_CHUNKS % SLOTS == 0
MLA_UNITS = [(h, part) for h in range(MLA_H) for part in range(3)]
SWA_UNITS = [(h, part) for h in range(SWA_H) for part in range(2)]


def mla_end(unit):
    return (unit[0], 2 * S) if unit[1] == 2 else None


def swa_end(unit):
    return (unit[0] // 2, S) if unit[0] % 2 and unit[1] else None


def streams(width):
    return [(s, slice(S * s, S * s + S)) for s in range(width // S)]


class Counts:

    def __init__(self, eng, per_pass, measured):
        self.eng, self.per_pass, self.measured = eng, per_pass, measured
        self.seen, self.made = {}, {}
        self.i = self.loop = self.last = None

    def value(self, sem, n):
        if self.i is None:
            return n
        return n + self.i * self.per_pass[self.loop].get(sem.name, 0)

    def next(self, sem, k=1):
        self.seen[sem] = self.seen.get(sem, 0) + k
        return self.value(sem, self.seen[sem])

    def did(self, sem, k=1):
        self.made[sem] = self.made.get(sem, 0) + k
        self.last = sem
        return k

    def own(self):
        return self.value(self.last, self.made[self.last])

    def credit(self, sem, k=1):
        self.eng.sem_inc(sem, k)
        self.made[sem] = self.made.get(sem, 0) + k

    def passes(self, name, times, *rings):
        before = dict(self.seen), dict(self.made), [r.used for r in rings]
        for r in rings:
            r.seam()
        with self.eng.Fori(0, times) as i:
            self.i, self.loop = i, name
            yield i
            self.i = self.loop = None
        for r, n in zip(rings, before[2]):
            r.seam()
            self.note(name, r.free.name, r.used - n)
            r.used += (times - 1) * (r.used - n)
            r.seam()
        for now, then in ((self.seen, before[0]), (self.made, before[1])):
            for sem, n in now.items():
                step = n - then.get(sem, 0)
                if step:
                    self.note(name, sem.name, step)
                    now[sem] = n + (times - 1) * step

    def note(self, name, sem, step):
        had = self.measured.setdefault(name, {}).setdefault(sem, step)
        assert had == step, (name, sem, had, step)


class Ring:

    def __init__(self, counts, banks, full, free):
        self.counts, self.banks, self.full, self.free = counts, banks, full, free
        self.used = 0
        self.at = 0
        self.last_use = [0] * len(banks)

    def awaited(self):
        return self.counts.value(self.free, self.last_use[self.at % len(self.banks)] + 1)

    def all_used(self):
        return self.counts.value(self.free, self.used + 1)

    def claim(self):
        b = self.at % len(self.banks)
        self.at += 1
        self.used += 1
        self.last_use[b] = self.used
        return self.banks[b]

    def seam(self):
        self.at = 0
        self.last_use = [self.used] * len(self.banks)

def constants():
    p = np.arange(P)[:, None]
    k = np.arange(P)[None, :]
    f = np.float32
    zeros = np.zeros((P, P), f)
    out = {"ident": np.eye(P, dtype=f), "ones": np.ones((P, P), f)}
    r = np.zeros((P, P), f)
    for h in (0, HALF):
        for j in range(32):
            r[h + 32 + j, h + j] = -1
            r[h + j, h + 32 + j] = 1
    out["rot"] = r
    out["fold"] = np.tile(np.eye(2, dtype=f), (P // 2, 1))
    out["neg_tri"] = np.where(p >= k, -1, 0).astype(f)
    out["neg_ones"] = np.full((P, P), -1, f)
    out["row_mask"] = np.concatenate([zeros, np.where(k > p, NEG / SCALE, 0)], 1).astype(f)
    out["sb_mask"] = np.concatenate([np.where(p < k, 0, NEG), zeros], 1).astype(f)
    out["idx_mask"] = np.concatenate([zeros, np.where((p < 64) & (k >= 64), NEG, 0)], 1).astype(f)
    pos = np.arange(S, dtype=f)
    inv = f(10000.0) ** (-np.arange(32, dtype=f) / f(32))
    ang = (pos[:, None] * inv[None, :]).astype(f).T
    for name, fn, idle in (("cos", np.cos, 1), ("sin", np.sin, 0)):
        t = np.tile(fn(ang).astype(f), (4, 1))
        a = t.copy()
        a[:HALF] = idle
        out[name + "_a"], out[name + "_b"] = a, t
    inv = np.exp(f(-np.log(10000.0)) * np.arange(16, dtype=f) / f(16)).astype(f)
    row, col = (np.arange(S) // 64).astype(f), (np.arange(S) % 64).astype(f)
    ang = np.concatenate([row[:, None] * inv, col[:, None] * inv], -1).astype(f).T
    out["cos_2"], out["sin_2"] = (np.tile(fn(ang).astype(f), (4, 1)) for fn in (np.cos, np.sin))
    q, kk = np.arange(P)[:, None], np.arange(S)[None, :]
    out["win_mask"] = np.concatenate([np.where(abs(kk - (q + P * b)) <= WINDOW, 0, NEG / SCALE) for b in range(2)], 1).astype(f)
    return out


FIXED_CONSTS = {"ident": P, "ones": P, "rot": P, "fold": 2}
PHASE1_CONSTS = {"neg_tri": P, "neg_ones": P, "row_mask": S, "sb_mask": S, "idx_mask": S,
                 "cos_a": S, "sin_a": S, "cos_b": S, "sin_b": S}
PHASE2_CONSTS = {"cos_2": S, "sin_2": S, "win_mask": 2 * S}
CONST_AT = {}
for _group in (FIXED_CONSTS, PHASE1_CONSTS, PHASE2_CONSTS):
    _a = 0
    for _name, _n in _group.items():
        CONST_AT[_name] = (_a, _n)
        _a += _n
N_FIXED = sum(FIXED_CONSTS.values())
N_PHASE = sum(PHASE1_CONSTS.values())
N_PHASE2 = sum(PHASE2_CONSTS.values())
N_ROWS_DMA = 4 * LAYERS + LAYERS + 1 + LAYERS + 4

PER_PASS = {'ffn00': {'a_free': 11,
           'a_full': 11,
           'chunk_used': 21,
           'd_free': 19,
           'd_full': 19,
           'hi_made': 21,
           'landed0': 896,
           'landed1': 896,
           'landed2': 896,
           'lo_made': 21,
           's_free': 0,
           't_free': 0,
           'tile_squared': 8,
           'unit_hi_made': 11,
           'unit_lo_made': 11,
           'unit_ready': 11,
           'v_free': 0,
           'v_step': 15,
           'x_tile': 8},
 'ffn01': {'a_free': 11,
           'a_full': 11,
           'chunk_used': 21,
           'd_free': 19,
           'd_full': 19,
           'hi_made': 21,
           'landed0': 896,
           'landed1': 896,
           'landed2': 896,
           'lo_made': 21,
           's_free': 0,
           't_free': 0,
           'tile_squared': 8,
           'unit_hi_made': 11,
           'unit_lo_made': 11,
           'unit_ready': 11,
           'v_free': 0,
           'v_step': 15,
           'x_tile': 8},
 'ffn10': {'a_free': 11,
           'a_full': 11,
           'chunk_used': 21,
           'd_free': 19,
           'd_full': 19,
           'hi_made': 21,
           'landed0': 896,
           'landed1': 896,
           'landed2': 896,
           'lo_made': 21,
           's_free': 0,
           't_free': 0,
           'tile_squared': 8,
           'unit_hi_made': 11,
           'unit_lo_made': 11,
           'unit_ready': 11,
           'v_free': 0,
           'v_step': 15,
           'x_tile': 8},
 'ffn11': {'a_free': 11,
           'a_full': 11,
           'chunk_used': 21,
           'd_free': 19,
           'd_full': 19,
           'hi_made': 21,
           'landed0': 896,
           'landed1': 896,
           'landed2': 896,
           'lo_made': 21,
           's_free': 0,
           't_free': 0,
           'tile_squared': 8,
           'unit_hi_made': 11,
           'unit_lo_made': 11,
           'unit_ready': 11,
           'v_free': 0,
           'v_step': 7,
           'x_tile': 8},
 'layers': {'a_free': 40,
            'a_full': 40,
            'a_step': 24,
            'abs_ready': 5,
            'arg_ready': 5,
            'bf_in': 16,
            'centred': 16,
            'chunk_used': 108,
            'd_free': 91,
            'd_full': 91,
            'exp_made': 22,
            'f_hi_made': 16,
            'f_lo_made': 16,
            'ff_abs': 1,
            'ff_log': 1,
            'ff_sum': 1,
            'gate_made': 16,
            'gate_used': 12,
            'hi_made': 108,
            'landed0': 4608,
            'landed1': 4608,
            'landed2': 4608,
            'lo_made': 108,
            'log_made': 5,
            'logits_ready': 11,
            'm_hi_made': 1,
            'm_lo_made': 1,
            'm_ready': 1,
            'o_hi_made': 9,
            'o_lo_made': 9,
            'o_ready': 9,
            'p_copied': 1,
            'p_hi_made': 1,
            'p_in': 16,
            'p_lo_made': 1,
            'p_room': 1,
            'relu_used': 8,
            'roped': 5,
            'rstd_made': 2,
            's_free': 20,
            's_full': 20,
            'scaled': 16,
            'soft_ready': 5,
            'squared': 16,
            'stick_ready': 5,
            'sum_ready': 2,
            't_free': 17,
            't_full': 17,
            'v_free': 9,
            'v_full': 16,
            'v_step': 190,
            'variance_ready': 2,
            'weights_ready': 11,
            'x_hi_made': 16,
            'x_lo_made': 16,
            'x_ready': 16}}


def build(nc, dram, out, per_pass, measured):
    ctx = ExitStack()
    with ctx:
        def sem(name):
            return ctx.enter_context(nc.semaphore(name))

        base = (nc.sbuf_base + 31) // 32 * 32
        top = [base]

        def fixed(name, shape, dt=F32):
            size = 4 * int(np.prod(shape[1:]))
            t = nc.alloc_sbuf_tensor_at(name, shape, dt, offset=top[0])
            top[0] += (size + 31) // 32 * 32
            return t

        raw = [fixed(f"raw{s}", [P, CHUNK]) for s in range(SLOTS)]
        w_hi = [fixed(f"w_hi{s}", [P, CHUNK], F32R) for s in range(SLOTS)]
        w_lo = [fixed(f"w_lo{s}", [P, CHUNK], F32R) for s in range(SLOTS)]
        xs = fixed("xs", [P, KT, 2 * S])
        cst = fixed("cst", [P, N_FIXED])
        phase = fixed("phase", [P, N_PHASE])
        cols_a = fixed("cols_a", [P, 120])
        cols_mod = fixed("cols_mod", [P, LAYERS, 72])
        cols_d = fixed("cols_d", [P, 22])
        bf = fixed("bf", [P, 1])
        ln_cols = fixed("ln_cols", [P, 4, KT])
        mods = fixed("mods", [P, LAYERS, 144])
        cond_st = fixed("cond_st", [P, 4 * KT + P - 4], F32R)
        cond = fixed("cond", [P, 2, KT])
        small = fixed("small", [P, 64])
        one = small[:, 2:3]
        stat = [small[:, 8 + 8 * b:16 + 8 * b] for b in range(3)]
        amod = fixed("amod", [P, KT, 2])
        hgate = fixed("hgate", [P, KT, 2])
        sink = fixed("sink", [P, SWA_H])
        nsink = fixed("nsink", [P, SWA_H])
        cq8 = fixed("cq8", [P, 2, 6])
        iwt = fixed("iwt", [P, 2, 8])
        top8 = fixed("top8", [P, 2, 8])
        t1 = fixed("t1", [P, 2, 512])
        t2 = fixed("t2", [P, 2, 512])
        t3 = fixed("t3", [P, 2, 512])
        prob = [t1[:, 0, :], t1[:, 1, :], t3[:, 0, :]]
        work = top[0]

        def mod_col(l, j, k, s):
            a = 16 * j + 2 * k + s
            return mods[:, l, a:a + 1]
        assert work + 94 * 1024 <= nc.sbuf_usable_end, (work, nc.sbuf_usable_end)

        def at(name, kib, shape, dt=F32):
            t = nc.alloc_sbuf_tensor_at(name, shape, dt, offset=work + int(kib * 1024))
            assert kib * 1024 + 4 * int(np.prod(shape[1:])) <= 94 * 1024, name
            return t

        x_hi = at("x_hi", 0, [P, KT, S], F32R)
        x_lo = at("x_lo", 8, [P, KT, S], F32R)
        qk = at("qk", 16, [P, QK_TILES, S])
        v_tok = at("v_tok", 36, [P, 2, 768])
        gates = at("gates", 43, [P, 2, KT, S])
        o_hi = at("o_hi", 59, [P, 2, 3, S], F32R)
        o_lo = at("o_lo", 65, [P, 2, 3, S], F32R)
        decay = at("decay", 71, [P, 2, 384])
        score = at("score", 74, [P, 384])
        chosen = at("chosen", 75.5, [P, 384])
        o32 = at("o32", 77, [P, 2, S])
        merged = at("merged", 79, [P, KT, S])
        p_tok = at("p_tok", 87, [P, 2, 256])
        p_hi = at("p_hi", 89, [P, 2, S], F32R)
        p_lo = at("p_lo", 91, [P, 2, S], F32R)
        m_hi = at("m_hi", 16, [P, KT, S], F32R)
        m_lo = at("m_lo", 24, [P, KT, S], F32R)
        f_hi = at("f_hi", 16, [P, 32, S], F32R)
        f_lo = at("f_lo", 48, [P, 32, S], F32R)
        x_sum = at("x_sum", 88, [P, S])[:, :]
        mod_rows = at("mod_rows", 93, [P, 256])
        sq1 = at("sq1", 80, [P, KT, S])
        ple_g = at("ple_g", 80, [P, KT, S])
        rows_a = at("rows_a", 32, [P, P])
        rows_m = at("rows_m", 33, [P, LAYERS, P])
        rows_d = at("rows_d", 35, [P, P])
        x_tok = at("x_tok", 40, [P, 2, D])
        c_tok = at("c_tok", 48, [P, 2, D])
        y_tok = at("y_tok", 60, [P, 2, D])

        h_hi = at("h_hi", 0, [P, KT, 2 * S], F32R)
        h_lo = at("h_lo", 16, [P, KT, 2 * S], F32R)
        un_hi = at("un_hi", 32, [P, HT, 2 * S], F32R)
        un_lo = at("un_lo", 54.5, [P, HT, 2 * S], F32R)
        sqt = at("sqt", 80, [P, 2, 2 * S])
        acc = at("acc", 84, [P, 2, 2 * S])
        qn = at("qn", 0, [P, MLA_H, 2 * S])
        kn = at("kn", 16, [P, MLA_H, 2 * S])
        cqkv = at("cqkv", 32, [P, 6, 2 * S])
        vm = at("vm", 32, [P, 4, D])
        cq_hi = at("cq_hi", 44, [P, 4, 2 * S], F32R)
        cq_lo = at("cq_lo", 52, [P, 4, 2 * S], F32R)
        ckv_hi = at("ckv_hi", 60, [P, 2, 2 * S], F32R)
        ckv_lo = at("ckv_lo", 64, [P, 2, 2 * S], F32R)
        om_hi = at("om_hi", 48, [P, KT, 2 * S], F32R)
        om_lo = at("om_lo", 64, [P, KT, 2 * S], F32R)
        qr = at("qr", 80, [P, 4, 2 * S])
        qrot = at("qrot", 88, [P, 4, S])
        kr = at("kr", 92, [P, 2 * S])
        q2 = at("q2", 32, [P, KT, S])
        q2rot = at("q2rot", 40, [P, KT, S])
        kd = at("kd", 48, [P, SWA_KV, 2 * S])
        vw = at("vw", 56, [P, 4, SWA_KV * DH])
        ow_hi = at("ow_hi", 60, [P, KT, S], F32R)
        ow_lo = at("ow_lo", 68, [P, KT, S], F32R)

        def const(t, name):
            a, n = CONST_AT[name]
            return t[:, a:a + n]

        ident, ones, rot, fold = (const(cst, n) for n in ("ident", "ones", "rot", "fold"))
        cond_cols = cond_st[:, 0:4 * KT].rearrange("p (k c) -> p c k", c=4)
        neg_tri, neg_ones, row_mask, sb_mask, idx_mask = (
            const(phase, n) for n in ("neg_tri", "neg_ones", "row_mask", "sb_mask", "idx_mask"))
        cos_a, sin_a, cos_b, sin_b = (const(phase, n) for n in ("cos_a", "sin_a", "cos_b", "sin_b"))
        cos_2, sin_2, win_mask = (const(phase, n) for n in ("cos_2", "sin_2", "win_mask"))

        bank = [nc.alloc_psum_tensor(f"bank{b}", [P, 512], F32) for b in range(8)]

        landed = [sem(f"landed{s}") for s in range(SLOTS)]
        hi_made, lo_made, chunk_used = sem("hi_made"), sem("lo_made"), sem("chunk_used")
        raw_set = sem("raw_set")
        consts_in, rows_in, x_in, bf_in, p_in, phase_in = (
            sem(n) for n in ("consts_in", "rows_in", "x_in", "bf_in", "p_in", "phase_in"))
        d_full, d_free = sem("d_full"), sem("d_free")
        a_full, a_free = sem("a_full"), sem("a_free")
        s_full, s_free = sem("s_full"), sem("s_free")
        t_full, t_free = sem("t_full"), sem("t_free")
        v_full, v_free = sem("v_full"), sem("v_free")
        apart = sem("apart")
        v_step, a_step = sem("v_step"), sem("a_step")
        x_ready, x_hi_made, x_lo_made = sem("x_ready"), sem("x_hi_made"), sem("x_lo_made")
        inputs_ready, sum_ready, scaled = sem("inputs_ready"), sem("sum_ready"), sem("scaled")
        x_tile, tile_squared, acc_ready = sem("x_tile"), sem("tile_squared"), sem("acc_ready")
        cond_exp, cond_ready, cond_hi_made, cond_lo_made = (
            sem(n) for n in ("cond_exp", "cond_ready", "cond_hi_made", "cond_lo_made"))
        p_room, p_copied, p_hi_made, p_lo_made = (sem(n) for n in ("p_room", "p_copied", "p_hi_made", "p_lo_made"))
        roped = sem("roped")
        ff_abs, ff_log, ff_sum = sem("ff_abs"), sem("ff_log"), sem("ff_sum")
        logits_ready, exp_made, weights_ready, turned = (
            sem(n) for n in ("logits_ready", "exp_made", "weights_ready", "turned"))
        abs_ready, log_made, soft_ready, arg_ready, stick_ready = (
            sem(n) for n in ("abs_ready", "log_made", "soft_ready", "arg_ready", "stick_ready"))
        relu_made, relu_used = sem("relu_made"), sem("relu_used")
        o_ready, o_hi_made, o_lo_made = sem("o_ready"), sem("o_hi_made"), sem("o_lo_made")
        gate_made, gate_used = sem("gate_made"), sem("gate_used")
        m_ready, m_hi_made, m_lo_made = sem("m_ready"), sem("m_hi_made"), sem("m_lo_made")
        centred, squared, variance_ready, rstd_made, result_ready = (
            sem(n) for n in ("centred", "squared", "variance_ready", "rstd_made", "result_ready"))
        ple_exp = sem("ple_exp")
        relu2_made, f_hi_made, f_lo_made = sem("relu2_made"), sem("f_hi_made"), sem("f_lo_made")
        u_ready, h_hi_made, h_lo_made = sem("u_ready"), sem("h_hi_made"), sem("h_lo_made")
        unit_ready, unit_hi_made, unit_lo_made = sem("unit_ready"), sem("unit_hi_made"), sem("unit_lo_made")
        c_tile, q_ready = sem("c_tile"), sem("q_ready")
        turn_full = sem("turn_full")
        o_full, o_free = sem("o_full"), sem("o_free")
        stored, y_copied = sem("stored"), sem("y_copied")

        block = ctx.enter_context(nc.Block())

        @block.sync
        def _(sp):
            c = Counts(sp, per_pass, measured)
            n = [0]

            def chunk(pieces):
                s = n[0] % SLOTS
                sp.wait_ge(lo_made, c.value(lo_made, n[0] + 1))
                for k, (dst, src) in enumerate(pieces(raw[s])):
                    last = k == len(pieces(raw[s])) - 1
                    sp.dma_start(dst, src).then_inc(landed[s], c.did(landed[s], LANDED - 16 * k if last else 16))
                n[0] += 1

            def view(slot, kt, width):
                return slot[:, 0:kt * width].rearrange("p (k n) -> p k n", k=kt)

            def whole(src, kt, width):
                return lambda slot: [(view(slot, kt, width), src.rearrange("(k p) n -> p k n", p=P))]

            sp.dma_start(cst[:, :], dram["constants"][:, 0:N_FIXED]).then_inc(consts_in, 16)
            sp.dma_start(phase[:, :], dram["constants"][:, N_FIXED:N_FIXED + N_PHASE]).then_inc(consts_in, 16)
            rows = 0
            for l in range(LAYERS):
                for name in ("ln1_g", "ln1_b", "ln2_g", "ln2_b"):
                    sp.dma_start(rows_a[rows:rows + KT, :], dram[name][l].rearrange("(t p) -> t p", p=P)).then_inc(rows_in, 16)
                    rows += KT
            for l in range(LAYERS):
                sp.dma_start(rows_a[rows:rows + 24, :], dram["norm_g_2"][l].rearrange("a (t p) -> (a t) p", p=P)).then_inc(rows_in, 16)
                rows += 24
            sp.dma_start(rows_a[rows:rows + KT, :], dram["final_norm_g_2"].rearrange("(t p) -> t p", p=P)).then_inc(rows_in, 16)
            for l in range(LAYERS):
                sp.dma_start(rows_m[0:72, l, :], dram["mod_b_2"][l].rearrange("(t p) -> t p", p=P)).then_inc(rows_in, 16)
            sp.dma_start(rows_d[0:4, :], dram["mla_q_norm_2"][0].rearrange("(t p) -> t p", p=P)).then_inc(rows_in, 16)
            sp.dma_start(rows_d[4:6, :], dram["mla_kv_norm_2"][0].rearrange("(t p) -> t p", p=P)).then_inc(rows_in, 16)
            sp.dma_start(rows_d[6:14, :], dram["c_2"][0].rearrange("(t p) -> t p", p=P)).then_inc(rows_in, 16)
            sp.dma_start(rows_d[14:22, :], dram["c_ctx_2"].rearrange("(t p) -> t p", p=P)).then_inc(rows_in, 16)
            sp.dma_start(x_tok[:, :, :], dram["x"][0].rearrange("(t p) d -> p t d", p=P)).then_inc(x_in, 16)
            sp.dma_start(c_tok[:, :, :], dram["ctx_2"][0].rearrange("(t p) d -> p t d", p=P)).then_inc(x_in, 16)
            sp.wait_ge(raw_set, c.value(raw_set, 1))

            for i in c.passes("layers", LAYERS):
                w_in, ups = dram["w_in"][i], [dram[k][i] for k in ("w_up_fox", "w_up_sb", "w_up_dsa")]

                def qkv(pieces):
                    return lambda slot: [(view(slot, KT, 256)[:, :, a:a + w],
                                          w_in[:, b:b + w].rearrange("(k p) n -> p k n", p=P)) for a, b, w in pieces]

                def up(b, half):
                    src, cols = ups[b], slice(512 * half, 512 * half + 512)
                    if b == 0:
                        return whole(src[:, cols], 3, 512)
                    return lambda slot: [
                        (view(slot, 3, 512)[:, 0:2, :], src[0:256, cols].rearrange("(k p) n -> p k n", p=P)),
                        (view(slot, 3, 512)[0:HALF, 2, :], src[256:320, cols])]

                for k, (kind, what) in enumerate(stream1()):
                    if k == 6:
                        sp.wait_ge(p_room, c.next(p_room))
                        sp.dma_start(p_tok[:, :, :], dram["p"][i, 0].rearrange("(t p) d -> p t d", p=P)).then_inc(p_in, c.did(p_in, 16))
                        sp.dma_start(bf[FF_COL:FF_COL + 6, :], dram["b_forget"][i].rearrange("(a b) -> a b", b=1)).then_inc(bf_in, c.did(bf_in, 16))
                    if kind in ("qk", "v"):
                        chunk(qkv(QKV_PIECES[what + (10 if kind == "v" else 0)]))
                    elif kind == "gate":
                        chunk(qkv([(0, GATE + D * what[0] + 256 * what[1], 256)]))
                    elif kind == "up":
                        chunk(up(*what))
                    elif kind == "mod":
                        chunk(whole(dram["mod_w_2"][i][:, 256 * what:256 * what + 256], KT, 256))
                    elif kind == "out":
                        chunk(whole(dram["w_out"][i][:, 256 * what:256 * what + 256], KT, 256))
                    elif kind == "plegate":
                        chunk(whole(dram["w_ple_gate"][i][:, 256 * what:256 * what + 256], KT, 256))
                    elif kind == "ple":
                        chunk(whole(dram["w_ple"][i], 2, D))
                    elif kind == "ffin":
                        chunk(whole(dram["w_ff_in"][i][:, 256 * what:256 * what + 256], KT, 256))
                    else:
                        col, k2 = what
                        chunk(whole(dram["w_ff_out"][i][2048 * k2:2048 * k2 + 2048, P * col:P * col + P], 16, P))
            n[0] += (LAYERS - 1) * CHUNKS1
            sp.wait_ge(m_ready, LAYERS)
            sp.dma_start(phase[:, 0:N_PHASE2], dram["constants"][:, N_FIXED + N_PHASE:]).then_inc(phase_in, 16)
            sp.dma_start(sink[:, :], dram["swa_sink_2"][0:1, :].to_broadcast([P, SWA_H])).then_inc(phase_in, 16)

            def each_k(srcs, kt, heads, width):
                def pieces(slot):
                    v = slot[:, 0:kt * heads * width].rearrange("p (k h n) -> p k h n", k=kt, h=heads)
                    return [(v[:, k], srcs(k)) for k in range(kt)]
                return pieces

            def unit_ffn(l, which):
                w_in, w_out = dram["ffn_w_in_2"][l, which], dram["ffn_w_out_2"][l, which]
                for j in c.passes(f"ffn{l}{which}", 2):
                    for t in range(HT):
                        g, u = (w_in[:, bass.ds(j * (HT * P) + (a + P * t), P)].rearrange("(k p) n -> p k n", p=P)
                                for a in (0, D_FF2))
                        if t in SPLIT_TILES:
                            chunk(lambda slot: [(view(slot, KT, P), g)])
                            chunk(lambda slot: [(view(slot, KT, P), u)])
                        else:
                            chunk(lambda slot: [(view(slot, KT, 2 * P)[:, :, 0:P], g), (view(slot, KT, 2 * P)[:, :, P:2 * P], u)])
                    for t in range(KT):
                        chunk(whole(w_out[bass.ds(j * (HT * P), HT * P), P * t:P * t + P], HT, P))
                n[0] += FFN_CHUNKS

            def columns(w, cols):
                return lambda slot: [(view(slot, KT, 256)[:, :, a:a + z], w[:, b:b + z].rearrange("(k p) n -> p k n", p=P))
                                     for a, b, z in cols]

            unit_ffn(0, 0)
            down = dram["mla_w_down_2"][0]
            for q in range(3):
                chunk(whole(down[:, 256 * q:256 * q + 256], KT, 256))
            kr_src = down[:, Q_RANK + KV_RANK:].rearrange("(k p) n -> p k n", p=P)
            chunk(lambda slot: [(view(slot, KT, P)[:, :, 0:ROPE], kr_src), (view(slot, KT, P)[:, :, ROPE:P], kr_src)])
            uq = dram["mla_w_uq_2"][0].rearrange("(k p) (h n) -> k p h n", p=P, h=MLA_H)
            ukv = dram["mla_w_ukv_2"][0].rearrange("(k p) (h n) -> k p h n", p=P, h=MLA_H)
            for q in range(2):
                chunk(each_k(lambda k: uq[k][:, 4 * q:4 * q + 4, 0:NOPE], 4, 4, NOPE))
            chunk(each_k(lambda k: uq[k][:, :, NOPE:NOPE + ROPE], 4, MLA_H, ROPE))
            chunk(each_k(lambda k: ukv[k][:, :, 0:NOPE], 2, MLA_H, NOPE))
            chunk(each_k(lambda k: ukv[k][:, :, NOPE:NOPE + MV], 2, MLA_H, MV))
            for q in range(4):
                chunk(whole(dram["mla_w_o_2"][0][:, 256 * q:256 * q + 256], KT, 256))
            unit_ffn(0, 1)
            unit_ffn(1, 0)
            qkv_w = dram["swa_w_qkv_2"][0]
            k_at, v_at = SWA_H * DH, (SWA_H + SWA_KV) * DH
            for q in range(2):
                chunk(columns(qkv_w, [(DH * j, k_at + DH * (2 * q + j // 2), DH) for j in range(4)]))
            chunk(columns(qkv_w, [(0, v_at, 256)]))
            for q in range(4):
                chunk(columns(qkv_w, [(0, 256 * q, 256)]))
            for q in range(4):
                chunk(columns(dram["swa_w_o_2"][0], [(0, 256 * q, 256)]))
            unit_ffn(1, 1)
            for _ in range(2):
                sp.wait_ge(lo_made, c.value(lo_made, n[0] + 1))
                sp.sem_inc(landed[n[0] % SLOTS], LANDED)
                n[0] += 1
            sp.wait_ge(y_copied, 1)
            sp.dma_start(out.rearrange("(t p) d -> p t d", p=P), y_tok[:, :, :]).then_inc(stored, 16)
            sp.wait_ge(stored, 16)

        @block.scalar
        def _(act):
            c = Counts(act, per_pass, measured)
            n = [0]

            def prep(upto):
                while n[0] <= upto:
                    s = n[0] % SLOTS
                    act.wait_ge(landed[s], c.value(landed[s], LANDED * (n[0] // SLOTS + 1)))
                    act.wait_ge(chunk_used, c.value(chunk_used, n[0] + 1))
                    act.copy(w_hi[s][:, :], raw[s][:, :]).then_inc(hi_made, c.did(hi_made))
                    n[0] += 1

            def do(func, o, i, bias=0.0, scale=1.0, **kw):
                return act.activation(o, i, func, bias=bias, scale=scale, **kw)

            def split_hi(dst, src, ready, made):
                act.wait_ge(ready, c.next(ready))
                act.wait_ge(c.last, c.own())
                do(ACT.Copy, dst, src).then_inc(made, c.did(made))

            def rstd(v, r):
                act.wait_ge(variance_ready, c.next(variance_ready))
                act.wait_ge(c.last, c.own())
                do(ACT.Ln, r, v).then_inc(a_step, c.did(a_step))
                act.wait_ge(c.last, c.own())
                do(ACT.Exp, r, r, scale=-0.5).then_inc(rstd_made, c.did(rstd_made))

            def layer_norm(g, bias):
                for k in range(KT):
                    act.wait_ge(centred, c.next(centred))
                    do(ACT.Square, sq1[:, k, :], xs[:, k, 0:S]).then_inc(squared, c.did(squared))
                rstd(t1[:, 0, 0:S], t1[:, 1, 0:S])
                for k in range(KT):
                    act.wait_ge(scaled, c.next(scaled))
                    do(ACT.Identity, x_hi[:, k, :], xs[:, k, 0:S], bias=ln_cols[:, bias, k:k + 1]).then_inc(x_hi_made, c.did(x_hi_made))
                for k in range(KT):
                    act.wait_ge(x_lo_made, c.next(x_lo_made))
                    do(ACT.Identity, xs[:, k, 0:S], xs[:, k, 0:S], bias=ln_cols[:, bias, k:k + 1]).then_inc(x_ready, c.did(x_ready))

            a_at = [0]
            used = [0]

            def passed():
                prep(used[0] + 2)
                used[0] += 1

            def load_exp_and_ln():
                act.add_instruction(mybir.InstLoadActFuncSet(
                    act_func_set_id=EXP_LN_SET, name=nc.get_next_instruction_name(), engine=mybir.EngineType.Activation))

            c.credit(a_free)
            load_exp_and_ln()
            act.wait_ge(raw_set, 1)
            prep(1)
            act.wait_ge(cond_ready, c.next(cond_ready))
            act.wait_ge(c.last, c.own())
            do(ACT.Exp, t3[:, 0, 0:16].rearrange("p (c k) -> p c k", c=2), cond[:, :, :], scale=-1.0).then_inc(cond_exp, c.did(cond_exp))
            act.wait_ge(cond_ready, c.next(cond_ready))
            act.wait_ge(c.last, c.own())
            do(ACT.Copy, cond_cols[:, 0:2, :], cond[:, :, :]).then_inc(cond_hi_made, c.did(cond_hi_made))

            def sigmoid(o):
                act.wait_ge(c.last, c.own())
                do(ACT.Exp, o, bank[6 + a_at[0] % 2][:, :].rearrange("p (t s) -> p t s", t=2), scale=-1.0).then_inc(a_free, c.did(a_free))
                act.wait_ge(c.last, c.own())
                do(ACT.Ln, o, o, bias=one).then_inc(a_step, c.did(a_step))
                act.wait_ge(c.last, c.own())
                do(ACT.Exp, o, o, scale=-1.0).then_inc(gate_made, c.did(gate_made))

            def mod_skip():
                passed()

            def advance(m):
                if m % 2:
                    mod_skip()

            act.wait_ge(inputs_ready, c.next(inputs_ready))
            for k in range(KT):
                do(ACT.Copy, x_hi[:, k, :], xs[:, k, 0:S]).then_inc(x_hi_made, c.did(x_hi_made))
            c.seen[x_lo_made] = KT
            for i in c.passes("layers", LAYERS):
                a_at[0] = 0
                m = 0
                for _ in range(5):
                    passed(), advance(m)
                    m += 1
                split_hi(p_hi[:, :, :], t3[:, 0, :].rearrange("p (t s) -> p t s", t=2), p_copied, p_hi_made)
                for _ in range(8):
                    passed(), advance(m)
                    m += 1
                act.wait_ge(ff_abs, c.next(ff_abs))
                fr = slice(FF_COL, FF_COL + 6)
                act.wait_ge(c.last, c.own())
                do(ACT.Exp, t3[fr, 0, 256:512], t3[fr, 0, 0:256], scale=-1.0).then_inc(a_step, c.did(a_step))
                act.wait_ge(c.last, c.own())
                do(ACT.Ln, t3[fr, 0, 256:512], t3[fr, 0, 256:512], bias=one[fr, :]).then_inc(ff_log, c.did(ff_log))

                for what, a in SCRIPT:
                    kind = HEADS[a][0] if what in ("score", "turn", "weigh") else None
                    if what == "score" and kind != "sb":
                        act.wait_ge(logits_ready, c.next(logits_ready))
                        st, L = stat[a % 2], t1[:, a % 2, :]
                        act.wait_ge(c.last, c.own())
                        do(ACT.Exp, L[:, 0:128], L[:, 0:128], bias=st[:, 2:3], scale=SCALE, accum_out=st[:, 4:5]).then_inc(exp_made, c.did(exp_made))
                        do(ACT.Exp, L[:, 128:384], L[:, 128:384], bias=st[:, 3:4], scale=SCALE,
                           accum_out=st[:, 5:6]).then_inc(exp_made, c.did(exp_made))
                    elif what == "score":
                        act.wait_ge(abs_ready, c.next(abs_ready))
                        z = t3[:, a % 2, 0:384]
                        act.wait_ge(c.last, c.own())
                        do(ACT.Exp, z, z, scale=-1.0).then_inc(a_step, c.did(a_step))
                        act.wait_ge(c.last, c.own())
                        do(ACT.Ln, z, z, bias=one).then_inc(log_made, c.did(log_made))
                    elif what == "turn" and kind == "sb":
                        act.wait_ge(arg_ready, c.next(arg_ready))
                        act.wait_ge(c.last, c.own())
                        do(ACT.Exp, t2[:, a % 2, 0:384], t2[:, a % 2, 0:384]).then_inc(stick_ready, c.did(stick_ready))
                    elif what == "weigh" and ends_tile(*HEADS[a]):
                        br, h = ("fox", "sb", "dsa").index(kind), HEADS[a][1]
                        rows = slice(0, P if h % 2 else HALF)
                        split_hi(o_hi[rows, br % 2, h // 2, :], o32[rows, (h // 2) % 2, :], o_ready, o_hi_made)
                    elif what == "index":
                        act.wait_ge(a_full, c.next(a_full))
                        if a >= 2:
                            act.wait_ge(relu_used, c.next(relu_used))
                        do(ACT.Relu, t3[:, a % 2, 0:384], bank[6 + a_at[0] % 2][:, 0:384]).then_inc(a_free, c.did(a_free))
                        a_at[0] += 1
                    elif what == "chunk":
                        passed()
                        kind, w = MAIN[m]
                        if kind == "gate":
                            b, col = w
                            act.wait_ge(a_full, c.next(a_full))
                            if w == (2, 0):
                                act.wait_ge(gate_used, c.next(gate_used, 4))
                            sigmoid(gates[:, b % 2, 2 * col:2 * col + 2, :])
                            a_at[0] += 1
                        advance(m)
                        m += 1
                act.wait_ge(relu_used, c.next(relu_used, 2))
                for _ in range(2):
                    passed(), advance(m)
                    m += 1
                act.wait_ge(gate_used, c.next(gate_used, 8))
                split_hi(m_hi[:, :, :], merged[:, :, :], m_ready, m_hi_made)
                for _ in range(4):
                    passed(), advance(m)
                    m += 1
                layer_norm(0, 1)
                for k in range(4):
                    passed(), advance(m)
                    m += 1
                    act.wait_ge(a_full, c.next(a_full))
                    sigmoid(ple_g[:, 2 * k:2 * k + 2, :])
                    a_at[0] += 1
                passed(), advance(m)
                m += 1
                for k in range(16):
                    passed(), advance(m)
                    m += 1
                    act.wait_ge(a_full, c.next(a_full))
                    if k >= 2:
                        act.wait_ge(f_lo_made, c.next(f_lo_made))
                    act.wait_ge(c.last, c.own())
                    do(ACT.Relu, t1[:, k % 2, :], bank[6 + a_at[0] % 2][:, :]).then_inc(a_free, c.did(a_free))
                    a_at[0] += 1
                    act.wait_ge(c.last, c.own())
                    do(ACT.Square, f_hi[:, 2 * k:2 * k + 2, :],
                       t1[:, k % 2, :].rearrange("p (t s) -> p t s", t=2)).then_inc(f_hi_made, c.did(f_hi_made))
                act.wait_ge(f_lo_made, c.next(f_lo_made, 2))
                for k in range(16):
                    passed(), advance(m)
                    m += 1
                assert m == len(MAIN)
                layer_norm(2, 3)
                act.wait_ge(c.last, c.own())
            n[0] += (LAYERS - 1) * CHUNKS1
            used[0] += (LAYERS - 1) * CHUNKS1
            c.credit(turned)

            def square_tile(t, width):
                act.wait_ge(x_tile, c.next(x_tile))
                do(ACT.Square, acc[:, 0, 0:width] if t == 0 else sqt[:, t % 2, 0:width], xs[:, t, 0:width]).then_inc(tile_squared, c.did(tile_squared))

            def state_rms(width):
                load_exp_and_ln()
                rstd(t1[:, 0, 0:width], t1[:, 1, 0:width])

            def modulated(l, j, width):
                state_rms(width)
                for k in range(KT):
                    act.wait_ge(u_ready, c.next(u_ready))
                    for s, cols in streams(width):
                        signal = h_hi_made if cols.stop == width else a_step
                        do(ACT.Identity, h_hi[:, k, cols], t2[:, k % 2, cols],
                           bias=mod_col(l, 3 * j, k, s)).then_inc(signal, c.did(signal))

            def unit_ffn(l, which, width):
                modulated(l, 2 * which, width)
                for j in c.passes(f"ffn{l}{which}", 2):
                    a_at[0] = 0

                    def unit_hi(t):
                        act.wait_ge(unit_ready, c.next(unit_ready))
                        act.wait_ge(c.last, c.own())
                        do(ACT.Copy, un_hi[:, t, 0:width], t2[:, t % 2, 0:width]).then_inc(unit_hi_made, c.did(unit_hi_made))

                    for t in range(HT):
                        passed()
                        act.wait_ge(a_full, c.next(a_full))
                        act.wait_ge(c.last, c.own())
                        do(ACT.Silu, t1[:, t % 2, 0:width], bank[6 + a_at[0] % 2][:, 0:width]).then_inc(a_free, c.did(a_free))
                        a_at[0] += 1
                        if t in SPLIT_TILES:
                            passed()
                        if t:
                            unit_hi(t - 1)
                    unit_hi(HT - 1)
                    for t in range(KT):
                        passed()
                        square_tile(t, width)
                n[0] += FFN_CHUNKS
                used[0] += FFN_CHUNKS

            def soft_attention(units, scale, hi, ends, with_sink):
                for s in range(len(units) + 4):
                    if s >= 4 and ends(units[s - 4]) is not None:
                        t, width = ends(units[s - 4])
                        act.wait_ge(o_full, c.next(o_full))
                        do(ACT.Copy, hi[:, t, 0:width], bank[4 + t % 2][:, 0:width]).then_inc(o_hi_made, c.did(o_hi_made))
                    if 2 <= s < len(units) + 2:
                        act.wait_ge(turn_full, c.next(turn_full))
                        do(ACT.Copy, t2[:, s % 2, :], bank[2][:, :]).then_inc(turned, c.did(turned))
                    if s < len(units):
                        act.wait_ge(logits_ready, c.next(logits_ready))
                        st, L, b = stat[s % 3], prob[s % 3], bank[s % 2]
                        h, part = units[s]
                        if part < 2:
                            act.wait_ge(c.last, c.own())
                            signal = a_step if with_sink else exp_made
                            do(ACT.Exp, L, b[:, :], bias=st[:, 2:3], scale=scale, accum_out=st[:, 4:5]).then_inc(signal, c.did(signal))
                            if with_sink:
                                act.wait_ge(c.last, c.own())
                                do(ACT.Exp, st[:, 5:6], sink[:, h:h + 1], bias=st[:, 2:3]).then_inc(exp_made, c.did(exp_made))
                        else:
                            for q in range(2):
                                act.wait_ge(c.last, c.own())
                                signal = exp_made if q else a_step
                                do(ACT.Exp, L[:, S * q:S * q + S], b[:, S * q:S * q + S], bias=st[:, 2 + q:3 + q], scale=scale,
                                   accum_out=st[:, 4 + q:5 + q]).then_inc(signal, c.did(signal))

            def mla():
                modulated(0, 1, 2 * S)
                for k in range(6):
                    if k % 2 == 0:
                        passed()
                    act.wait_ge(c_tile, c.next(c_tile))
                    do(ACT.Square, acc[:, k // 4, :] if k in (0, 4) else sqt[:, k % 2, :], cqkv[:, k, :]).then_inc(tile_squared, c.did(tile_squared))
                passed()
                rstd(t1[:, 0, :], t1[:, 1, :])
                rstd(t3[:, 0, :], t3[:, 1, :])
                for k in range(6):
                    act.wait_ge(u_ready, c.next(u_ready))
                    dst = cq_hi[:, k, :] if k < 4 else ckv_hi[:, k - 4, :]
                    do(ACT.Copy, dst, cqkv[:, k, :]).then_inc(h_hi_made, c.did(h_hi_made))
                for _ in range(5):
                    passed()
                soft_attention(MLA_UNITS, MLA_SCALE, om_hi, mla_end, False)
                for t in range(KT):
                    if t % 2 == 0:
                        passed()
                    square_tile(t, 2 * S)

            def swa():
                modulated(1, 1, 2 * S)
                for _ in range(7):
                    passed()
                soft_attention(SWA_UNITS, SCALE, ow_hi, swa_end, True)
                for t in range(KT):
                    if t % 2 == 0:
                        passed()
                    square_tile(t, S)

            for t in range(KT):
                square_tile(t, 2 * S)
            unit_ffn(0, 0, 2 * S)
            mla()
            unit_ffn(0, 1, 2 * S)
            unit_ffn(1, 0, 2 * S)
            swa()
            unit_ffn(1, 1, S)
            state_rms(S)

        @block.vector
        def _(dve):
            c = Counts(dve, per_pass, measured)
            n, used = [0], [0]

            def prep(upto):
                while n[0] <= upto:
                    s = n[0] % SLOTS
                    dve.wait_ge(hi_made, c.value(hi_made, n[0] + 1))
                    dve.tensor_tensor(w_lo[s][:, :], raw[s][:, :], w_hi[s][:, :].bitcast(F32), ALU.subtract).then_inc(lo_made, c.did(lo_made))
                    n[0] += 1

            def passed():
                prep(used[0] + 2)
                used[0] += 1

            def tt(o, a, b, op):
                return dve.tensor_tensor(o, a, b, op)

            def ts(o, a, s1, s2, op0, op1=None):
                kw = {} if op1 is None else {"op1": op1}
                return dve.tensor_scalar(o, a, s1, s2, op0, **kw)

            def stt(o, a, s1, b, op0, op1):
                return dve.scalar_tensor_tensor(out=o, in0=a, scalar=s1, in1=b, op0=op0, op1=op1)

            def copy(o, a):
                return dve.tensor_copy(o, a)

            def recip(o, a):
                return dve.reciprocal(o, a)

            def lo(dst, src, hi, hi_sem, sem):
                dve.wait_ge(hi_sem, c.next(hi_sem))
                dve.wait_ge(c.last, c.own())
                tt(dst, src, hi.bitcast(F32), ALU.subtract).then_inc(sem, c.did(sem))

            d_at, s_at = [0], [0]

            def bump(sem):
                dve.wait_ge(c.last, c.own())
                dve.sem_inc(sem, 1)
                c.made[sem] = c.made.get(sem, 0) + 1

            def settle_apart():
                dve.wait_ge(c.last, c.own())
                dve.sem_inc(apart, 1)

            def d_bank():
                d_at[0] += 1
                return bank[4 + (d_at[0] - 1) % 2]

            def s_bank():
                s_at[0] += 1
                return bank[(s_at[0] - 1) % 2]

            def pair(t):
                return t.rearrange("p (t s) -> p t s", t=2)

            for s in range(SLOTS):
                dve.memset(raw[s][:, :], 0.0).then_inc(v_step, c.did(v_step))
            dve.memset(one, 1.0).then_inc(v_step, c.did(v_step))
            dve.wait_ge(c.last, c.own())
            copy(cond_st[:, 4 * KT:], raw[0][:, 0:P - 4]).then_inc(v_step, c.did(v_step))
            dve.wait_ge(c.last, c.own())
            c.credit(lo_made, SLOTS)
            for s in (d_free, s_free, t_free, v_free, p_room, raw_set):
                c.credit(s)
            c.seen[a_free] = 1
            dve.wait_ge(consts_in, 32)
            prep(1)
            dve.wait_ge(d_full, c.next(d_full))
            b = d_bank()
            dve.wait_ge(c.last, c.own())
            copy(cols_a[:, :], b[:, 0:120]).then_inc(v_step, c.did(v_step))
            copy(cols_mod[:, :, :], b[:, 120:264].rearrange("p (l t) -> p l t", l=2)).then_inc(v_step, c.did(v_step))
            copy(cols_d[:, :], b[:, 264:286]).then_inc(d_free, c.did(d_free))
            dve.wait_ge(c.last, c.own())
            copy(cond[:, :, :], cols_d[:, 6:22].rearrange("p (c k) -> p c k", c=2)).then_inc(cond_ready, c.did(cond_ready))
            e = t3[:, 0, 0:16].rearrange("p (c k) -> p c k", c=2)
            dve.wait_ge(cond_exp, c.next(cond_exp))
            dve.wait_ge(c.last, c.own())
            ts(e, e, 1.0, None, ALU.add).then_inc(v_step, c.did(v_step))
            dve.wait_ge(c.last, c.own())
            recip(e, e).then_inc(v_step, c.did(v_step))
            dve.wait_ge(c.last, c.own())
            tt(cond[:, :, :], cond[:, :, :], e, ALU.mult).then_inc(cond_ready, c.did(cond_ready))
            lo(cond_cols[:, 2:4, :], cond[:, :, :], cond_cols[:, 0:2, :], cond_hi_made, cond_lo_made)
            for half in range(2):
                for q in range(4):
                    dve.wait_ge(d_full, c.next(d_full))
                    b = d_bank()
                    copy(xs[:, 2 * q:2 * q + 2, half * S:half * S + S], pair(b[:, :])).then_inc(d_free, c.did(d_free))
            bump(inputs_ready)
            for k in range(KT):
                lo(x_lo[:, k, :], xs[:, k, 0:S], x_hi[:, k, :], x_hi_made, x_lo_made)

            def variance(v, b, cnt, eps):
                dve.wait_ge(c.last, c.own())
                ts(v, b[:, 0:v.shape[-1]], 1.0 / cnt, eps, ALU.mult, ALU.add).then_inc(s_free, c.did(s_free))
                bump(variance_ready)

            def refine(v, r, w):
                dve.wait_ge(rstd_made, c.next(rstd_made))
                dve.wait_ge(c.last, c.own())
                stt(w, r, -0.5, r, ALU.mult, ALU.mult).then_inc(v_step, c.did(v_step))
                dve.wait_ge(c.last, c.own())
                tt(w, w, v, ALU.mult).then_inc(v_step, c.did(v_step))
                dve.wait_ge(c.last, c.own())
                stt(r, w, 1.5, r, ALU.add, ALU.mult).then_inc(v_step, c.did(v_step))

            def add_up(t):
                if t == 0:
                    return
                dve.wait_ge(c.last, c.own())
                tt(x_sum, xs[:, 0, 0:S] if t == 1 else x_sum, xs[:, t, 0:S], ALU.add).then_inc(v_step, c.did(v_step))

            def layer_norm(g, bias):
                bump(sum_ready)
                dve.wait_ge(s_full, c.next(s_full))
                b = s_bank()
                for k in range(KT):
                    if k == 0:
                        dve.wait_ge(c.last, c.own())
                    stt(xs[:, k, 0:S], b[:, 0:S], -1.0 / D, xs[:, k, 0:S], ALU.mult, ALU.add).then_inc(centred, c.did(centred))
                bump(s_free)
                dve.wait_ge(s_full, c.next(s_full))
                b = s_bank()
                variance(t1[:, 0, 0:S], b, D, LN_EPS)
                refine(t1[:, 0, 0:S], t1[:, 1, 0:S], t2[:, 0, 0:S])
                dve.wait_ge(c.last, c.own())
                for k in range(KT + 1):
                    if k < KT:
                        stt(xs[:, k, 0:S], xs[:, k, 0:S], ln_cols[:, g, k:k + 1], t1[:, 1, 0:S], ALU.mult, ALU.mult).then_inc(scaled, c.did(scaled))
                    if k:
                        dve.wait_ge(x_hi_made, c.next(x_hi_made))
                        dve.wait_ge(c.last, c.own())
                        stt(x_lo[:, k - 1, :], xs[:, k - 1, 0:S], ln_cols[:, bias, k - 1:k], x_hi[:, k - 1, :].bitcast(F32),
                            ALU.add, ALU.subtract).then_inc(x_lo_made, c.did(x_lo_made))

            for i in c.passes("layers", LAYERS):
                d_at[0] = s_at[0] = 0
                m = 0

                def chunk_of(m):
                    passed()

                def mod(m):
                    if m % 2 == 0:
                        return
                    passed()
                    j = m // 2
                    dve.wait_ge(d_full, c.next(d_full))
                    b = d_bank()
                    if j:
                        mod_columns(b, j - 1)
                    copy(mod_rows[0:4, :], b[0:4, 0:256]).then_inc(d_free, c.did(d_free))

                def mod_columns(b, j):
                    dve.wait_ge(c.last, c.own())
                    signal = d_free if j == MODS - 1 else v_step
                    tt(mods[:, i, 4 * j:4 * j + 4].rearrange("p (t c) -> p t c", c=2),
                       b[:, 256:260].rearrange("p (t c) -> p t c", c=2),
                       cols_mod[:, i, 2 * j:2 * j + 2].unsqueeze(2).to_broadcast([P, 2, 2]), ALU.add).then_inc(signal, c.did(signal))

                def up_done(w):
                    b, half = w
                    dve.wait_ge(gate_made, c.next(gate_made, 2))
                    for q in range(2):
                        t = 4 * half + 2 * q
                        g = gates[:, b % 2, t:t + 2, :]
                        dve.wait_ge(c.last, c.own())
                        dve.wait_ge(d_full, c.next(d_full))
                        tt(g, pair(d_bank()[:, :]), g, ALU.mult).then_inc(d_free, c.did(d_free))
                        if b == 0:
                            dve.wait_ge(c.last, c.own())
                            copy(merged[:, t:t + 2, :], g).then_inc(gate_used, c.did(gate_used))
                        else:
                            dve.wait_ge(c.last, c.own())
                            tt(merged[:, t:t + 2, :], merged[:, t:t + 2, :], g, ALU.add).then_inc(gate_used, c.did(gate_used))

                dve.wait_ge(c.last, c.own())
                copy(ln_cols[:, :, :], cols_a[:, bass.ds(i * 32, 32)].rearrange("p (a k) -> p a k", k=KT)).then_inc(v_step, c.did(v_step))
                for k in range(5):
                    chunk_of(m)
                    dve.wait_ge(c.last, c.own())
                    dve.wait_ge(d_full, c.next(d_full))
                    copy(qk[:, 2 * k:2 * k + 2, :], pair(d_bank()[:, :])).then_inc(d_free, c.did(d_free))
                    mod(m)
                    m += 1
                dve.wait_ge(t_full, c.next(t_full))
                dve.wait_ge(c.last, c.own())
                copy(t3[:, 0, :], bank[2][:, :]).then_inc(t_free, c.did(t_free))
                bump(p_room)
                bump(p_copied)
                lo(p_lo[:, :, :], pair(t3[:, 0, :]), p_hi[:, :, :], p_hi_made, p_lo_made)
                for k in range(5, 10):
                    chunk_of(m)
                    dve.wait_ge(c.last, c.own())
                    dve.wait_ge(d_full, c.next(d_full))
                    copy(qk[:, 2 * k:2 * k + 2, :], pair(d_bank()[:, :])).then_inc(d_free, c.did(d_free))
                    if k == 5:
                        dve.wait_ge(c.last, c.own())
                        dve.wait_ge(d_full, c.next(d_full))
                        copy(iwt[:, :, :], d_bank()[:, 0:16].rearrange("p (t c) -> p t c", t=2)).then_inc(d_free, c.did(d_free))
                    mod(m)
                    m += 1
                for k in range(3):
                    chunk_of(m)
                    dve.wait_ge(c.last, c.own())
                    dve.wait_ge(d_full, c.next(d_full))
                    copy(v_tok[:, :, 256 * k:256 * k + 256], pair(d_bank()[:, :])).then_inc(d_free, c.did(d_free))
                    mod(m)
                    m += 1
                fr = slice(FF_COL, FF_COL + 6)
                z, w, cum = qk[fr, T_SK4, :], t3[fr, 0, 256:512], t3[fr, 1, 0:256]
                dve.wait_ge(bf_in, c.next(bf_in, 16))
                dve.wait_ge(c.last, c.own())
                ts(z, z, bf[fr, :], None, ALU.add).then_inc(v_step, c.did(v_step))
                dve.wait_ge(c.last, c.own())
                stt(t3[fr, 0, 0:256], z, -1.0, z, ALU.mult, ALU.max).then_inc(ff_abs, c.did(ff_abs))
                dve.wait_ge(ff_log, c.next(ff_log))
                dve.wait_ge(c.last, c.own())
                stt(w, z, 0.0, w, ALU.min, ALU.subtract).then_inc(v_step, c.did(v_step))
                dve.wait_ge(c.last, c.own())
                dve.tensor_tensor_scan(cum, ones[fr, 0:1].to_broadcast([6, S]), w, 0.0, ALU.mult, ALU.add).then_inc(ff_sum, c.did(ff_sum))
                dve.wait_ge(d_full, c.next(d_full))
                b = d_bank()
                dve.wait_ge(c.last, c.own())
                ts(cq8[:, :, :], b[:, 0:12].rearrange("p (t h) -> p t h", t=2), 1.0 / SCALE, None, ALU.mult).then_inc(d_free, c.did(d_free))
                for k, (t, cnt) in enumerate([(11, 1), (12, 2), (14, 2), (16, 2), (18, 2)]):
                    dve.wait_ge(d_full, c.next(d_full))
                    b = d_bank()
                    cs, sn = (cos_a, sin_a) if k == 0 else (cos_b, sin_b)
                    for j in range(cnt):
                        dve.wait_ge(c.last, c.own())
                        signal = d_free if j == cnt - 1 else v_step
                        tt(t2[:, k % 2, S * j:S * j + S], b[:, S * j:S * j + S], sn, ALU.mult).then_inc(signal, c.did(signal))
                    for j in range(cnt):
                        tt(qk[:, t + j, :], qk[:, t + j, :], cs, ALU.mult).then_inc(v_step, c.did(v_step))
                    dve.wait_ge(c.last, c.own())
                    tt(qk[:, t:t + cnt, :], qk[:, t:t + cnt, :],
                       t2[:, k % 2, 0:cnt * S].rearrange("p (t s) -> p t s", t=cnt), ALU.add).then_inc(roped, c.did(roped))

                for what, a in SCRIPT:
                    kind, h = HEADS[a] if what in ("score", "turn", "weigh", "decay") else (None, None)
                    if what == "decay":
                        dve.wait_ge(d_full, c.next(d_full))
                        b = d_bank()
                        dve.wait_ge(c.last, c.own())
                        stt(decay[:, a % 2, 0:128], b[:, 0:128], -1.0 / SCALE, row_mask[:, 128:256], ALU.mult, ALU.add).then_inc(v_step, c.did(v_step))
                        dve.wait_ge(c.last, c.own())
                        stt(decay[:, a % 2, 128:384], b[:, 0:256], -1.0 / SCALE, row_mask, ALU.mult, ALU.add).then_inc(d_free, c.did(d_free))
                    elif what == "score" and kind != "sb":
                        dve.wait_ge(s_full, c.next(s_full))
                        b, L, st = s_bank(), t1[:, a % 2, :], stat[a % 2]
                        if kind == "fox":
                            dve.wait_ge(c.last, c.own())
                            stt(L[:, 0:128], b[:, 0:128], cq8[:, 0, h:h + 1], decay[:, a % 2, 0:128], ALU.add, ALU.add).then_inc(v_step, c.did(v_step))
                            dve.wait_ge(c.last, c.own())
                            stt(L[:, 128:384], b[:, 128:384], cq8[:, 1, h:h + 1], decay[:, a % 2, 128:384], ALU.add, ALU.add).then_inc(s_free, c.did(s_free))
                        else:
                            dve.wait_ge(c.last, c.own())
                            tt(L[:, 0:384], b[:, 0:384], chosen[:, :], ALU.add).then_inc(s_free, c.did(s_free))
                        dve.wait_ge(c.last, c.own())
                        dve.tensor_reduce(st[:, 0:1], L[:, 0:128], AX.X, ALU.max).then_inc(v_step, c.did(v_step))
                        dve.tensor_reduce(st[:, 1:2], L[:, 128:384], AX.X, ALU.max).then_inc(v_step, c.did(v_step))
                        dve.wait_ge(c.last, c.own())
                        ts(st[:, 2:4], st[:, 0:2], -SCALE, None, ALU.mult).then_inc(logits_ready, c.did(logits_ready))
                    elif what == "score":
                        dve.wait_ge(s_full, c.next(s_full))
                        b, z = s_bank(), t1[:, a % 2, :]
                        dve.wait_ge(c.last, c.own())
                        stt(z[:, 0:256], b[:, 0:256], SCALE, sb_mask, ALU.mult, ALU.add).then_inc(v_step, c.did(v_step))
                        dve.wait_ge(c.last, c.own())
                        stt(z[:, 256:384], b[:, 256:384], SCALE, sb_mask[:, 0:128], ALU.mult, ALU.add).then_inc(s_free, c.did(s_free))
                        dve.wait_ge(c.last, c.own())
                        stt(t3[:, a % 2, 0:384], z[:, 0:384], -1.0, z[:, 0:384], ALU.mult, ALU.max).then_inc(abs_ready, c.did(abs_ready))
                    elif what == "turn" and kind != "sb":
                        L, st = t1[:, a % 2, :], stat[a % 2]
                        dve.wait_ge(exp_made, c.next(exp_made, 2))
                        dve.wait_ge(c.last, c.own())
                        recip(st[:, 6:8], st[:, 4:6]).then_inc(v_step, c.did(v_step))
                        dve.wait_ge(c.last, c.own())
                        ts(L[:, 0:128], L[:, 0:128], st[:, 6:7], None, ALU.mult).then_inc(v_step, c.did(v_step))
                        ts(L[:, 128:384], L[:, 128:384], st[:, 7:8], None, ALU.mult).then_inc(weights_ready, c.did(weights_ready))
                        dve.wait_ge(t_full, c.next(t_full))
                        dve.wait_ge(c.last, c.own())
                        copy(t2[:, a % 2, 0:384], bank[2][:, 0:384]).then_inc(t_free, c.did(t_free))
                    elif what == "turn":
                        z, sp_ = t1[:, a % 2, 0:384], t3[:, a % 2, 0:384]
                        dve.wait_ge(log_made, c.next(log_made))
                        dve.wait_ge(c.last, c.own())
                        stt(sp_, z, 0.0, sp_, ALU.max, ALU.add).then_inc(soft_ready, c.did(soft_ready))
                        dve.wait_ge(t_full, c.next(t_full))
                        dve.wait_ge(c.last, c.own())
                        tt(t2[:, a % 2, 0:384], bank[2][:, 0:384], z, ALU.add).then_inc(t_free, c.did(t_free))
                        bump(arg_ready)
                    elif what == "weigh":
                        dve.wait_ge(v_full, c.next(v_full))
                        if ends_tile(kind, h):
                            rows, br = slice(0, P if h % 2 else HALF), ("fox", "sb", "dsa").index(kind)
                            dve.wait_ge(c.last, c.own())
                            copy(o32[rows, (h // 2) % 2, :], bank[3][rows, 0:S]).then_inc(v_free, c.did(v_free))
                            bump(o_ready)
                            lo(o_lo[rows, br % 2, h // 2, :], o32[rows, (h // 2) % 2, :], o_hi[rows, br % 2, h // 2, :],
                               o_hi_made, o_lo_made)
                    elif what == "index":
                        dve.wait_ge(a_free, c.next(a_free))
                        for q, cols, first in ((0, slice(0, 128), idx_mask[:, 128:256]), (1, slice(128, 384), idx_mask)):
                            r = t3[:, a % 2, cols]
                            if q == 0:
                                dve.wait_ge(c.last, c.own())
                            signal = relu_used if q else v_step
                            stt(score[:, cols], r, iwt[:, q, a:a + 1], first if a == 0 else score[:, cols], ALU.mult, ALU.add).then_inc(signal, c.did(signal))
                    elif what == "topk":
                        settle_apart()
                        for r in range(TOPK // 8):
                            for q, cols in ((0, slice(0, 128)), (1, slice(128, 384))):
                                dve.max(top8[:, q, :], score[:, cols]).then_inc(v_step, c.did(v_step))
                            settle_apart()
                            for q, cols in ((0, slice(0, 128)), (1, slice(128, 384))):
                                dve.match_replace(out=score[:, cols], in_to_replace=top8[:, q, :],
                                                         in_values=score[:, cols], imm_value=MARK).then_inc(v_step, c.did(v_step))
                            settle_apart()
                        dve.wait_ge(c.last, c.own())
                        ts(chosen[:, :], score[:, :], MARK, NEG / SCALE, ALU.not_equal, ALU.mult).then_inc(v_step, c.did(v_step))
                    elif what == "chunk":
                        chunk_of(m)
                        kind, w = MAIN[m]
                        if kind == "gate":
                            c.seen[a_free] += 1
                        else:
                            up_done(w)
                        mod(m)
                        m += 1

                for w in ((2, 0), (2, 1)):
                    chunk_of(m)
                    up_done(w)
                    mod(m)
                    m += 1
                bump(m_ready)
                lo(m_lo[:, :, :], merged[:, :, :], m_hi[:, :, :], m_hi_made, m_lo_made)
                for k in range(4):
                    chunk_of(m)
                    dve.wait_ge(c.last, c.own())
                    dve.wait_ge(d_full, c.next(d_full))
                    stt(xs[:, 2 * k:2 * k + 2, 0:S], xs[:, 2 * k:2 * k + 2, 0:S], ALPHA, pair(d_bank()[:, :]), ALU.mult, ALU.add).then_inc(d_free, c.did(d_free))
                    add_up(2 * k)
                    add_up(2 * k + 1)
                    mod(m)
                    m += 1
                layer_norm(0, 1)
                for k in range(4):
                    chunk_of(m)
                    mod(m)
                    m += 1
                c.seen[a_free] += 4
                dve.wait_ge(gate_made, c.next(gate_made, 4))
                chunk_of(m)
                for k in range(4):
                    if k == 0:
                        dve.wait_ge(c.last, c.own())
                    dve.wait_ge(d_full, c.next(d_full))
                    tt(ple_g[:, 2 * k:2 * k + 2, :], pair(d_bank()[:, :]), ple_g[:, 2 * k:2 * k + 2, :], ALU.mult).then_inc(d_free, c.did(d_free))
                dve.wait_ge(x_ready, c.next(x_ready, KT))
                dve.wait_ge(c.last, c.own())
                stt(xs[:, :, 0:S], xs[:, :, 0:S], ALPHA, ple_g[:, :, :], ALU.mult, ALU.add).then_inc(v_step, c.did(v_step))
                mod(m)
                m += 1
                for k in range(16):
                    chunk_of(m)
                    dve.wait_ge(f_hi_made, c.next(f_hi_made))
                    dve.wait_ge(a_free, c.next(a_free))
                    sq = pair(t2[:, k % 2, :])
                    r = pair(t1[:, k % 2, :])
                    dve.wait_ge(c.last, c.own())
                    tt(sq, r, r, ALU.mult).then_inc(v_step, c.did(v_step))
                    dve.wait_ge(c.last, c.own())
                    tt(f_lo[:, 2 * k:2 * k + 2, :], sq, f_hi[:, 2 * k:2 * k + 2, :].bitcast(F32), ALU.subtract).then_inc(f_lo_made, c.did(f_lo_made))
                    mod(m)
                    m += 1
                for k in range(16):
                    chunk_of(m)
                    if k % 2:
                        t = k // 2
                        dve.wait_ge(c.last, c.own())
                        dve.wait_ge(d_full, c.next(d_full))
                        tt(xs[:, t, 0:S], d_bank()[:, 0:S], xs[:, t, 0:S], ALU.add).then_inc(d_free, c.did(d_free))
                        add_up(t)
                    mod(m)
                    m += 1
                dve.wait_ge(d_full, c.next(d_full))
                b = d_bank()
                mod_columns(b, MODS - 1)
                layer_norm(2, 3)
                dve.wait_ge(x_ready, c.next(x_ready, KT))
                dve.wait_ge(c.last, c.own())
            n[0] += (LAYERS - 1) * CHUNKS1
            used[0] += (LAYERS - 1) * CHUNKS1
            c.credit(o_free)
            dve.wait_ge(phase_in, 32)
            dve.wait_ge(c.last, c.own())
            ts(nsink[:, :], sink[:, :], -1.0, None, ALU.mult).then_inc(v_step, c.did(v_step))

            def add_square(t, width):
                dve.wait_ge(tile_squared, c.next(tile_squared))
                if t:
                    dve.wait_ge(c.last, c.own())
                    tt(acc[:, 0, 0:width], acc[:, 0, 0:width], sqt[:, t % 2, 0:width], ALU.add).then_inc(v_step, c.did(v_step))

            def state_rms(width):
                s_at[0] = 0
                dve.wait_ge(s_full, c.next(s_full))
                b = s_bank()
                variance(t1[:, 0, 0:width], b, D, RMS_EPS)
                refine(t1[:, 0, 0:width], t1[:, 1, 0:width], t2[:, 1, 0:width])
                dve.wait_ge(c.last, c.own())

            def residual(t, b, width, sem=d_free):
                dve.wait_ge(c.last, c.own())
                for s, cols in streams(width):
                    signal = sem if cols.stop == width else v_step
                    stt(xs[:, t, cols], b[:, cols], hgate[:, t, s:s + 1], xs[:, t, cols], ALU.mult, ALU.add).then_inc(signal, c.did(signal))
                bump(x_tile)
                if t:
                    add_square(t - 1, width)

            def modulated(l, j, width):
                def triple(k):
                    return mods[:, l, 16 * k:16 * k + 16].rearrange("p (t c) -> p t c", c=2)
                g = cols_a[:, 64 + 24 * l + 8 * j:72 + 24 * l + 8 * j]
                dve.wait_ge(c.last, c.own())
                stt(amod[:, :, :], triple(3 * j + 1), 1.0, g.unsqueeze(2).to_broadcast([P, KT, 2]), ALU.add, ALU.mult).then_inc(v_step, c.did(v_step))
                ts(hgate[:, :, :], triple(3 * j + 2), 0.5 if j != 1 else 1.0, None, ALU.mult).then_inc(v_step, c.did(v_step))
                state_rms(width)
                for k in range(KT + 1):
                    if k < KT:
                        dve.wait_ge(c.last, c.own())
                        for s, cols in streams(width):
                            signal = u_ready if cols.stop == width else v_step
                            stt(t2[:, k % 2, cols], xs[:, k, cols], amod[:, k, s:s + 1], t1[:, 1, cols], ALU.mult, ALU.mult).then_inc(signal, c.did(signal))
                    if k:
                        dve.wait_ge(h_hi_made, c.next(h_hi_made))
                        for s, cols in streams(width):
                            if k == KT and s == 0:
                                dve.wait_ge(c.last, c.own())
                            signal = h_lo_made if cols.stop == width else v_step
                            stt(h_lo[:, k - 1, cols], t2[:, (k - 1) % 2, cols], mod_col(l, 3 * j, k - 1, s),
                                h_hi[:, k - 1, cols].bitcast(F32), ALU.add, ALU.subtract).then_inc(signal, c.did(signal))

            def unit_ffn(l, which, width):
                modulated(l, 2 * which, width)
                for j in c.passes(f"ffn{l}{which}", 2):
                    d_at[0] = 0

                    def unit_lo(t):
                        dve.wait_ge(unit_hi_made, c.next(unit_hi_made))
                        tt(un_lo[:, t, 0:width], t2[:, t % 2, 0:width], un_hi[:, t, 0:width].bitcast(F32), ALU.subtract).then_inc(unit_lo_made, c.did(unit_lo_made))

                    for t in range(HT):
                        passed()
                        if t in SPLIT_TILES:
                            passed()
                        dve.wait_ge(a_free, c.next(a_free))
                        dve.wait_ge(c.last, c.own())
                        dve.wait_ge(d_full, c.next(d_full))
                        tt(t2[:, t % 2, 0:width], d_bank()[:, 0:width], t1[:, t % 2, 0:width], ALU.mult).then_inc(d_free, c.did(d_free))
                        bump(unit_ready)
                        if t:
                            unit_lo(t - 1)
                    unit_lo(HT - 1)
                    for t in range(KT):
                        passed()
                        dve.wait_ge(d_full, c.next(d_full))
                        b = d_bank()
                        residual(t, b, width)
                    add_square(KT - 1, width)
                    dve.wait_ge(c.last, c.own())
                n[0] += FFN_CHUNKS
                used[0] += FFN_CHUNKS
                d_at[0] = 0
                bump(acc_ready)

            def rotate(dst, src):
                k, cnt = d_at[0] % 2, src.shape[1]
                turn = t2[:, k, 0:S * cnt].rearrange("p (t s) -> p t s", t=cnt)
                cs, sn = (z.unsqueeze(1).to_broadcast([P, cnt, S]) for z in (cos_2, sin_2))
                dve.wait_ge(d_full, c.next(d_full))
                b = d_bank()
                dve.wait_ge(c.last, c.own())
                tt(turn, b[:, 0:S * cnt].rearrange("p (t s) -> p t s", t=cnt), sn, ALU.mult).then_inc(d_free, c.did(d_free))
                tt(dst, src, cs, ALU.mult).then_inc(v_step, c.did(v_step))
                dve.wait_ge(c.last, c.own())
                tt(dst, dst, turn, ALU.add).then_inc(roped, c.did(roped))

            def soft_attention(units, scale, hi, lo_part, ends, with_sink):
                for s in range(len(units) + 4):
                    if 1 <= s <= len(units):
                        st, L = stat[(s - 1) % 3], prob[(s - 1) % 3]
                        dve.wait_ge(exp_made, c.next(exp_made))
                        if units[s - 1][1] < 2:
                            if with_sink:
                                dve.wait_ge(c.last, c.own())
                                tt(st[:, 4:5], st[:, 4:5], st[:, 5:6], ALU.add).then_inc(v_step, c.did(v_step))
                            dve.wait_ge(c.last, c.own())
                            recip(st[:, 6:7], st[:, 4:5]).then_inc(s_free, c.did(s_free))
                            dve.wait_ge(c.last, c.own())
                            ts(L, L, st[:, 6:7], None, ALU.mult).then_inc(weights_ready, c.did(weights_ready))
                        else:
                            dve.wait_ge(c.last, c.own())
                            recip(st[:, 6:8], st[:, 4:6]).then_inc(s_free, c.did(s_free))
                            for q in range(2):
                                dve.wait_ge(c.last, c.own())
                                signal = weights_ready if q else v_step
                                ts(L[:, S * q:S * q + S], L[:, S * q:S * q + S], st[:, 6 + q:7 + q], None, ALU.mult).then_inc(signal, c.did(signal))
                    if s < len(units):
                        h, part = units[s]
                        st, b = stat[s % 3], bank[s % 2]
                        dve.wait_ge(s_full, c.next(s_full))
                        if with_sink:
                            dve.wait_ge(c.last, c.own())
                            tt(b[:, 0:S], b[:, 0:S], win_mask[:, S * part:S * part + S], ALU.add).then_inc(v_step, c.did(v_step))
                        dve.wait_ge(c.last, c.own())
                        if part < 2:
                            dve.tensor_reduce(st[:, 0:1], b[:, :], AX.X, ALU.max).then_inc(v_step, c.did(v_step))
                            if with_sink:
                                dve.wait_ge(c.last, c.own())
                                stt(st[:, 2:3], st[:, 0:1], -scale, nsink[:, h:h + 1], ALU.mult, ALU.min).then_inc(logits_ready, c.did(logits_ready))
                            else:
                                dve.wait_ge(c.last, c.own())
                                ts(st[:, 2:3], st[:, 0:1], -scale, None, ALU.mult).then_inc(logits_ready, c.did(logits_ready))
                        else:
                            dve.tensor_reduce(st[:, 0:2], pair(b[:, :]), AX.X, ALU.max).then_inc(v_step, c.did(v_step))
                            dve.wait_ge(c.last, c.own())
                            ts(st[:, 2:4], st[:, 0:2], -scale, None, ALU.mult).then_inc(logits_ready, c.did(logits_ready))
                    if s >= 4 and ends(units[s - 4]) is not None:
                        t, width = ends(units[s - 4])
                        lo(lo_part[:, t, 0:width], bank[4 + t % 2][:, 0:width], hi[:, t, 0:width], o_hi_made, o_free)

            def mla():
                modulated(0, 1, 2 * S)
                def add_rank(k):
                    dve.wait_ge(tile_squared, c.next(tile_squared))
                    if k not in (0, 4):
                        dve.wait_ge(c.last, c.own())
                        tt(acc[:, k // 4, :], acc[:, k // 4, :], sqt[:, k % 2, :], ALU.add).then_inc(v_step, c.did(v_step))

                for k in range(6):
                    if k % 2 == 0:
                        passed()
                    dve.wait_ge(c.last, c.own())
                    dve.wait_ge(d_full, c.next(d_full))
                    copy(cqkv[:, k, :], d_bank()[:, :]).then_inc(d_free, c.did(d_free))
                    bump(c_tile)
                    if k:
                        add_rank(k - 1)
                add_rank(5)
                bump(acc_ready)
                passed()
                dve.wait_ge(c.last, c.own())
                dve.wait_ge(d_full, c.next(d_full))
                copy(kr[:, :], d_bank()[:, :]).then_inc(d_free, c.did(d_free))
                s_at[0] = 0
                dve.wait_ge(s_full, c.next(s_full))
                b = s_bank()
                variance(t1[:, 0, :], b, Q_RANK, RMS_EPS)
                dve.wait_ge(s_full, c.next(s_full))
                b = s_bank()
                variance(t3[:, 0, :], b, KV_RANK, RMS_EPS)
                for v, ks, hi, lo_part in ((t1, range(4), cq_hi, cq_lo), (t3, range(4, 6), ckv_hi, ckv_lo)):
                    refine(v[:, 0, :], v[:, 1, :], t2[:, 1, :])
                    dve.wait_ge(c.last, c.own())
                    for k in ks:
                        stt(cqkv[:, k, :], cqkv[:, k, :], cols_d[:, k:k + 1], v[:, 1, :], ALU.mult, ALU.mult).then_inc(u_ready, c.did(u_ready))
                    for k in ks:
                        lo(lo_part[:, k - ks[0], :], cqkv[:, k, :], hi[:, k - ks[0], :], h_hi_made, h_lo_made)
                for q in range(2):
                    passed()
                    for j in range(4):
                        dve.wait_ge(c.last, c.own())
                        dve.wait_ge(d_full, c.next(d_full))
                        copy(qn[:, 4 * q + j, :], d_bank()[:, :]).then_inc(d_free, c.did(d_free))
                passed()
                for j in range(4):
                    dve.wait_ge(c.last, c.own())
                    dve.wait_ge(d_full, c.next(d_full))
                    copy(qr[:, j, :], d_bank()[:, :]).then_inc(d_free, c.did(d_free))
                bump(q_ready)
                passed()
                for j in range(MLA_H):
                    dve.wait_ge(c.last, c.own())
                    dve.wait_ge(d_full, c.next(d_full))
                    copy(kn[:, j, :], d_bank()[:, :]).then_inc(d_free, c.did(d_free))
                passed()
                for j in range(8):
                    dve.wait_ge(c.last, c.own())
                    dve.wait_ge(d_full, c.next(d_full))
                    copy(vm[:, j // 2, 512 * (j % 2):512 * (j % 2) + 512], d_bank()[:, :]).then_inc(d_free, c.did(d_free))
                for q in range(2):
                    rotate(qrot[:, 2 * q:2 * q + 2, :], qr[:, 2 * q:2 * q + 2, 0:S])
                rotate(kr[:, 0:S].unsqueeze(1), kr[:, 0:S].unsqueeze(1))
                soft_attention(MLA_UNITS, MLA_SCALE, om_hi, om_lo, mla_end, False)
                for q in range(4):
                    passed()
                    for j in range(2):
                        dve.wait_ge(d_full, c.next(d_full))
                        b = d_bank()
                        residual(2 * q + j, b, 2 * S)
                add_square(KT - 1, 2 * S)
                bump(acc_ready)

            def swa():
                modulated(1, 1, 2 * S)
                for q in range(2):
                    passed()
                    for j in range(2):
                        dve.wait_ge(c.last, c.own())
                        dve.wait_ge(d_full, c.next(d_full))
                        copy(kd[:, 2 * q + j, :], d_bank()[:, :]).then_inc(d_free, c.did(d_free))
                passed()
                for j in range(2):
                    dve.wait_ge(c.last, c.own())
                    dve.wait_ge(d_full, c.next(d_full))
                    copy(vw[:, 2 * j:2 * j + 2, :], pair(d_bank()[:, :])).then_inc(d_free, c.did(d_free))
                for q in range(4):
                    passed()
                    dve.wait_ge(c.last, c.own())
                    dve.wait_ge(d_full, c.next(d_full))
                    copy(q2[:, 2 * q:2 * q + 2, :], pair(d_bank()[:, :])).then_inc(d_free, c.did(d_free))
                bump(q_ready)
                for q in range(2):
                    rotate(kd[:, 2 * q:2 * q + 2, 0:S], kd[:, 2 * q:2 * q + 2, 0:S])
                for q in range(4):
                    rotate(q2rot[:, 2 * q:2 * q + 2, :], q2[:, 2 * q:2 * q + 2, :])
                soft_attention(SWA_UNITS, SCALE, ow_hi, ow_lo, swa_end, True)
                for q in range(4):
                    passed()
                    dve.wait_ge(d_full, c.next(d_full))
                    b = d_bank()
                    for j in range(2):
                        residual(2 * q + j, b[:, S * j:S * j + S], S, d_free if j else v_step)
                add_square(KT - 1, S)
                bump(acc_ready)

            for t in range(KT):
                bump(x_tile)
                if t:
                    add_square(t - 1, 2 * S)
            add_square(KT - 1, 2 * S)
            bump(acc_ready)
            unit_ffn(0, 0, 2 * S)
            mla()
            unit_ffn(0, 1, 2 * S)
            unit_ffn(1, 0, 2 * S)
            swa()
            unit_ffn(1, 1, S)
            state_rms(S)
            for k in range(KT):
                stt(xs[:, k, 0:S], xs[:, k, 0:S], cols_a[:, 112 + k:113 + k], t1[:, 1, 0:S], ALU.mult, ALU.mult).then_inc(v_step, c.did(v_step))
            bump(result_ready)
            d_at[0] = 0
            for t in range(2):
                for q in range(2):
                    dve.wait_ge(d_full, c.next(d_full))
                    copy(y_tok[:, t, 512 * q:512 * q + 512], d_bank()[:, :]).then_inc(d_free, c.did(d_free))
            bump(y_copied)

        @block.tensor
        def _(pe):
            c = Counts(pe, per_pass, measured)
            n = [0]
            owed = [False]
            rd = Ring(c, bank[4:6], d_full, d_free)
            ra = Ring(c, bank[6:8], a_full, a_free)
            rs = Ring(c, bank[0:2], s_full, s_free)
            rt = Ring(c, bank[2:3], t_full, t_free)
            rv = Ring(c, bank[3:4], v_full, v_free)
            rings = (rd, ra, rs, rt, rv)

            def mm(o, l, r, start, stop, give=None, transpose=False):
                ins = pe.transpose(o, l, r) if transpose else pe.matmul(o, l, r, start=start, stop=stop)
                if give is not None:
                    ins.then_inc(give, c.did(give))
                elif owed[0]:
                    ins.then_inc(chunk_used, c.did(chunk_used))
                    owed[0] = False

            def flush():
                if owed[0]:
                    pe.wait_ge(rd.free, rd.awaited())
                    b = rd.claim()
                    rd.used -= 1
                    rd.at -= 1
                    rd.last_use[rd.at % 2] = rd.used
                    mm(b[:, 0:2], ident, ident[:, 0:2], True, True)

            def chunk():
                s = n[0] % SLOTS
                pe.wait_ge(lo_made, c.value(lo_made, n[0] + 1 + SLOTS))
                n[0] += 1
                return w_hi[s], w_lo[s]

            def parts(w, kt, width):
                return [t[:, 0:kt * width].rearrange("p (k n) -> p k n", k=kt) for t in w]

            def product(o, l, r, first, last, give=None):
                mm(o, l[0], r[0], first, False)
                mm(o, l[0], r[1], False, False)
                mm(o, l[1], r[0], False, last, give)

            def tile(o, w, col, x, kts, first=True, last=True, give=None, width=P):
                for q, (k, r) in enumerate(kts):
                    end = q == len(kts) - 1
                    product(o, [t[:, k, col:col + width] for t in w], r, first and q == 0, last and end,
                            give if end else None)

            def x_tiles(hi, lo, kt, cols=slice(0, S)):
                return [(k, (hi[:, k, cols], lo[:, k, cols])) for k in range(kt)]

            c.credit(chunk_used, SLOTS)
            pe.wait_ge(consts_in, 32)
            pe.wait_ge(rows_in, 16 * N_ROWS_DMA)
            pe.wait_ge(rd.free, rd.awaited())
            b = rd.claim()
            mm(b[:, 0:120], rows_a[0:120, :], ident[0:120, 0:120], True, True, transpose=True)
            for l in range(LAYERS):
                mm(b[:, 120 + 72 * l:192 + 72 * l], rows_m[0:72, l, :], ident[0:72, 0:72], True, True, transpose=True)
            mm(b[:, 264:286], rows_d[0:22, :], ident[0:22, 0:22], True, True, d_full, transpose=True)
            pe.wait_ge(x_in, 32)
            for src in (x_tok, c_tok):
                for q in range(4):
                    pe.wait_ge(rd.free, rd.awaited())
                    b = rd.claim()
                    for j in range(4):
                        k, t = 2 * q + j // 2, j % 2
                        mm(b[:, P * j:P * j + P], src[:, t, P * k:P * k + P], ident, True, True,
                           d_full if j == 3 else None, transpose=True)
            pe.wait_ge(cond_hi_made, c.next(cond_hi_made))
            pe.wait_ge(cond_lo_made, c.next(cond_lo_made))

            def layer_norm_sums():
                pe.wait_ge(sum_ready, c.next(sum_ready))
                pe.wait_ge(rs.free, rs.awaited())
                mm(rs.claim()[:, 0:S], ones, x_sum, True, True, s_full)
                pe.wait_ge(rs.free, rs.awaited())
                b = rs.claim()
                for k in range(KT):
                    pe.wait_ge(squared, c.next(squared))
                    mm(b[:, 0:S], ones, sq1[:, k, :], k == 0, k == KT - 1, s_full if k == KT - 1 else None)

            def tile_by_tile(o, w, x, made, give=None):
                for k in range(KT):
                    pe.wait_ge(made, c.next(made))
                    product(o, [t[:, k, 0:P] for t in w], x[k][1], k == 0, k == KT - 1, give if k == KT - 1 else None)

            rows_at = [0]
            for i in c.passes("layers", LAYERS, *rings):
                m = 0

                def done(m):
                    owed[0] = True
                    if m % 2 == 0:
                        return
                    if m > 1:
                        rows_ready()
                    w = parts(chunk(), KT, 256)
                    pe.wait_ge(rd.free, rd.awaited())
                    b = rd.claim()
                    if m > 1:
                        mod_turn(b)
                    for k in range(KT):
                        for z in range(2):
                            mm(b[:, 0:256], cond_st[:, 4 * k:4 * k + P], w[z][:, k, :], k == 0 and z == 0, k == KT - 1 and z == 1,
                               d_full if k == KT - 1 and z == 1 else None)
                    rows_at[0] = rd.used
                    owed[0] = True

                def rows_ready():
                    pe.wait_ge(d_free, c.value(d_free, rows_at[0] + 1))
                    pe.sem_inc(apart, 1)

                def mod_turn(b, give=None):
                    for t in range(2):
                        mm(b[:, 256 + 2 * t:258 + 2 * t], mod_rows[0:4, P * t:P * t + P], fold[0:4, :], True, True,
                           give if t else None)

                def two_tiles(w, ring, xk, give, made=None):
                    pe.wait_ge(ring.free, ring.awaited())
                    b = ring.claim()
                    if made is not None:
                        tile_by_tile(b[:, 0:S], w, xk, made)
                    for t in range(0 if made is None else 1, 2):
                        tile(b[:, S * t:S * t + S], w, P * t, None, xk, give=give if t else None)

                def up_chunk(w):
                    b, half = w
                    if half == 0:
                        pe.wait_ge(o_lo_made, c.next(o_lo_made, 3))
                    w = parts(chunk(), 3, 512)
                    for q in range(2):
                        pe.wait_ge(rd.free, rd.awaited())
                        d = rd.claim()
                        for t in range(2):
                            for k in range(3):
                                rows = slice(0, HALF if b and k == 2 else P)
                                cols = slice(P * (2 * q + t), P * (2 * q + t) + P)
                                product(d[:, S * t:S * t + S], [z[rows, k, cols] for z in w],
                                        (o_hi[rows, b % 2, k, :], o_lo[rows, b % 2, k, :]), k == 0, k == 2,
                                        d_full if t and k == 2 else None)

                xk = x_tiles(x_hi, x_lo, KT)
                for k in range(10):
                    if k == 5:
                        pe.wait_ge(p_in, c.next(p_in, 16))
                        pe.wait_ge(rt.free, rt.awaited())
                        b = rt.claim()
                        for j in range(4):
                            mm(b[:, P * j:P * j + P], p_tok[:, j % 2, P * (j // 2):P * (j // 2) + P], ident, True, True,
                               t_full if j == 3 else None, transpose=True)
                    w = parts(chunk(), KT, 256)
                    two_tiles(w, rd, xk, d_full, None if k else x_lo_made)
                    if k == 5:
                        pe.wait_ge(rd.free, rd.awaited())
                        b = rd.claim()
                        for t in range(2):
                            for kk in range(KT):
                                toks = slice(P * t, P * t + P)
                                product(b[:, 8 * t:8 * t + 8], (x_hi[:, kk, toks], x_lo[:, kk, toks]),
                                        [q[:, kk, IW_COL:IW_COL + 8] for q in w], kk == 0, kk == KT - 1,
                                        d_full if t and kk == KT - 1 else None)
                    done(m)
                    m += 1
                for k in range(3):
                    w = parts(chunk(), KT, 256)
                    pe.wait_ge(rd.free, rd.awaited())
                    b = rd.claim()
                    for t in range(2):
                        for kk in range(KT):
                            toks = slice(P * t, P * t + P)
                            product(b[:, S * t:S * t + S], (x_hi[:, kk, toks], x_lo[:, kk, toks]),
                                    [q[:, kk, :] for q in w], kk == 0, kk == KT - 1,
                                    d_full if t and kk == KT - 1 else None)
                    done(m)
                    m += 1
                flush()
                fr = slice(FF_COL, FF_COL + 6)
                cum = t3[fr, 1, 0:256]
                pe.wait_ge(ff_sum, c.next(ff_sum))
                pe.wait_ge(rd.free, rd.awaited())
                b = rd.claim()
                pe.sem_inc(apart, 1)
                for t in range(2):
                    mm(b[:, 6 * t:6 * t + 6], cum[:, P * t:P * t + P], ident[fr, fr], True, True, d_full if t else None, transpose=True)
                for k, (t, cnt) in enumerate([(11, 1), (12, 2), (14, 2), (16, 2), (18, 2)]):
                    pe.wait_ge(rd.free, rd.awaited())
                    b = rd.claim()
                    for j in range(cnt):
                        mm(b[:, S * j:S * j + S], rot, qk[:, t + j, :], True, True, d_full if j == cnt - 1 else None)
                pe.wait_ge(roped, c.next(roped, 5))

                v_tiles = 0
                for what, a in SCRIPT:
                    if what in ("score", "turn", "weigh", "decay"):
                        kind, h = HEADS[a]
                        tq, tk, half, vcol = head_place(kind, h)
                        hp = slice(HALF * half, HALF * half + HALF)
                    if what == "decay":
                        pe.wait_ge(rd.free, rd.awaited())
                        b = rd.claim()
                        mm(b[:, 0:S], ident[fr, FF_COL + h:FF_COL + h + 1].to_broadcast([6, P]), cum, True, True, d_full)
                    elif what == "score" and kind != "sb":
                        pe.wait_ge(rs.free, rs.awaited())
                        b = rs.claim()
                        mm(b[:, 0:128], qk[hp, tq, 0:128], qk[hp, tk, 0:128], True, True)
                        mm(b[:, 128:384], qk[hp, tq, 128:256], qk[hp, tk, :], True, True, s_full)
                    elif what == "score":
                        pe.wait_ge(rs.free, rs.awaited())
                        b = rs.claim()
                        mm(b[:, 0:256], qk[hp, tk, 0:128], qk[hp, tq, :], True, True)
                        mm(b[:, 256:384], qk[hp, tk, 128:256], qk[hp, tq, 128:256], True, True, s_full)
                    elif what == "turn" and kind != "sb":
                        pe.wait_ge(weights_ready, c.next(weights_ready))
                        pe.wait_ge(rt.free, rt.awaited())
                        b = rt.claim()
                        for j in range(3):
                            mm(b[:, P * j:P * j + P], t1[:, a % 2, P * j:P * j + P], ident, True, True, t_full if j == 2 else None, transpose=True)
                    elif what == "turn":
                        pe.wait_ge(soft_ready, c.next(soft_ready))
                        pe.wait_ge(rt.free, rt.awaited())
                        b = rt.claim()
                        z = t3[:, a % 2, :]
                        mm(b[:, 0:256], neg_tri, z[:, 0:256], True, False)
                        mm(b[:, 128:256], neg_ones, z[:, 256:384], False, True)
                        mm(b[:, 256:384], neg_tri, z[:, 256:384], True, True, t_full)
                    elif what == "weigh":
                        if kind == "sb":
                            pe.wait_ge(stick_ready, c.next(stick_ready))
                        else:
                            pe.wait_ge(rt.free, rt.all_used())
                        if h % 2 == 0:
                            pe.wait_ge(rv.free, rv.awaited())
                            ob = rv.claim()
                        wt, o = t2[:, a % 2, :], ob[HALF * (h % 2):HALF * (h % 2) + HALF, 0:S]
                        mm(o, v_tok[:, 0, vcol:vcol + DH], wt[:, 0:256], True, False)
                        mm(ob[HALF * (h % 2):HALF * (h % 2) + HALF, 128:256], v_tok[:, 1, vcol:vcol + DH], wt[:, 256:384], False, True, v_full)
                    elif what == "index":
                        pe.wait_ge(ra.free, ra.awaited())
                        b = ra.claim()
                        hp = slice(HALF * (a % 2), HALF * (a % 2) + HALF)
                        q = T_IQ + a // 2
                        mm(b[:, 0:128], qk[hp, q, 0:128], qk[hp, T_IK, 0:128], True, True)
                        mm(b[:, 128:384], qk[hp, q, 128:256], qk[hp, T_IK, :], True, True, a_full)
                    elif what == "chunk":
                        kind, w = MAIN[m]
                        if kind == "gate":
                            two_tiles(parts(chunk(), KT, 256), ra, xk, a_full)
                        else:
                            up_chunk(w)
                        done(m)
                        m += 1

                for w in ((2, 0), (2, 1)):
                    up_chunk(w)
                    done(m)
                    m += 1
                pe.wait_ge(m_hi_made, c.next(m_hi_made))
                pe.wait_ge(m_lo_made, c.next(m_lo_made))
                mk = x_tiles(m_hi, m_lo, KT)
                for k in range(4):
                    two_tiles(parts(chunk(), KT, 256), rd, mk, d_full)
                    done(m)
                    m += 1
                flush()
                layer_norm_sums()
                for k in range(4):
                    two_tiles(parts(chunk(), KT, 256), ra, xk, a_full, None if k else x_lo_made)
                    done(m)
                    m += 1
                pe.wait_ge(p_hi_made, c.next(p_hi_made))
                pe.wait_ge(p_lo_made, c.next(p_lo_made))
                w = parts(chunk(), 2, D)
                for q in range(4):
                    pe.wait_ge(rd.free, rd.awaited())
                    b = rd.claim()
                    for t in range(2):
                        tile(b[:, S * t:S * t + S], w, P * (2 * q + t), None, x_tiles(p_hi, p_lo, 2), give=d_full if t else None)
                done(m)
                m += 1
                for k in range(16):
                    two_tiles(parts(chunk(), KT, 256), ra, xk, a_full)
                    done(m)
                    m += 1
                pe.wait_ge(f_lo_made, c.next(f_lo_made, 16))
                for k in range(16):
                    w = parts(chunk(), 16, P)
                    if k % 2 == 0:
                        pe.wait_ge(rd.free, rd.awaited())
                        ob = rd.claim()
                    tile(ob[:, 0:S], w, 0, None, [(q, (f_hi[:, 16 * (k % 2) + q, :], f_lo[:, 16 * (k % 2) + q, :])) for q in range(16)],
                         first=(k % 2 == 0), last=(k % 2 == 1), give=d_full if k % 2 else None)
                    done(m)
                    m += 1
                rows_ready()
                pe.wait_ge(rd.free, rd.awaited())
                mod_turn(rd.claim(), d_full)
                flush()
                layer_norm_sums()
            n[0] += (LAYERS - 1) * CHUNKS1
            rt2 = Ring(c, bank[2:3], turn_full, turned)
            ro = Ring(c, bank[4:6], o_full, o_free)
            pe.wait_ge(phase_in, 32)

            def modulated(width):
                rs.seam()
                pe.wait_ge(acc_ready, c.next(acc_ready))
                pe.wait_ge(rs.free, rs.awaited())
                mm(rs.claim()[:, 0:width], ones, acc[:, 0, 0:width], True, True, s_full)
                made = c.seen.get(h_lo_made, 0)
                c.seen[h_lo_made] = made + KT
                return x_tiles(h_hi, h_lo, KT, slice(0, width)), made

            def first_tile(o, w, x, made, give):
                for k, (_, r) in enumerate(x):
                    pe.wait_ge(h_lo_made, made + k + 1)
                    product(o, [t[:, k, 0:P] for t in w], r, k == 0, k == len(x) - 1, give if k == len(x) - 1 else None)

            def unit_ffn(l, which, width):
                xk, made = modulated(width)
                for j in c.passes(f"ffn{l}{which}", 2, *rings):
                    for t in range(HT):
                        w = parts(chunk(), KT, P if t in SPLIT_TILES else 2 * P)
                        pe.wait_ge(ra.free, ra.awaited())
                        o = ra.claim()[:, 0:width]
                        if t == 0:
                            first_tile(o, w, xk, made, a_full)
                        else:
                            tile(o, w, 0, None, xk, give=a_full)
                        if t in SPLIT_TILES:
                            owed[0] = True
                            w = parts(chunk(), KT, P)
                        pe.wait_ge(rd.free, rd.awaited())
                        tile(rd.claim()[:, 0:width], w, 0 if t in SPLIT_TILES else P, None, xk, give=d_full)
                        owed[0] = True
                    pe.wait_ge(unit_lo_made, c.next(unit_lo_made, HT))
                    uk = x_tiles(un_hi, un_lo, HT, slice(0, width))
                    for t in range(KT):
                        pe.wait_ge(rd.free, rd.awaited())
                        tile(rd.claim()[:, 0:width], parts(chunk(), HT, P), 0, None, uk, give=d_full)
                        owed[0] = True
                    flush()
                n[0] += FFN_CHUNKS

            def rotation(srcs):
                pe.wait_ge(rd.free, rd.awaited())
                b = rd.claim()
                for j, src in enumerate(srcs):
                    mm(b[:, S * j:S * j + S], rot, src, True, True, d_full if j == len(srcs) - 1 else None)

            def soft_attention(units, score, weigh):
                pe.wait_ge(rd.free, rd.all_used())
                rs.seam()
                ro.seam()
                for s in range(len(units) + 3):
                    if s < len(units):
                        pe.wait_ge(rs.free, rs.awaited())
                        score(rs.claim(), *units[s])
                    if 2 <= s < len(units) + 2:
                        pe.wait_ge(weights_ready, c.next(weights_ready))
                        pe.wait_ge(rt2.free, rt2.awaited())
                        b = rt2.claim()
                        for j in range(4):
                            mm(b[:, P * j:P * j + P], prob[(s - 2) % 3][:, P * j:P * j + P], ident, True, True,
                               turn_full if j == 3 else None, transpose=True)
                    if s >= 3:
                        if s == len(units) + 2:
                            pe.wait_ge(rt2.free, rt2.all_used())
                        else:
                            pe.wait_ge(turned, c.value(turned, rt2.used))
                        weigh(t2[:, (s - 3) % 2, :], *units[s - 3])
                pe.wait_ge(ro.free, ro.all_used())
                rs.seam()

            def mla():
                xk, made = modulated(2 * S)
                for q in range(4):
                    w = parts(chunk(), KT, 256 if q < 3 else P)
                    for j in range(2 if q < 3 else 1):
                        pe.wait_ge(rd.free, rd.awaited())
                        o = rd.claim()[:, :]
                        if q == 0 and j == 0:
                            first_tile(o, w, xk, made, d_full)
                        else:
                            tile(o, w, P * j, None, xk, give=d_full)
                    owed[0] = True
                flush()
                rs.seam()
                pe.wait_ge(acc_ready, c.next(acc_ready))
                for j in range(2):
                    pe.wait_ge(rs.free, rs.awaited())
                    mm(rs.claim()[:, :], ones, acc[:, j, :], True, True, s_full)
                made = c.seen[h_lo_made]
                c.seen[h_lo_made] = made + 6
                qk_, kvk = x_tiles(cq_hi, cq_lo, 4, slice(0, 2 * S)), x_tiles(ckv_hi, ckv_lo, 2, slice(0, 2 * S))
                for q in range(3):
                    w = parts(chunk(), 4, 512)
                    for j in range(4):
                        pe.wait_ge(rd.free, rd.awaited())
                        o = rd.claim()[:, :]
                        if q == 0 and j == 0:
                            first_tile(o, w, qk_, made, d_full)
                        else:
                            tile(o, w, P * j, None, qk_, give=d_full)
                    owed[0] = True
                pe.wait_ge(h_lo_made, made + 6)
                w = parts(chunk(), 2, D)
                for j in range(MLA_H):
                    pe.wait_ge(rd.free, rd.awaited())
                    tile(rd.claim()[:, :], w, P * j, None, kvk, give=d_full)
                owed[0] = True
                w = parts(chunk(), 2, D)
                for j in range(8):
                    toks = slice(P * (j // 2), P * (j // 2) + P)
                    pe.wait_ge(rd.free, rd.awaited())
                    b = rd.claim()
                    for k in range(2):
                        product(b[:, :], (ckv_hi[:, k, toks], ckv_lo[:, k, toks]),
                                [z[:, k, 512 * (j % 2):512 * (j % 2) + 512] for z in w], k == 0, k == 1, d_full if k else None)
                owed[0] = True
                flush()
                pe.wait_ge(q_ready, c.next(q_ready))
                for q in range(2):
                    rotation([qr[:, 2 * q + j, 0:S] for j in range(2)])
                rotation([kr[:, 0:S]])
                pe.wait_ge(roped, c.next(roped, 3))

                def score(b, h, part):
                    hp = slice(HALF * (h % 2), HALF * (h % 2) + HALF)
                    if part < 2:
                        toks = slice(P * part, P * part + P)
                        mm(b[:, :], qn[:, h, toks], kn[:, h, :], True, False)
                        mm(b[:, 0:S], qrot[hp, h // 2, toks], kr[hp, 0:S], False, False)
                        mm(b[:, S:2 * S], qr[hp, h // 2, toks], kr[hp, S:2 * S], False, True, s_full)
                    else:
                        for q in range(2):
                            toks = slice(S + P * q, S + P * q + P)
                            mm(b[:, S * q:S * q + S], qn[:, h, toks], kn[:, h, S:2 * S], True, False)
                            mm(b[:, S * q:S * q + S], qr[hp, h // 2, toks], kr[hp, S:2 * S], False, True, s_full if q else None)

                ob = [None]

                def weigh(wt, h, part):
                    if part == 0:
                        pe.wait_ge(ro.free, ro.awaited())
                        ob[0] = ro.claim()
                    if part < 2:
                        for k in range(4):
                            mm(ob[0][:, P * part:P * part + P], vm[:, k, P * h:P * h + P], wt[:, P * k:P * k + P], k == 0, k == 3)
                    else:
                        for q in range(2):
                            for k in range(2):
                                mm(ob[0][:, S + P * q:S + P * q + P], vm[:, 2 + k, P * h:P * h + P],
                                   wt[:, P * (2 * q + k):P * (2 * q + k) + P], k == 0, k == 1, o_full if q and k else None)

                soft_attention(MLA_UNITS, score, weigh)
                ok = x_tiles(om_hi, om_lo, KT, slice(0, 2 * S))
                for q in range(4):
                    w = parts(chunk(), KT, 256)
                    for j in range(2):
                        pe.wait_ge(rd.free, rd.awaited())
                        tile(rd.claim()[:, :], w, P * j, None, ok, give=d_full)
                    owed[0] = True
                flush()

            def swa():
                xk, made = modulated(2 * S)
                for q in range(2):
                    w = parts(chunk(), KT, 256)
                    for j in range(2):
                        pe.wait_ge(rd.free, rd.awaited())
                        o = rd.claim()[:, :]
                        if q == 0 and j == 0:
                            first_tile(o, w, xk, made, d_full)
                        else:
                            tile(o, w, P * j, None, xk, give=d_full)
                    owed[0] = True
                w = parts(chunk(), KT, 256)
                for j in range(2):
                    pe.wait_ge(rd.free, rd.awaited())
                    b = rd.claim()
                    for t in range(2):
                        toks = slice(P * (2 * j + t), P * (2 * j + t) + P)
                        for k in range(KT):
                            product(b[:, S * t:S * t + S], (h_hi[:, k, toks], h_lo[:, k, toks]), [z[:, k, :] for z in w],
                                    k == 0, k == KT - 1, d_full if t and k == KT - 1 else None)
                owed[0] = True
                for q in range(4):
                    w = parts(chunk(), KT, 256)
                    pe.wait_ge(rd.free, rd.awaited())
                    b = rd.claim()
                    for j in range(2):
                        tile(b[:, S * j:S * j + S], w, P * j, None, x_tiles(h_hi, h_lo, KT), give=d_full if j else None)
                    owed[0] = True
                flush()
                pe.wait_ge(q_ready, c.next(q_ready))
                for q in range(2):
                    rotation([kd[:, 2 * q + j, 0:S] for j in range(2)])
                for q in range(4):
                    rotation([q2[:, 2 * q + j, :] for j in range(2)])
                pe.wait_ge(roped, c.next(roped, 6))

                def score(b, h, part):
                    hp, toks, g = slice(HALF * (h % 2), HALF * (h % 2) + HALF), slice(P * part, P * part + P), h // (SWA_H // SWA_KV)
                    mm(b[:, 0:S], q2rot[hp, h // 2, toks], kd[hp, g, 0:S], True, True)
                    mm(b[:, S:2 * S], q2[hp, h // 2, toks], kd[hp, g, S:2 * S], True, True, s_full)

                ob = [None]

                def weigh(wt, h, part):
                    if h % 2 == 0 and part == 0:
                        pe.wait_ge(ro.free, ro.awaited())
                        ob[0] = ro.claim()
                    g = h // (SWA_H // SWA_KV)
                    o = ob[0][HALF * (h % 2):HALF * (h % 2) + HALF, P * part:P * part + P]
                    for k in range(4):
                        mm(o, vw[:, k, DH * g:DH * g + DH], wt[:, P * k:P * k + P], k == 0, k == 3,
                           o_full if k == 3 and h % 2 and part else None)

                soft_attention(SWA_UNITS, score, weigh)
                ok = x_tiles(ow_hi, ow_lo, KT)
                for q in range(4):
                    w = parts(chunk(), KT, 256)
                    pe.wait_ge(rd.free, rd.awaited())
                    b = rd.claim()
                    for j in range(2):
                        tile(b[:, S * j:S * j + S], w, P * j, None, ok, give=d_full if j else None)
                    owed[0] = True
                flush()

            unit_ffn(0, 0, 2 * S)
            mla()
            unit_ffn(0, 1, 2 * S)
            unit_ffn(1, 0, 2 * S)
            swa()
            unit_ffn(1, 1, S)
            rs.seam()
            pe.wait_ge(acc_ready, c.next(acc_ready))
            pe.wait_ge(rs.free, rs.awaited())
            mm(rs.claim()[:, 0:S], ones, acc[:, 0, 0:S], True, True, s_full)
            pe.wait_ge(result_ready, c.next(result_ready))
            rd.seam()
            for t in range(2):
                for q in range(2):
                    pe.wait_ge(rd.free, rd.awaited())
                    b = rd.claim()
                    for j in range(4):
                        mm(b[:, P * j:P * j + P], xs[:, 4 * q + j, P * t:P * t + P], ident, True, True,
                           d_full if j == 3 else None, transpose=True)


INPUTS = ["x", "p", "w_in", "b_forget", "w_up_fox", "w_up_sb", "w_up_dsa", "w_out", "ln1_g", "ln1_b", "w_ff_in",
          "w_ff_out", "w_ple", "w_ple_gate", "ln2_g", "ln2_b", "c_2", "ctx_2", "c_ctx_2", "mod_w_2", "mod_b_2",
          "norm_g_2", "final_norm_g_2", "ffn_w_in_2", "ffn_w_out_2", "mla_w_down_2", "mla_q_norm_2",
          "mla_kv_norm_2", "mla_w_uq_2", "mla_w_ukv_2", "mla_w_o_2", "swa_w_qkv_2", "swa_sink_2", "swa_w_o_2"]


def kernel(**inputs):
    import concourse.bacc as bacc
    from concourse.bass_utils import run_bass_kernel_spmd

    nc = bacc.Bacc("TRN2", target_bir_lowering=False, num_devices=1)
    arrays, dram = {}, {}
    for name in INPUTS:
        arrays[f"in_{name}"] = np.ascontiguousarray(inputs[name])
        dram[name] = nc.dram_tensor(f"in_{name}", arrays[f"in_{name}"].shape, F32, kind="ExternalInput").ap()
    table = constants()
    arrays["constants"] = np.concatenate([table[k] for g in (FIXED_CONSTS, PHASE1_CONSTS, PHASE2_CONSTS) for k in g], 1)
    dram["constants"] = nc.dram_tensor("constants", arrays["constants"].shape, F32, kind="ExternalInput").ap()
    out = nc.dram_tensor("out", (1, S, D), F32, kind="ExternalOutput").ap()
    measured = {}
    build(nc, dram, out[0], PER_PASS, measured)
    assert measured == PER_PASS, measured
    r = run_bass_kernel_spmd(nc, [arrays], core_ids=[0])
    return r.results[0]["out"]
```
